# Optimizing a Trainium2 kernel written in Bass

```python
import jax, jax.numpy as jnp
from jax import lax
import numpy as np
import math

D_MODEL = 1024
BATCH = 1
SEQ = 512
DEPTH = 1

GRID_W = 64
N_HEADS = 16
HEAD_DIM = D_MODEL // N_HEADS
ATTN_WIDTH = N_HEADS * HEAD_DIM
WIN_ROWS = 8
WIN_COLS = 16
Q_COLS = 16
K_COLS = 32
N_CBLK = GRID_W // Q_COLS
LRU_WIDTH = D_MODEL
LRU_BLOCKS = 16
LRU_BLOCK = LRU_WIDTH // LRU_BLOCKS
LRU_C = 8.0
CONV_W = 4
CONV_LEFT = 2
D_FF = 2816
FFN_RES = 0.5
EPS = 1e-6
IN_WIDTH = 2 * LRU_WIDTH + 3 * ATTN_WIDTH + 2 * D_MODEL


def _rmsnorm(x, g):
    xf = x.astype(jnp.float32)
    y = xf * lax.rsqrt(jnp.mean(xf * xf, axis=-1, keepdims=True) + EPS)
    return (y * g.astype(jnp.float32)).astype(x.dtype)

def _swiglu(h, w_gu, w_down):
    g, u = jnp.split(h @ w_gu, 2, axis=-1)
    return (jax.nn.silu(g) * u) @ w_down

def _centred_dwconv(x, w, b):
    S = x.shape[1]
    xp = jnp.pad(x, ((0, 0), (CONV_LEFT, CONV_W - 1 - CONV_LEFT), (0, 0)))
    y = b
    for k in range(CONV_W):
        y = y + xp[:, k:k + S] * w[k]
    return y

def _lin_combine(left, right):
    a1, b1 = left
    a2, b2 = right
    return a1 * a2, a2 * b1 + b2

def _rglru_scan(xc, w_gates, b_gates, lam):
    B_, S, W = xc.shape
    xb = xc.reshape(B_, S, LRU_BLOCKS, LRU_BLOCK)
    gates = jnp.einsum('bsni,gnio->gbsno', xb, w_gates.astype(jnp.float32)).reshape(2, B_, S, W)
    gates = gates + b_gates.astype(jnp.float32)[:, None, None, :]
    r = jax.nn.sigmoid(gates[0])
    i = jax.nn.sigmoid(gates[1])
    log_a = -LRU_C * r * jax.nn.softplus(-lam.astype(jnp.float32))
    a = jnp.exp(log_a)
    bx = jnp.sqrt(-jnp.expm1(2.0 * log_a)) * (i * xc)
    _, h = lax.associative_scan(_lin_combine, (a, bx), axis=1)
    return h

def _col_tables():
    qc = np.arange(GRID_W).reshape(N_CBLK, Q_COLS)
    kstart = np.clip(np.arange(N_CBLK) * Q_COLS - WIN_COLS // 2, 0, GRID_W - K_COLS)
    kc = kstart[:, None] + np.arange(K_COLS)[None, :]
    cs = np.clip(qc - WIN_COLS // 2, 0, GRID_W - WIN_COLS)
    valid = (kc[:, None, :] >= cs[:, :, None]) & (kc[:, None, :] < cs[:, :, None] + WIN_COLS)
    dc = np.clip(kc[:, None, :] - qc[:, :, None], -(WIN_COLS - 1), WIN_COLS - 1) + WIN_COLS - 1
    return kc, valid, dc

def _neighbourhood_attention(q, k, v, rpb):
    B_, S, H, Dh = q.shape
    rows = S // GRID_W
    kr = min(WIN_ROWS, rows)
    kc, valid, dc = _col_tables()
    kg = k.reshape(B_, rows, GRID_W, H, Dh)[:, :, kc]
    vg = v.reshape(B_, rows, GRID_W, H, Dh)[:, :, kc]
    qg = jnp.moveaxis(q.reshape(B_, rows, N_CBLK, Q_COLS, H, Dh), 1, 0)
    rpb32 = rpb.astype(jnp.float32)
    mask = valid[None, None, :, :, None, :]

    def row_block(args):
        r, q_r = args
        rs = jnp.clip(r - kr // 2, 0, rows - kr)
        k_r = lax.dynamic_slice_in_dim(kg, rs, kr, axis=1)
        v_r = lax.dynamic_slice_in_dim(vg, rs, kr, axis=1)
        s = jnp.einsum('bnqhd,brnkhd->bhnqrk', q_r, k_r, preferred_element_type=jnp.float32)
        dr = rs + jnp.arange(kr) - r + WIN_ROWS - 1
        bias = rpb32[:, dr][:, :, dc]
        s = s + jnp.transpose(bias, (0, 2, 3, 1, 4))[None]
        s = jnp.where(mask, s, -jnp.inf)
        shp = s.shape
        p = jax.nn.softmax(s.reshape(shp[:4] + (kr * K_COLS,)), axis=-1).reshape(shp)
        return jnp.einsum('bhnqrk,brnkhd->bnqhd', p.astype(v.dtype), v_r)

    o = lax.map(row_block, (jnp.arange(rows), qg))
    return jnp.moveaxis(o, 0, 1).reshape(B_, S, H * Dh)

def first_inputs(seed: int = 0) -> dict:
    key = jax.random.key(seed)
    ks = jax.random.split(key, 20)
    f32 = jnp.float32
    nrm = lambda k, shape, s: jax.random.normal(k, shape, f32) * s
    u = jax.random.uniform(ks[10], (DEPTH, 2, LRU_WIDTH), f32, minval=0.9, maxval=0.999)
    sg = u ** (1.0 / LRU_C)
    lru_lambda = jnp.log(sg) - jnp.log1p(-sg)
    return {
        'x': jax.random.normal(ks[0], (BATCH, SEQ, D_MODEL), f32),
        'norm_ffn1': 1.0 + nrm(ks[1], (DEPTH, D_MODEL), 0.02),
        'w_ffn1_gu': nrm(ks[2], (DEPTH, D_MODEL, 2 * D_FF), D_MODEL ** -0.5),
        'w_ffn1_down': nrm(ks[3], (DEPTH, D_FF, D_MODEL), D_FF ** -0.5),
        'norm_mix': 1.0 + nrm(ks[4], (DEPTH, D_MODEL), 0.02),
        'w_in': nrm(ks[5], (DEPTH, D_MODEL, IN_WIDTH), D_MODEL ** -0.5),
        'conv_w': nrm(ks[6], (DEPTH, CONV_W, LRU_WIDTH), CONV_W ** -0.5),
        'conv_b': nrm(ks[7], (DEPTH, LRU_WIDTH), 0.01),
        'lru_w_gates': nrm(ks[8], (DEPTH, 2, 2, LRU_BLOCKS, LRU_BLOCK, LRU_BLOCK), LRU_BLOCK ** -0.5),
        'lru_b_gates': nrm(ks[9], (DEPTH, 2, 2, LRU_WIDTH), 0.1),
        'lru_lambda': lru_lambda,
        'q_norm': 1.0 + nrm(ks[11], (DEPTH, HEAD_DIM), 0.02),
        'k_norm': 1.0 + nrm(ks[12], (DEPTH, HEAD_DIM), 0.02),
        'rel_pos_bias': nrm(ks[13], (DEPTH, N_HEADS, 2 * WIN_ROWS - 1, 2 * WIN_COLS - 1), 0.1),
        'w_out': nrm(ks[14], (DEPTH, D_MODEL, D_MODEL), D_MODEL ** -0.5),
        'norm_ffn2': 1.0 + nrm(ks[15], (DEPTH, D_MODEL), 0.02),
        'w_ffn2_gu': nrm(ks[16], (DEPTH, D_MODEL, 2 * D_FF), D_MODEL ** -0.5),
        'w_ffn2_down': nrm(ks[17], (DEPTH, D_FF, D_MODEL), D_FF ** -0.5),
    }

def first_block(x, norm_ffn1, w_ffn1_gu, w_ffn1_down, norm_mix, w_in, conv_w, conv_b,
              lru_w_gates, lru_b_gates, lru_lambda, q_norm, k_norm, rel_pos_bias, w_out,
              norm_ffn2, w_ffn2_gu, w_ffn2_down):
    B_, S, _ = x.shape
    splits = list(np.cumsum([LRU_WIDTH, LRU_WIDTH, ATTN_WIDTH, ATTN_WIDTH, ATTN_WIDTH, D_MODEL]))
    for l in range(DEPTH):
        x = x + FFN_RES * _swiglu(_rmsnorm(x, norm_ffn1[l]), w_ffn1_gu[l], w_ffn1_down[l])

        h = _rmsnorm(x, norm_mix[l])
        xr, gr, q, k, v, ga, gb = jnp.split(h @ w_in[l], splits, axis=-1)

        xc = _centred_dwconv(xr, conv_w[l], conv_b[l]).astype(jnp.float32)
        h_fwd = _rglru_scan(xc, lru_w_gates[l, 0], lru_b_gates[l, 0], lru_lambda[l, 0])
        h_bwd = jnp.flip(_rglru_scan(jnp.flip(xc, 1), lru_w_gates[l, 1], lru_b_gates[l, 1],
                                     lru_lambda[l, 1]), 1)
        y_lru = ((h_fwd + h_bwd) * jax.nn.gelu(gr.astype(jnp.float32))).astype(x.dtype)

        q = _rmsnorm(q.reshape(B_, S, N_HEADS, HEAD_DIM), q_norm[l]) * (HEAD_DIM ** -0.5)
        k = _rmsnorm(k.reshape(B_, S, N_HEADS, HEAD_DIM), k_norm[l])
        v = v.reshape(B_, S, N_HEADS, HEAD_DIM)
        y_att = _neighbourhood_attention(q, k, v, rel_pos_bias[l]).astype(x.dtype)

        y = jax.nn.sigmoid(ga) * y_lru + jax.nn.sigmoid(gb) * y_att
        x = x + y @ w_out[l]

        x = x + FFN_RES * _swiglu(_rmsnorm(x, norm_ffn2[l]), w_ffn2_gu[l], w_ffn2_down[l])
    return x


DEPTH_2 = 2

HEAD_DIM_2 = 64
SC_WIDTH = 512
SC_TAPS = 3
DA_HEADS = 8
DA_WIDTH = DA_HEADS * HEAD_DIM_2
DA_PAIRS = ((128, 1), (512, 4), (2048, 16))
CC_WIDTH = 512
CC_TAPS = 31
SB_HEADS = 8
SB_WIDTH = SB_HEADS * HEAD_DIM_2
BLOCK_Q = 128
FFN_TAPS = 3
REL_BUCKETS = 32
REL_MAX_DIST = 2048

N_EVEN = (DEPTH_2 + 1) // 2
N_ODD = DEPTH_2 // 2
EVEN_IN = 3 * SC_WIDTH + 3 * DA_WIDTH
EVEN_MIX = SC_WIDTH + DA_WIDTH
ODD_IN = 2 * CC_WIDTH + 3 * SB_WIDTH
ODD_MIX = CC_WIDTH + SB_WIDTH


def rms_norm(x, g):
    xf = x.astype(jnp.float32)
    y = xf * lax.rsqrt(jnp.mean(xf * xf, axis=-1, keepdims=True) + EPS)
    return (y * g.astype(jnp.float32)).astype(x.dtype)

def layer_norm(x, g, b):
    xf = x.astype(jnp.float32)
    mu = jnp.mean(xf, axis=-1, keepdims=True)
    var = jnp.mean(jnp.square(xf - mu), axis=-1, keepdims=True)
    y = (xf - mu) * lax.rsqrt(var + EPS) * g.astype(jnp.float32) + b.astype(jnp.float32)
    return y.astype(x.dtype)

def causal_dwconv(x, w):
    taps, c = w.shape
    return lax.conv_general_dilated(
        x, w[:, None, :].astype(x.dtype), window_strides=(1,),
        padding=((taps - 1, 0),), dimension_numbers=("NWC", "WIO", "NWC"),
        feature_group_count=c)

def t5_bucket(dist):
    max_exact = REL_BUCKETS // 2
    d = jnp.maximum(dist, 1).astype(jnp.float32)
    large = max_exact + (jnp.log(d / max_exact) / math.log(REL_MAX_DIST / max_exact)
                         * (REL_BUCKETS - max_exact)).astype(jnp.int32)
    large = jnp.minimum(large, REL_BUCKETS - 1)
    return jnp.where(dist < max_exact, dist, large)

def dilated_branch(q, k, v, span, dilation, rel_bias):
    b, s, h, dh = q.shape
    L = s // dilation
    n = b * dilation

    def to_sub(t):
        return jnp.swapaxes(t.reshape(b, L, dilation, h, dh), 1, 2).reshape(n, L, h, dh)

    def from_sub(t):
        t = t.reshape((b, dilation, L) + t.shape[3:])
        return jnp.swapaxes(t, 1, 2).reshape((b, s) + t.shape[3:])

    qs, ks, vs = to_sub(q), to_sub(k), to_sub(v)
    bq = math.gcd(BLOCK_Q, L)
    nb = L // bq
    kp = jnp.pad(ks, ((0, 0), (span, 0), (0, 0), (0, 0)))
    vp = jnp.pad(vs, ((0, 0), (span, 0), (0, 0), (0, 0)))
    idx = jnp.arange(nb)[:, None] * bq + jnp.arange(bq + span)[None, :]
    kb = kp[:, idx]
    vb = vp[:, idx]
    qb = qs.reshape(n, nb, bq, h, dh)
    logits = jnp.einsum("nbqhd,nbkhd->nbhqk", qb, kb) / math.sqrt(dh)
    rel = jnp.arange(bq)[:, None] - jnp.arange(bq + span)[None, :] + span
    valid = ((rel >= 0) & (rel <= span))[None] & ((idx - span) >= 0)[:, None, :]
    bias = rel_bias.astype(jnp.float32)[t5_bucket(jnp.clip(rel, 0, span) * dilation)]
    logits = logits + jnp.transpose(bias, (2, 0, 1))[None, None]
    logits = jnp.where(valid[None, :, None], logits, -jnp.inf)
    m = jnp.max(logits, axis=-1)
    p = jnp.exp(logits - m[..., None])
    den = jnp.sum(p, axis=-1)
    u = jnp.einsum("nbhqk,nbkhd->nbqhd", p, vb)
    m = jnp.transpose(m, (0, 1, 3, 2))
    den = jnp.transpose(den, (0, 1, 3, 2))
    return from_sub(u), from_sub(m), from_sub(den)

def stick_breaking(q, k, v):
    b, s, h, dh = q.shape
    nb = s // BLOCK_Q
    qb = jnp.moveaxis(q.reshape(b, nb, BLOCK_Q, h, dh), 1, 0)
    kpos = jnp.arange(s)

    def one_block(args):
        qi, start = args
        z = jnp.einsum("bqhd,bkhd->bhqk", qi, k) / math.sqrt(dh)
        qpos = start + jnp.arange(BLOCK_Q)
        before = (kpos[None, :] < qpos[:, None])[None, None]
        log_beta = jax.nn.log_sigmoid(z)
        log_rest = jnp.where(before, log_beta - z, 0.0)
        later = lax.cumsum(log_rest, axis=3, reverse=True) - log_rest
        a = jnp.where(before, jnp.exp(log_beta + later), 0.0)
        return jnp.einsum("bhqk,bkhd->bqhd", a, v)

    o = lax.map(one_block, (qb, jnp.arange(nb) * BLOCK_Q))
    return jnp.moveaxis(o, 0, 1).reshape(b, s, h, dh)

def even_mixer(h, w_in, w_out, w_sc, rel_bias):
    b, s, _ = h.shape
    p = h @ w_in
    o1 = SC_WIDTH
    o3 = 3 * SC_WIDTH
    gate_b, gate_c, xa, q, k, v = jnp.split(
        p, [o1, 2 * o1, o3, o3 + DA_WIDTH, o3 + 2 * DA_WIDTH], axis=-1)
    y_a = gate_b * causal_dwconv(gate_c * xa, w_sc)
    heads = lambda t: t.reshape(b, s, DA_HEADS, HEAD_DIM_2).astype(jnp.float32)
    q, k, v = heads(q), heads(k), heads(v)
    outs = [dilated_branch(q, k, v, win // dil, dil, rel_bias) for win, dil in DA_PAIRS]
    u = jnp.stack([o[0] for o in outs])
    m = jnp.stack([o[1] for o in outs])
    den = jnp.stack([o[2] for o in outs])
    wgt = jnp.exp(m - jnp.max(m, axis=0, keepdims=True))
    o = jnp.einsum("gbsh,gbshd->bshd", wgt, u) / jnp.sum(wgt * den, axis=0)[..., None]
    y_b = o.reshape(b, s, DA_WIDTH).astype(h.dtype)
    return jnp.concatenate([y_a, y_b], axis=-1) @ w_out

def odd_mixer(h, w_in, w_out, w_cc, b_cc, ln_g, ln_b):
    b, s, _ = h.shape
    p = h @ w_in
    c2 = 2 * CC_WIDTH
    a, gate, q, k, v = jnp.split(
        p, [CC_WIDTH, c2, c2 + SB_WIDTH, c2 + 2 * SB_WIDTH], axis=-1)
    g = a * jax.nn.sigmoid(gate)
    g = causal_dwconv(g, w_cc) + b_cc.astype(g.dtype)
    y_c = jax.nn.silu(layer_norm(g, ln_g, ln_b))
    heads = lambda t: t.reshape(b, s, SB_HEADS, HEAD_DIM_2).astype(jnp.float32)
    y_d = stick_breaking(heads(q), heads(k), heads(v)).reshape(b, s, SB_WIDTH).astype(h.dtype)
    return jnp.concatenate([y_c.astype(h.dtype), y_d], axis=-1) @ w_out

def conv_ffn(h, w_up, w_conv, b_conv, w_down):
    g, u = jnp.split(h @ w_up, 2, axis=-1)
    g = causal_dwconv(g, w_conv) + b_conv.astype(g.dtype)
    return (jax.nn.silu(g) * u) @ w_down

def second_inputs(seed: int = 0) -> dict:
    key = jax.random.key(seed)
    ks = jax.random.split(key, 20)
    nrm = lambda k, shape, scale: jax.random.normal(k, shape, jnp.float32) * scale
    return {
        "x": nrm(ks[0], (BATCH, SEQ, D_MODEL), 1.0),
        "norm_g": 1.0 + nrm(ks[1], (DEPTH_2, 4, D_MODEL), 0.05),
        "rel_bias": nrm(ks[2], (REL_BUCKETS, DA_HEADS), 0.5),
        "w_in_even": nrm(ks[3], (N_EVEN, D_MODEL, EVEN_IN), D_MODEL ** -0.5),
        "w_out_even": nrm(ks[4], (N_EVEN, EVEN_MIX, D_MODEL), EVEN_MIX ** -0.5),
        "w_sc": nrm(ks[5], (N_EVEN, SC_TAPS, SC_WIDTH), SC_TAPS ** -0.5),
        "w_in_odd": nrm(ks[6], (N_ODD, D_MODEL, ODD_IN), D_MODEL ** -0.5),
        "w_out_odd": nrm(ks[7], (N_ODD, ODD_MIX, D_MODEL), ODD_MIX ** -0.5),
        "w_cc": nrm(ks[8], (N_ODD, CC_TAPS, CC_WIDTH), CC_TAPS ** -0.5),
        "b_cc": nrm(ks[9], (N_ODD, CC_WIDTH), 0.02),
        "ln_cc_g": 1.0 + nrm(ks[10], (N_ODD, CC_WIDTH), 0.05),
        "ln_cc_b": nrm(ks[11], (N_ODD, CC_WIDTH), 0.02),
        "w_up": nrm(ks[12], (DEPTH_2, D_MODEL, 2 * D_FF), D_MODEL ** -0.5),
        "w_ffn_conv": nrm(ks[13], (DEPTH_2, FFN_TAPS, D_FF), FFN_TAPS ** -0.5),
        "b_ffn_conv": nrm(ks[14], (DEPTH_2, D_FF), 0.02),
        "w_down": nrm(ks[15], (DEPTH_2, D_FF, D_MODEL), D_FF ** -0.5),
    }

def second_block(x, norm_g, rel_bias, w_in_even, w_out_even, w_sc, w_in_odd, w_out_odd,
              w_cc, b_cc, ln_cc_g, ln_cc_b, w_up, w_ffn_conv, b_ffn_conv, w_down):
    for layer in range(DEPTH_2):
        h = rms_norm(x, norm_g[layer, 0])
        if layer % 2 == 0:
            i = layer // 2
            mix = even_mixer(h, w_in_even[i], w_out_even[i], w_sc[i], rel_bias)
        else:
            i = layer // 2
            mix = odd_mixer(h, w_in_odd[i], w_out_odd[i], w_cc[i], b_cc[i], ln_cc_g[i], ln_cc_b[i])
        x = x + rms_norm(mix, norm_g[layer, 1])
        h = rms_norm(x, norm_g[layer, 2])
        x = x + rms_norm(conv_ffn(h, w_up[layer], w_ffn_conv[layer], b_ffn_conv[layer], w_down[layer]),
                         norm_g[layer, 3])
    return x


def setup_inputs(seed=0):
    out = dict(first_inputs(seed))
    for name, value in second_inputs(seed + 1).items():
        if name != "x":
            out[name + "_2"] = value
    return out


def reference(
    x, norm_ffn1, w_ffn1_gu, w_ffn1_down, norm_mix, w_in, conv_w, conv_b, lru_w_gates,
    lru_b_gates, lru_lambda, q_norm, k_norm, rel_pos_bias, w_out, norm_ffn2, w_ffn2_gu,
    w_ffn2_down, norm_g_2, rel_bias_2, w_in_even_2, w_out_even_2, w_sc_2, w_in_odd_2,
    w_out_odd_2, w_cc_2, b_cc_2, ln_cc_g_2, ln_cc_b_2, w_up_2, w_ffn_conv_2, b_ffn_conv_2,
    w_down_2,
):
    x = first_block(
        x, norm_ffn1, w_ffn1_gu, w_ffn1_down, norm_mix, w_in, conv_w, conv_b, lru_w_gates,
        lru_b_gates, lru_lambda, q_norm, k_norm, rel_pos_bias, w_out, norm_ffn2, w_ffn2_gu,
        w_ffn2_down,
    )
    return second_block(
        x, norm_g_2, rel_bias_2, w_in_even_2, w_out_even_2, w_sc_2, w_in_odd_2, w_out_odd_2,
        w_cc_2, b_cc_2, ln_cc_g_2, ln_cc_b_2, w_up_2, w_ffn_conv_2, b_ffn_conv_2, w_down_2,
    )


_drawn_inputs = setup_inputs


def setup_inputs(seed=0):
    import zlib

    import numpy as np

    out = dict(_drawn_inputs(seed))
    spreads = {}
    factors = {'norm_ffn1': 3.245,
     'norm_mix': 3.57,
     'q_norm': 8.0,
     'k_norm': 8.0,
     'rel_pos_bias': 14.614,
     'norm_ffn2': 13.157,
     'b_cc_2': 133.9,
     'ln_cc_b_2': 200.0,
     'b_ffn_conv_2': 123.933,
     'conv_b': 2.892,
     'norm_g_2': 18.804,
     'rel_bias_2': 63.088,
     'ln_cc_g_2': 64.0}
    for name, (base, spread) in spreads.items():
        noise = np.random.default_rng([zlib.crc32(name.encode()), seed]).standard_normal(out[name].shape)
        drawn = base * np.exp(spread * noise) if base else spread * noise
        out[name] = __import__('jax').numpy.asarray(drawn.astype(out[name].dtype))
    for name, factor in factors.items():
        out[name] = (out[name] * factor).astype(out[name].dtype)
    return out
```

```python
from collections import namedtuple
from contextlib import ExitStack

import numpy as np
import concourse.bass as bass
from concourse import mybir

P = 128
SEQ = 512
D = 1024
DT = D // P
FF = 2816
FT = FF // P
EPS = 1e-6
GRID_W, ROWS = 64, 8
RPB_DR, RPB_DC, RPB_W = 15, 31, 64
RUN = 7 * RPB_W + 48
NEG = -1.0e30
LAM_ABS = 7
SMALL = 24
MEMSETS = 3
HALF_W = 512
GELU_C = 0.7978845608028654
KSTART = (0, 8, 24, 32)
MASK_OF = (0, 1, 1, 2)
DIST = 640

F32 = mybir.dt.float32
F32R = mybir.dt.float32r
ALU = mybir.AluOpType
ACT = mybir.ActivationFunctionType

COLS = {}
_at = 0
for _name, _n in (("norm_ffn1", 8), ("norm_mix", 8), ("norm_ffn2", 8), ("conv_w", 32), ("conv_b", 8), ("lru_b_gates", 32),
                  ("lru_lambda", 16), ("q_norm", 1), ("k_norm", 1), ("norm_g_2", 64), ("w_sc_2", 12), ("w_cc_2", 124),
                  ("b_cc_2", 4), ("ln_cc_g_2", 4), ("ln_cc_b_2", 4), ("w_ffn_conv_2", 132), ("b_ffn_conv_2", 44)):
    COLS[_name] = _at
    _at += _n
N_COLS = _at


def Names(**things):
    return namedtuple("Names", list(things))(**things)


def wait(eng, sem, value):
    if not (isinstance(value, int) and value <= 0):
        eng.wait_ge(sem, value)


def own_wait(eng, held):
    eng.sem_inc(held, 1)


class Stream:

    units_before = 0
    loads_before = [0] * 5

    def __init__(self, dram, bodies, per, K):
        self.dram, self.bodies, self.per, self.K = dram, bodies, per, K
        self.raw = {4: (0, 1, 2, 3), 5: (0, 1, 2, 3, 4), 6: (0, 1, 2, 3, 4, 2), 7: (0, 1, 2, 3, 4, 2, 3)}[per]
        self.split = {(4, 8): (0, 1, 2, 3), (4, 11): (0, 1, 2, 1), (5, 8): (0, 1, 2, 3, 2), (6, 8): (0, 1, 2, 3, 0, 1),
                      (7, 8): (0, 1, 2, 3, 0, 1, 2)}[per, K]
        self.bank = {4: (0, 1, 2, 3), 5: (0, 1, 2, 3, 0), 6: (0, 1, 2, 3, 0, 1), 7: (0, 1, 2, 3, 0, 1, 2)}[per]
        self.n0 = Stream.units_before
        self.l0 = list(Stream.loads_before)
        Stream.units_before += bodies * per
        Stream.loads_before = [l + bodies * self.raw.count(s) for s, l in enumerate(self.l0)]

    def done(self, i, j):
        return self.n0 + self.per * i + (j + 1)

    def before(self, ring, i, j):
        back = next(b for b in range(1, self.per + 1) if ring[(j - b) % self.per] == ring[j])
        if isinstance(i, int) and i == 0 and j - back < 0:
            return self.n0
        return self.n0 + self.per * i + (j - back + 1)

    def loaded(self, i, j):
        s = self.raw[j]
        return 16 * (self.l0[s] + self.raw[:j + 1].count(s)) + 16 * self.raw.count(s) * i


def gated_recurrence_mixer(k, st, t, h1):
    bank, S, free, scratch = k.bank, k.S, k.free, k.scratch
    N = st.bodies
    free("m1")
    xr = scratch("m1", "xr", [516])
    gr = scratch("m1", "gr", [SEQ])
    qk = scratch("m1", "qk", [2, SEQ])
    vT = scratch("m1", "vT", [SEQ])
    tha = scratch("m1", "tha", [SEQ])
    thb = scratch("m1", "thb", [SEQ])
    xc = scratch("m1", "xc", [SEQ])
    qkr = scratch("m1", "qkr", [2, SEQ])
    qkn = scratch("m1", "qkn", [2, SEQ])
    g2 = scratch("m1", "g2", [SEQ])
    gate_a = scratch("m1", "gate_a", [SEQ])
    gate_b = scratch("m1", "gate_b", [SEQ])
    y1 = scratch("m1", "y1", [SEQ])
    y = scratch("m1", "y", [SEQ])
    ti = scratch("m1", "ti", [2, SEQ])
    t2 = scratch("m1", "t2", [2, SEQ])
    sq = scratch("m1", "sq", [2, SEQ])
    la = scratch("m1", "la", [2, SEQ])
    sqk = la
    prob = scratch("m1", "prob", [2, SEQ])
    probT = scratch("m1", "probT", [2, SEQ])
    v_tok = scratch("m1", "v_tok", [7, P])
    run = scratch("m1", "run", [2, RUN])
    bias = scratch("m1", "bias", [2, 4, 256])
    mask = scratch("m1", "mask", [3, 256])
    gate_w = scratch("m1", "gate_w", [4, P])
    mx = scratch("m1", "mx", [8])
    den = scratch("m1", "den", [8])
    M = k.sems("m1_", "evac gab_free zeroed sqk g2 g2p gth gelu qk_stat qk_rs qk_rr qkn conv gates gate_act t2_sqrt lru ix "
                      "v_tr v_ev scores biased negmax exps rden scaled p_tr p_ev pv bias_ready run_loaded gw_loaded "
                      "mask_loaded y1 gab yatt_used y_f y_hi y_ready hsum")
    PER = st.per

    def perm(ap):
        return ap.rearrange("p (c r) -> p r c", r=ROWS)

    def rows_of(ap):
        return ap.rearrange("p (r c) -> p r c", c=GRID_W)

    def load_params(sp, u):
        wait(sp, M.gates, 4 * u)
        src = t["gate_w"][u] if isinstance(u, int) else t["gate_w"][bass.ds(u, 1)].rearrange("a p g n -> p (a g) n")
        sp.dma_start(gate_w[:], src).then_inc(M.gw_loaded, 16)
        wait(sp, M.bias_ready, 8 * u)
        tab = t["rpb"]
        for r in range(ROWS):
            src = bass.AP(tensor=tab.tensor, offset=RPB_DR * RPB_W * 2 * u + (r * RPB_W + 1),
                          ap=[[1, 16], [RPB_DR * RPB_W, 2], [1, RUN]])
            sp.dma_start(run[r:P:ROWS], src).then_inc(M.run_loaded, 16)

    def sp(sp):
        for j in range(5):
            k.load_unit(sp, st, 0, j)
        sp.wait_ge(S.h_ready, h1)
        sp.dma_start(mask[:], t["win_mask"]).then_inc(M.mask_loaded, 16)
        load_params(sp, 0)
        for j in range(5, PER):
            k.load_unit(sp, st, 0, j)
        for j in range(PER):
            k.load_unit(sp, st, 1, j)
            if j == 4:
                load_params(sp, 1)
        with sp.Fori(2, N) as u:
            for j in range(PER):
                k.load_unit(sp, st, u, j)
                if j == 4:
                    load_params(sp, u)

    def evac(act, u, j):
        act.wait_ge(S.mm_done, st.done(u, j))
        src = bank[st.bank[j]][:]
        if j == 0:
            wait(act, M.conv, 4 * u)
            act.activation(xr[:, 2:2 + SEQ], src, ACT.Copy).then_inc(M.evac, 1)
        elif j == 1:
            wait(act, M.gelu, 2 * u)
            act.activation(gr[:], src, ACT.Copy).then_inc(M.evac, 1)
        elif j in (2, 3):
            wait(act, M.qkn, 2 * u)
            act.activation(qk[:, j - 2], src, ACT.Copy).then_inc(M.evac, 1)
        elif j == 4:
            wait(act, M.v_tr, 2 * u)
            act.activation(perm(vT[:]), rows_of(src), ACT.Copy).then_inc(M.evac, 1)
        else:
            wait(act, M.gab, 2 * u)
            act.activation((tha, thb)[j - 5][:], src, ACT.Tanh, scale=0.5).then_inc(M.evac, 1)

    def act_probs(act, p, s):
        act.wait_ge(M.negmax, 4 * p + (s + 1))
        for b in range(2):
            e = 2 * s + b
            act.activation(prob[:, s % 2, 256 * b:256 * b + 256], prob[:, s % 2, 256 * b:256 * b + 256], ACT.Exp,
                           bias=mx[:, e:e + 1], accum_out=den[:, e:e + 1]).then_inc(M.exps, 1)

    def act_probT(act, p, s):
        act.wait_ge(M.p_tr, 4 * p + (s + 1))
        wait(act, M.pv, 4 * p + (s - 1))
        act.activation(probT[:, s % 2], bank[6][:], ACT.Copy).then_inc(M.p_ev, 1)

    def act_gates(act, p, d):
        for g, dst in ((0, t2), (1, ti)):
            act.wait_ge(M.gates, 4 * p + (2 * d + g + 1))
            wait(act, M.lru, 6 * p + (3 * d - 3))
            n = (2 * d + g) * 8
            act.activation(dst[:, d], bank[4 + g][:], ACT.Tanh, scale=0.5, bias=k.colat(k.hbg, n, p))\
               .then_inc(M.gate_act, 1)
        act.wait_ge(M.gate_act, 8 * p + (4 * d + 1))
        act.wait_ge(M.qk_stat, 2 * p + 2)
        sc = k.colat(k.nsp4, 8 * d, p)
        act.activation(la[:, d], t2[:, d], ACT.Exp, scale=sc, bias=sc).then_inc(M.gate_act, 1)
        sc = k.colat(k.sp2, 8 * d, p)
        act.activation(t2[:, d], t2[:, d], ACT.Tanh, scale=sc, bias=sc).then_inc(M.gate_act, 1)

    def act(act):
        def body(p, units, prev, tail):
            u = p + 1

            def slot(j):
                if units:
                    k.split_hi(act, st, u, j)
            slot(0)
            if tail:
                act_probT(act, p - 1, 2)
            if prev:
                evac(act, p, 5)
                for n in range(2):
                    wait(act, M.lru, 6 * p)
                    act.wait_ge(M.evac, PER * p + (3 + n))
                    act.activation(sqk[:, n], qk[:, n], ACT.Square).then_inc(M.sqk, 1)
                wait(act, M.y1, 2 * p)
                act.activation(g2[:], gr[:], ACT.Square).then_inc(M.g2, 1)
            slot(1)
            if tail:
                act_probT(act, p - 1, 3)
            if prev:
                evac(act, p, 6)
                act.wait_ge(M.g2p, 2 * p + 2)
                act.activation(g2[:], g2[:], ACT.Tanh, scale=GELU_C).then_inc(M.gth, 1)
            slot(2)
            if units:
                evac(act, u, 0)
            slot(3)
            if units:
                evac(act, u, 1)
            if tail:
                act.wait_ge(M.y_f, p)
                act.activation(k.tile_of(k.aH, p - 1), y[:], ACT.Copy).then_inc(M.y_hi, 1)
            if prev:
                for n in range(2):
                    act.wait_ge(M.qk_stat, 2 * p + (n + 1))
                    act.activation(qkr[:, n], bank[6 + n][:], ACT.Ln, bias=k.eps_col[:]).then_inc(M.qk_rs, 1)
                for n in range(2):
                    act.wait_ge(M.qk_rs, 4 * p + (n + 1))
                    act.activation(qkr[:, n], qkr[:, n], ACT.Exp, scale=-0.5).then_inc(M.qk_rs, 1)
                act_gates(act, p, 0)
            slot(4)
            if prev:
                act_gates(act, p, 1)
                wait(act, M.hsum, p)
                for d in range(2):
                    act.wait_ge(M.gate_act, 8 * p + (4 * d + 4))
                    act.activation(sq[:, d], t2[:, d], ACT.Sqrt).then_inc(M.t2_sqrt, 1)
                act.wait_ge(M.v_tr, 2 * p + 1)
                act.activation(v_tok[:, 0:4], bank[6][:].rearrange("p (a n) -> p a n", a=4), ACT.Copy)\
                   .then_inc(M.v_ev, 1)
            if units:
                evac(act, u, 2)
            slot(5)
            if units:
                evac(act, u, 3)
            if prev:
                act.wait_ge(M.v_tr, 2 * p + 2)
                act.activation(v_tok[:, 4:7], bank[6][:, 0:384].rearrange("p (a n) -> p a n", a=3), ACT.Copy)\
                   .then_inc(M.v_ev, 1)
            slot(6)
            if units:
                evac(act, u, 4)
            if prev:
                act_probs(act, p, 0)
                act_probs(act, p, 1)
                act_probT(act, p, 0)
                act_probs(act, p, 2)
                act_probs(act, p, 3)
                act_probT(act, p, 1)
        body(-1, True, False, False)
        body(0, True, True, False)
        with act.Fori(1, N - 1) as p:
            body(p, True, True, True)
        body(N - 1, False, True, True)
        act_probT(act, N - 1, 2)
        act_probT(act, N - 1, 3)
        act.wait_ge(M.y_f, N)
        act.activation(k.tile_of(k.aH, N - 1), y[:], ACT.Copy).then_inc(M.y_hi, 1)

    def dve_scores(dve, p, s):
        dve.wait_ge(M.scores, 4 * p + (s + 1))
        wait(dve, M.p_tr, 4 * p + (s - 1))
        if s == 0:
            dve.wait_ge(M.bias_ready, 8 * p + 8)
        hh, pr = s // 2, s % 2
        for b in range(2):
            e = 2 * s + b
            own_wait(dve, k.held_dve)
            dve.tensor_tensor_reduce(out=prob[:, s % 2, 256 * b:256 * b + 256],
                                     in0=bank[4 + s % 2][:, 256 * b:256 * b + 256], in1=bias[:, hh, 2 * pr + b],
                                     scale=1.0, scalar=-3.0e38, op0=ALU.add, op1=ALU.max,
                                     accum_out=mx[:, e:e + 1]).then_inc(M.biased, 1)
        dve.wait_ge(M.biased, 8 * p + (2 * s + 2))
        dve.tensor_scalar(mx[:, 2 * s:2 * s + 2], mx[:, 2 * s:2 * s + 2], -1.0, None, ALU.mult).then_inc(M.negmax, 1)

    def dve_scale(dve, p, s):
        dve.wait_ge(M.exps, 8 * p + (2 * s + 2))
        dve.reciprocal(den[:, 2 * s:2 * s + 2], den[:, 2 * s:2 * s + 2]).then_inc(M.rden, 1)
        dve.wait_ge(M.rden, 4 * p + (s + 1))
        pair = den[:, 2 * s:2 * s + 2]
        by = bass.AP(tensor=pair.tensor, offset=pair.offset, ap=[pair.ap[0], [1, 2], [0, 256]])
        both = prob[:, s % 2].rearrange("p (b n) -> p b n", b=2)
        dve.tensor_tensor(both, both, by, ALU.mult).then_inc(M.scaled, 1)

    def dve_ix(dve, p, d):
        dve.wait_ge(M.gate_act, 8 * p + (4 * d + 2))
        dve.scalar_tensor_tensor(ti[:, d], ti[:, d], 1.0, xc[:], ALU.add, ALU.mult).then_inc(M.ix, 1)

    def dve_lru(dve, p, d):
        dve.wait_ge(M.t2_sqrt, 2 * p + (d + 1))
        dve.wait_ge(M.ix, 2 * p + (d + 1))
        dve.tensor_tensor(ti[:, d], ti[:, d], sq[:, d], ALU.mult).then_inc(M.lru, 1)
        dve.wait_ge(M.lru, 6 * p + (3 * d + 1))
        dve.scalar_tensor_tensor(ti[:, d], la[:, d], 1.0, ti[:, d], ALU.add, ALU.mult).then_inc(M.lru, 1)
        dve.wait_ge(M.lru, 6 * p + (3 * d + 2))
        o_, a_, b_ = (x[:, d] if d == 0 else x[:, d, ::-1] for x in (sq, la, ti))
        dve.tensor_tensor_scan(out=o_, data0=a_, data1=b_, initial=0.0, op0=ALU.mult, op1=ALU.add).then_inc(M.lru, 1)

    def dve_tail(dve, q):
        dve.wait_ge(M.pv, 4 * q + 4)
        dve.wait_ge(M.gab, 2 * q + 2)
        wait(dve, M.y_hi, q)
        wait(dve, M.y_ready, q)
        dve.tensor_tensor(rows_of(y[:]), perm(bank[7][:]), rows_of(gate_b[:]), ALU.mult).then_inc(M.yatt_used, 1)
        dve.wait_ge(M.yatt_used, q + 1)
        dve.wait_ge(M.y1, 2 * q + 2)
        dve.tensor_tensor(y[:], y[:], y1[:], ALU.add).then_inc(M.y_f, 1)

    def dve_low(dve, q):
        dve.wait_ge(M.y_hi, q + 1)
        dve.tensor_tensor(k.tile_of(k.aL, q), y[:], k.tile_of(k.aH, q).bitcast(F32), ALU.subtract)\
           .then_inc(M.y_ready, 1)

    def dve(dve):
        def body(p, units, prev, tail):
            u = p + 1

            def slot(j):
                if units:
                    k.split_lo(dve, st, u, j)
            slot(0)
            if prev:
                dve.wait_ge(M.evac, PER * p + 1)
                dve.wait_ge(M.zeroed, 2)
                wait(dve, M.gates, 4 * p)
                dve.tensor_scalar(xc[:], xr[:, 0:SEQ], k.colr("conv_w", p), k.colr("conv_b", p), ALU.mult, ALU.add)\
                   .then_inc(M.conv, 1)
                for n in range(1, 4):
                    dve.wait_ge(M.conv, 4 * p + n)
                    dve.scalar_tensor_tensor(xc[:], xr[:, n:n + SEQ], k.colr("conv_w", 8 * n + p), xc[:], ALU.mult,
                                             ALU.add).then_inc(M.conv, 1)
            slot(1)
            slot(2)
            if tail:
                dve_tail(dve, p - 1)
            slot(3)
            if tail:
                dve_low(dve, p - 1)
            if prev:
                for n in range(2):
                    dve.wait_ge(M.qk_rs, 4 * p + (n + 3))
                    src, by = qk[:, n], qkr[:, n]
                    dve.scalar_tensor_tensor(perm(qkn[:, n]), rows_of(src), k.qg[:] if n == 0 else k.col("k_norm"),
                                             rows_of(by), ALU.mult, ALU.mult).then_inc(M.qkn, 1)
                dve_ix(dve, p, 0)
            slot(4)
            if prev:
                dve_ix(dve, p, 1)
            slot(5)
            if prev:
                dve_lru(dve, p, 0)
                dve_lru(dve, p, 1)
            slot(6)
            if prev:
                dve_scores(dve, p, 0)
                dve_scores(dve, p, 1)
                dve_scale(dve, p, 0)
                dve_scale(dve, p, 1)
                dve_scores(dve, p, 2)
                dve_scale(dve, p, 2)
                dve_scores(dve, p, 3)
                dve_scale(dve, p, 3)
        dve.memset(xr[:, 0:2], 0.0).then_inc(M.zeroed, 1)
        dve.memset(xr[:, 2 + SEQ:3 + SEQ], 0.0).then_inc(M.zeroed, 1)
        body(-1, True, False, False)
        body(0, True, True, False)
        with dve.Fori(1, N - 1) as p:
            body(p, True, True, True)
        body(N - 1, False, True, True)
        dve_tail(dve, N - 1)
        dve_low(dve, N - 1)

    def pe_scores(pe, p, s):
        hh, pr = s // 2, s % 2
        if s < 2:
            pe.wait_ge(M.qkn, 2 * p + 2)
            pe.wait_ge(M.gate_act, 8 * p + (5 + s))
        else:
            pe.wait_ge(M.biased, 8 * p + 2 * (s - 1))
        for b in range(2):
            n = 2 * pr + b
            last = pe.matmul(bank[4 + s % 2][:, 256 * b:256 * b + 256],
                             qkn[64 * hh:64 * hh + 64, 0, P * n:P * n + P],
                             qkn[64 * hh:64 * hh + 64, 1, KSTART[n] * ROWS:KSTART[n] * ROWS + 256],
                             start=True, stop=True)
        last.then_inc(M.scores, 1)

    def pe_probT(pe, p, s):
        pe.wait_ge(M.scaled, 4 * p + (s + 1))
        if s == 0:
            pe.wait_ge(M.v_ev, 2 * p + 2)
        else:
            pe.wait_ge(M.p_ev, 4 * p + s)
        for n in range(4):
            last = pe.transpose(bank[6][:, P * n:P * n + P], prob[:, s % 2, P * n:P * n + P], k.ident[:])
        last.then_inc(M.p_tr, 1)

    def pe_pv(pe, p, s):
        hh, pr = s // 2, s % 2
        pe.wait_ge(M.p_ev, 4 * p + (s + 1))
        if s == 0:
            wait(pe, M.yatt_used, p)
        for b in range(2):
            n = 2 * pr + b
            off = KSTART[n] * ROWS
            for c in range(2):
                o_ = off + P * c
                vt = o_ // P if o_ % P == 0 else 4 + o_ // P
                last = pe.matmul(bank[7][64 * hh:64 * hh + 64, P * n:P * n + P], v_tok[:, vt, 64 * hh:64 * hh + 64],
                                 probT[:, s % 2, 256 * b + P * c:256 * b + P * c + P], start=c == 0, stop=c == 1)
        last.then_inc(M.pv, 1)

    def pe_gates(pe, p, d):
        for g in range(2):
            if d == 1:
                pe.wait_ge(M.gate_act, 8 * p + (g + 1))
            pe.matmul(bank[4 + g][:], gate_w[:, 2 * d + g], xc[:], start=True, stop=True).then_inc(M.gates, 1)

    def pe(pe, h0):
        def body(p, units, prev, tail):
            u = p + 1

            def unit(j):
                if not units:
                    return
                back = next(b for b in range(1, PER + 1) if st.bank[(j - b) % PER] == st.bank[j])
                wait(pe, M.evac, PER * u + (j - back + 1))
                ready = (lambda kk: pe.wait_ge(S.h_ready, h0 - 8 + kk + 1)) if isinstance(u, int) and u == 0 and j == 0 \
                    else None
                k.unit_product(pe, st, u, j, bank[st.bank[j]][:], (k.hH, k.hL), 0, True, True, ready)
            unit(0)
            if tail:
                pe_pv(pe, p - 1, 2)
                pe_probT(pe, p - 1, 3)
                pe_pv(pe, p - 1, 3)
            unit(1)
            if prev:
                pe.wait_ge(M.conv, 4 * p + 4)
                pe.wait_ge(M.gw_loaded, 16 * p + 16)
                wait(pe, M.biased, 8 * p)
                pe_gates(pe, p, 0)
                for n in range(2):
                    pe.wait_ge(M.sqk, 2 * p + (n + 1))
                    if n == 0:
                        wait(pe, M.p_ev, 4 * p)
                    else:
                        wait(pe, M.yatt_used, p)
                    pe.matmul(bank[6 + n][:], k.heads1[:], sqk[:, n], start=True, stop=True).then_inc(M.qk_stat, 1)
            unit(2)
            if prev:
                pe_gates(pe, p, 1)
                pe.wait_ge(M.evac, PER * p + 5)
                pe.wait_ge(M.qk_rs, 4 * p + 1)
                for n in range(4):
                    last = pe.transpose(bank[6][:, P * n:P * n + P], vT[:, P * n:P * n + P], k.ident[:])
                last.then_inc(M.v_tr, 1)
            unit(3)
            if prev:
                pe_scores(pe, p, 0)
                pe_scores(pe, p, 1)
                pe.wait_ge(M.v_ev, 2 * p + 1)
                for n in range(3):
                    last = pe.transpose(bank[6][:, P * n:P * n + P], vT[:, 64 + P * n:64 + P * n + P], k.ident[:])
                last.then_inc(M.v_tr, 1)
            unit(4)
            if prev:
                pe_probT(pe, p, 0)
                pe_scores(pe, p, 2)
            unit(5)
            if prev:
                pe.wait_ge(M.qk_rs, 4 * p + 2)
                pe_pv(pe, p, 0)
                pe_probT(pe, p, 1)
                pe_scores(pe, p, 3)
            unit(6)
            if prev:
                pe_pv(pe, p, 1)
                pe_probT(pe, p, 2)
        pe.wait_ge(S.consts, 48)
        body(-1, True, False, False)
        body(0, True, True, False)
        with pe.Fori(1, N - 1) as p:
            body(p, True, True, True)
        body(N - 1, False, True, True)
        pe_pv(pe, N - 1, 2)
        pe_probT(pe, N - 1, 3)
        pe_pv(pe, N - 1, 3)

    def pool(pool):
        def body(p):
            pool.wait_ge(M.run_loaded, 16 * ROWS * p + 16 * ROWS)
            wait(pool, M.biased, 8 * p)
            for hh in range(2):
                for n in range(4):
                    first = KSTART[n] - 16 * n + 16
                    src = bass.AP(tensor=run[:].tensor, offset=run[:, hh, RUN - 1 - first:RUN - first].offset,
                                  ap=[run[:].ap[0], [-1, 32], [-RPB_W, 8]])
                    pool.tensor_tensor(bias[:, hh, n].rearrange("p (c r) -> p c r", r=ROWS), src,
                                       mask[:, MASK_OF[n]].rearrange("p (c r) -> p c r", r=ROWS),
                                       ALU.add).then_inc(M.bias_ready, 1)
            pool.wait_ge(M.g2, p + 1)
            own_wait(pool, k.held_pool)
            pool.tensor_scalar(g2[:], g2[:], 0.044715, 1.0, ALU.mult, ALU.add).then_inc(M.g2p, 1)
            pool.wait_ge(M.g2p, 2 * p + 1)
            pool.tensor_tensor(g2[:], g2[:], gr[:], ALU.mult).then_inc(M.g2p, 1)
            pool.wait_ge(M.gth, p + 1)
            own_wait(pool, k.held_pool)
            pool.tensor_scalar(g2[:], g2[:], 1.0, None, ALU.add).then_inc(M.gelu, 1)
            pool.wait_ge(M.gelu, 2 * p + 1)
            wait(pool, M.hsum, p)
            pool.tensor_tensor(g2[:], g2[:], gr[:], ALU.mult).then_inc(M.gelu, 1)
            pool.wait_ge(M.evac, PER * p + 7)
            wait(pool, M.y1, 2 * p)
            own_wait(pool, k.held_pool)
            pool.tensor_scalar(gate_a[:], tha[:], 1.0, 0.125, ALU.add, ALU.mult).then_inc(M.gab, 1)
            wait(pool, M.yatt_used, p)
            own_wait(pool, k.held_pool)
            pool.tensor_scalar(gate_b[:], thb[:], 1.0, 0.5, ALU.add, ALU.mult).then_inc(M.gab, 1)
            pool.wait_ge(M.lru, 6 * p + 6)
            wait(pool, M.y_f, p)
            pool.tensor_tensor(y1[:], sq[:, 0], sq[:, 1], ALU.add).then_inc(M.hsum, 1)
            pool.wait_ge(M.hsum, p + 1)
            pool.wait_ge(M.gelu, 2 * p + 2)
            pool.tensor_tensor(y1[:], y1[:], g2[:], ALU.mult).then_inc(M.y1, 1)
            pool.wait_ge(M.y1, 2 * p + 1)
            pool.wait_ge(M.gab, 2 * p + 2)
            pool.tensor_tensor(y1[:], y1[:], gate_a[:], ALU.mult).then_inc(M.y1, 1)
        pool.wait_ge(M.mask_loaded, 16)
        body(0)
        with pool.Fori(1, N) as p:
            body(p)

    return Names(sp=sp, act=act, dve=dve, pe=pe, pool=pool, y_ready=lambda pe: lambda f: pe.wait_ge(M.y_ready, f + 1))


def score_tile(i):
    return P * (i + 1)


def conv_attention_mixer(k, st, t, h1):
    bank, S, scratch = k.bank, k.S, k.scratch
    N, PER = st.bodies, st.per
    k.free("m2")
    gb = scratch("m2", "gb", [SEQ])
    gc = scratch("m2", "gc", [SEQ])
    xa = scratch("m2", "xa", [SEQ])
    cu = scratch("m2", "cu", [SEQ])
    cc = scratch("m2", "cc", [SEQ])
    yc = scratch("m2", "yc", [SEQ])
    y = scratch("m2", "y", [SEQ])
    qk = scratch("m2", "qk", [2, SEQ])
    vT = scratch("m2", "vT", [SEQ])
    prob = scratch("m2", "prob", [4, SEQ])
    probT = scratch("m2", "probT", [2, SEQ])
    v_tok = scratch("m2", "v_tok", [4, P])
    bias = scratch("m2", "bias", [2, SEQ])
    mx = scratch("m2", "mx", [8])
    den = scratch("m2", "den", [8])
    buckets = scratch("m2", "buckets", [DIST + 8])
    dist_add = scratch("m2", "dist_add", [DIST])
    table = scratch("m2", "table", [DIST])
    M = k.sems("m2_", "evac cu cc yc yc_hi yc_low v_tr v_ev scores biased negmax exps rden scaled p_tr p_ev pv "
                      "bias_loaded tab_in tab_mm tab_sum tab_out y_f y_hi y_low")

    def load_params(act, u):
        wait(act, M.biased, 8 * u)
        for hh in range(2):
            src = bass.AP(tensor=t["dist_table"].tensor, offset=DIST * 2 * u + (DIST * hh + 1), ap=[[1, P], [1, SEQ]])
            act.dma_start(bias[:, hh], src).then_inc(M.bias_loaded, 16)

    def sp(sp):
        for j in range(5):
            k.load_unit(sp, st, 0, j)
        sp.wait_ge(S.h_ready, h1)
        sp.dma_start(buckets[0:32, 0:8], t["rel_bias_2"]).then_inc(M.tab_in, 16)
        sp.dma_start(buckets[0:32, 8:8 + DIST], t["dist_onehot"]).then_inc(M.tab_in, 16)
        sp.dma_start(dist_add[0:8, :], t["dist_add"]).then_inc(M.tab_in, 16)
        k.load_unit(sp, st, 0, 5)
        with sp.Fori(1, N) as u:
            for j in range(PER):
                k.load_unit(sp, st, u, j)

    def evac(act, u, j):
        act.wait_ge(S.mm_done, st.done(u, j))
        src = bank[st.bank[j]][:]
        if j == 0:
            wait(act, M.yc, u)
            act.activation(gb[:], src, ACT.Copy).then_inc(M.evac, 1)
        elif j in (1, 2):
            wait(act, M.cu, u)
            act.activation((gc, xa)[j - 1][:], src, ACT.Copy).then_inc(M.evac, 1)
        elif j in (3, 4):
            wait(act, M.scores, 8 * u)
            act.activation(qk[:, j - 3], src, ACT.Copy, scale=0.125 if j == 3 else 1.0).then_inc(M.evac, 1)
        else:
            wait(act, M.v_tr, u)
            act.activation(vT[:], src, ACT.Copy).then_inc(M.evac, 1)

    def act_probs(act, p, s):
        w = score_tile(s % 4)
        act.wait_ge(M.negmax, 8 * p + (s + 1))
        act.activation(prob[:, s % 4, 0:w], prob[:, s % 4, 0:w], ACT.Exp, bias=mx[:, s:s + 1],
                       accum_out=den[:, s:s + 1]).then_inc(M.exps, 1)

    def act_probT(act, p, s):
        w = score_tile(s % 4)
        act.wait_ge(M.p_tr, 8 * p + (s + 1))
        wait(act, M.pv, 8 * p + (s - 1))
        act.activation(probT[:, s % 2, 0:w], bank[6][:, 0:w], ACT.Copy).then_inc(M.p_ev, 1)

    def act(act):
        def body(p, units, prev):
            u = p + 1

            def slot(j):
                if units:
                    k.split_hi(act, st, u, j)
            slot(0)
            if prev:
                evac(act, p, 4)
            slot(1)
            if prev:
                evac(act, p, 5)
            slot(2)
            if prev:
                act.wait_ge(M.yc, p + 1)
                act.activation(k.tile_of(k.aH, p), yc[:], ACT.Copy).then_inc(M.yc_hi, 1)
                act_probs(act, p, 0)
                act_probs(act, p, 1)
            if units:
                evac(act, u, 0)
            slot(3)
            if prev:
                act.wait_ge(M.v_tr, p + 1)
                act.activation(v_tok[:], bank[7][:].rearrange("p (a n) -> p a n", a=4), ACT.Copy).then_inc(M.v_ev, 1)
                act_probs(act, p, 2)
                act_probT(act, p, 0)
                act_probs(act, p, 3)
                act_probT(act, p, 1)
            if units:
                evac(act, u, 1)
            slot(4)
            if prev:
                act_probs(act, p, 4)
                act_probT(act, p, 2)
                act_probs(act, p, 5)
                act_probT(act, p, 3)
            if units:
                evac(act, u, 2)
            slot(5)
            if prev:
                act_probs(act, p, 6)
                act_probT(act, p, 4)
                act_probs(act, p, 7)
                act_probT(act, p, 5)
                act_probT(act, p, 6)
                act_probT(act, p, 7)
                act.wait_ge(M.y_f, p + 1)
                act.activation(k.tile_of(k.aH, p + 4), y[:], ACT.Copy).then_inc(M.y_hi, 1)
            if units:
                evac(act, u, 3)
                if prev:
                    load_params(act, u)
        body(-1, True, False)
        act.wait_ge(M.tab_sum, 2)
        act.dma_start(t["dist_table"], table[0:8, :]).then_inc(M.tab_out, 16)
        act.wait_ge(M.tab_out, 16)
        load_params(act, 0)
        body(0, True, True)
        with act.Fori(1, N - 1) as p:
            body(p, True, True)
        body(N - 1, False, True)

    def dve_scores(dve, p, s):
        hh, i = s // 4, s % 4
        w = score_tile(i)
        dve.wait_ge(M.scores, 8 * p + (s + 1))
        wait(dve, M.p_tr, 8 * p + (s - 3))
        if s == 0:
            dve.wait_ge(M.bias_loaded, 32 * p + 32)
        own_wait(dve, k.held_dve)
        dve.tensor_tensor_reduce(out=prob[:, i, 0:w], in0=bank[4 + s % 2][:, 0:w], in1=bias[:, hh, 0:w][:, ::-1],
                                 scale=1.0, scalar=-3.0e38, op0=ALU.add, op1=ALU.max,
                                 accum_out=mx[:, s:s + 1]).then_inc(M.biased, 1)
        dve.wait_ge(M.biased, 8 * p + (s + 1))
        dve.tensor_scalar(mx[:, s:s + 1], mx[:, s:s + 1], -1.0, None, ALU.mult).then_inc(M.negmax, 1)

    def dve_scale(dve, p, s):
        w = score_tile(s % 4)
        dve.wait_ge(M.exps, 8 * p + (s + 1))
        dve.reciprocal(den[:, s:s + 1], den[:, s:s + 1]).then_inc(M.rden, 1)
        dve.wait_ge(M.rden, 8 * p + (s + 1))
        dve.tensor_scalar(prob[:, s % 4, 0:w], prob[:, s % 4, 0:w], den[:, s:s + 1], None, ALU.mult)\
           .then_inc(M.scaled, 1)

    def dve(dve):
        def body(p, units, prev):
            u = p + 1

            def slot(j):
                if units:
                    k.split_lo(dve, st, u, j)
            slot(0)
            if prev:
                dve.wait_ge(M.evac, PER * p + 3)
                dve.tensor_tensor(cu[:], gc[:], xa[:], ALU.mult).then_inc(M.cu, 1)
                dve.wait_ge(M.cu, p + 1)
                dve.tensor_scalar(cc[:], cu[:], k.colr("w_sc_2", 8 + p), None, ALU.mult).then_inc(M.cc, 1)
                for n, shift in enumerate((1, 2)):
                    dve.wait_ge(M.cc, 3 * p + (n + 1))
                    dve.scalar_tensor_tensor(cc[:, shift:], cu[:, 0:SEQ - shift], k.colr("w_sc_2", 4 * (2 - shift) + p),
                                             cc[:, shift:], ALU.mult, ALU.add).then_inc(M.cc, 1)
                dve.wait_ge(M.cc, 3 * p + 3)
                wait(dve, M.yc_low, p)
                dve.tensor_tensor(yc[:], cc[:], gb[:], ALU.mult).then_inc(M.yc, 1)
            slot(1)
            slot(2)
            if prev:
                dve_scores(dve, p, 0)
                dve_scores(dve, p, 1)
                dve.wait_ge(M.yc_hi, p + 1)
                dve.tensor_tensor(k.tile_of(k.aL, p), yc[:], k.tile_of(k.aH, p).bitcast(F32), ALU.subtract)\
                   .then_inc(M.yc_low, 1)
                dve_scale(dve, p, 0)
                dve_scale(dve, p, 1)
            slot(3)
            if prev:
                for s in (2, 3):
                    dve_scores(dve, p, s)
                    dve_scale(dve, p, s)
            slot(4)
            if prev:
                for s in (4, 5):
                    dve_scores(dve, p, s)
                    dve_scale(dve, p, s)
            slot(5)
            if prev:
                for s in (6, 7):
                    dve_scores(dve, p, s)
                    dve_scale(dve, p, s)
                dve.wait_ge(M.pv, 8 * p + 8)
                wait(dve, M.y_low, p)
                dve.tensor_copy(y[:], bank[7][:]).then_inc(M.y_f, 1)
                dve.wait_ge(M.y_hi, p + 1)
                dve.tensor_tensor(k.tile_of(k.aL, p + 4), y[:], k.tile_of(k.aH, p + 4).bitcast(F32), ALU.subtract)\
                   .then_inc(M.y_low, 1)
        body(-1, True, False)
        dve.wait_ge(M.tab_in, 48)
        for n, (a, b) in enumerate(((0, HALF_W), (HALF_W, DIST))):
            dve.wait_ge(M.tab_mm, n + 1)
            dve.tensor_tensor(table[0:8, a:b], bank[6 + n][0:8, 0:b - a], dist_add[0:8, a:b], ALU.add)\
               .then_inc(M.tab_sum, 1)
        body(0, True, True)
        with dve.Fori(1, N - 1) as p:
            body(p, True, True)
        body(N - 1, False, True)

    def pe_scores(pe, p, s):
        hh, i = s // 4, s % 4
        if s == 0:
            pe.wait_ge(M.evac, PER * p + 5)
        wait(pe, M.biased, 8 * p + (s - 1))
        pe.matmul(bank[4 + s % 2][:, 0:score_tile(i)], qk[64 * hh:64 * hh + 64, 0, P * i:P * i + P],
                  qk[64 * hh:64 * hh + 64, 1, 0:score_tile(i)], start=True, stop=True).then_inc(M.scores, 1)

    def pe_probT(pe, p, s):
        pe.wait_ge(M.scaled, 8 * p + (s + 1))
        if s == 0:
            wait(pe, M.p_ev, 8 * p)
        else:
            pe.wait_ge(M.p_ev, 8 * p + s)
        for n in range(s % 4 + 1):
            last = pe.transpose(bank[6][:, P * n:P * n + P], prob[:, s % 4, P * n:P * n + P], k.ident[:])
        last.then_inc(M.p_tr, 1)

    def pe_pv(pe, p, s):
        hh, i = s // 4, s % 4
        pe.wait_ge(M.p_ev, 8 * p + (s + 1))
        if s == 0:
            pe.wait_ge(M.v_ev, p + 1)
        for n in range(i + 1):
            last = pe.matmul(bank[7][64 * hh:64 * hh + 64, P * i:P * i + P], v_tok[:, n, 64 * hh:64 * hh + 64],
                             probT[:, s % 2, P * n:P * n + P], start=n == 0, stop=n == i)
        last.then_inc(M.pv, 1)

    def pe(pe, h0):
        def body(p, units, prev):
            u = p + 1

            def unit(j):
                if not units:
                    return
                back = next(b for b in range(1, PER + 1) if st.bank[(j - b) % PER] == st.bank[j])
                wait(pe, M.evac, PER * u + (j - back + 1))
                ready = (lambda kk: pe.wait_ge(S.h_ready, h0 - 8 + kk + 1)) if isinstance(u, int) and u == 0 and j == 0 \
                    else None
                k.unit_product(pe, st, u, j, bank[st.bank[j]][:], (k.hH, k.hL), 0, True, True, ready)
            unit(0)
            if prev:
                pe_scores(pe, p, 0)
                pe_scores(pe, p, 1)
                pe.wait_ge(M.evac, PER * p + 6)
                wait(pe, M.y_f, p)
                for n in range(4):
                    last = pe.transpose(bank[7][:, P * n:P * n + P], vT[:, P * n:P * n + P], k.ident[:])
                last.then_inc(M.v_tr, 1)
            unit(1)
            if prev:
                pe_probT(pe, p, 0)
                pe_scores(pe, p, 2)
            unit(2)
            if prev:
                pe_pv(pe, p, 0)
                pe_probT(pe, p, 1)
                pe_scores(pe, p, 3)
                pe_scores(pe, p, 4)
                pe_pv(pe, p, 1)
                pe_probT(pe, p, 2)
            unit(3)
            if prev:
                pe_scores(pe, p, 5)
                pe_pv(pe, p, 2)
                pe_probT(pe, p, 3)
                pe_scores(pe, p, 6)
            unit(4)
            if prev:
                pe_pv(pe, p, 3)
                pe_probT(pe, p, 4)
                pe_scores(pe, p, 7)
                pe_pv(pe, p, 4)
                pe_probT(pe, p, 5)
            unit(5)
            if prev:
                pe_pv(pe, p, 5)
                pe_probT(pe, p, 6)
                pe_pv(pe, p, 6)
                pe_probT(pe, p, 7)
                pe_pv(pe, p, 7)
        body(-1, True, False)
        pe.wait_ge(M.tab_in, 48)
        pe.matmul(bank[6][0:8, 0:HALF_W], buckets[0:32, 0:8], buckets[0:32, 8:8 + HALF_W], start=True, stop=True)\
          .then_inc(M.tab_mm, 1)
        pe.matmul(bank[7][0:8, 0:DIST - HALF_W], buckets[0:32, 0:8], buckets[0:32, 8 + HALF_W:8 + DIST], start=True,
                  stop=True).then_inc(M.tab_mm, 1)
        pe.wait_ge(M.tab_sum, 2)
        body(0, True, True)
        with pe.Fori(1, N - 1) as p:
            body(p, True, True)
        body(N - 1, False, True)

    def pool(pool):
        pass

    def y_ready(pe):
        return lambda f: pe.wait_ge(M.yc_low, f + 1) if f < 4 else pe.wait_ge(M.y_low, f - 3)

    return Names(sp=sp, act=act, dve=dve, pe=pe, pool=pool, y_ready=y_ready)


def stick_mixer(k, st, t, h1):
    bank, S, scratch = k.bank, k.S, k.scratch
    N, PER = st.bodies, st.per
    TAPS = 31
    k.free("m3")
    a_half = scratch("m3", "a_half", [SEQ])
    tg = scratch("m3", "tg", [SEQ])
    gp = scratch("m3", "gp", [TAPS - 1 + SEQ])
    acc = scratch("m3", "acc", [SEQ])
    cv = scratch("m3", "cv", [4, SEQ])
    qk = scratch("m3", "qk", [2, SEQ])
    vT = scratch("m3", "vT", [SEQ])
    rest = scratch("m3", "rest", [2, SEQ])
    beta = scratch("m3", "beta", [2, SEQ])
    later = scratch("m3", "later", [2, SEQ + 2])
    aw = scratch("m3", "aw", [4, SEQ])
    awT = scratch("m3", "awT", [2, SEQ])
    v_tok = scratch("m3", "v_tok", [4, P])
    zeros = scratch("m3", "zeros", [SEQ])
    before = scratch("m3", "before", [P])
    y = scratch("m3", "y", [SEQ])
    ln_sq = scratch("m3", "ln_sq", [2, SEQ])
    ln_sum = scratch("m3", "ln_sum", [SEQ])
    M = k.sems("m3_", "evac zeroed g cv v_tr v_ev scores masked sig scan aw_done a_tr a_ev pv mask_loaded y_f y_hi "
                      "y_low ln ln_mm ln_sq ln_rs silu yc_hi yc_low")

    def sp(sp):
        for j in range(PER):
            k.load_unit(sp, st, 0, j)
        sp.wait_ge(S.h_ready, h1)
        sp.dma_start(before[:], t["before"]).then_inc(M.mask_loaded, 16)
        with sp.Fori(1, N) as u:
            for j in range(PER):
                k.load_unit(sp, st, u, j)

    def evac(act, u, j):
        act.wait_ge(S.mm_done, st.done(u, j))
        src = bank[st.bank[j]][:]
        if j == 0:
            wait(act, M.g, u)
            act.activation(a_half[:], src, ACT.Copy, scale=0.5).then_inc(M.evac, 1)
        elif j == 1:
            wait(act, M.g, u)
            act.activation(tg[:], src, ACT.Tanh, scale=0.5).then_inc(M.evac, 1)
        elif j in (2, 3):
            wait(act, M.scores, 8 * u)
            act.activation(qk[:, j - 2], src, ACT.Copy).then_inc(M.evac, 1)
        else:
            wait(act, M.v_tr, u)
            act.activation(vT[:], src, ACT.Copy).then_inc(M.evac, 1)

    def act_sig(act, p, s):
        w = score_tile(s % 4)
        act.wait_ge(M.masked, 8 * p + (s + 1))
        wait(act, M.scan, 8 * p + (s - 1))
        act.activation(rest[:, s % 2, 0:w], bank[4 + s % 2][:, 0:w], ACT.Sigmoid, scale=-0.125).then_inc(M.sig, 1)
        wait(act, M.aw_done, 8 * p + (s - 1))
        act.activation(beta[:, s % 2, 0:w], bank[4 + s % 2][:, 0:w], ACT.Sigmoid, scale=0.125).then_inc(M.sig, 1)

    def act_awT(act, p, s):
        w = score_tile(s % 4)
        act.wait_ge(M.a_tr, 8 * p + (s + 1))
        wait(act, M.pv, 8 * p + (s - 1))
        act.activation(awT[:, s % 2, 0:w], bank[6][:, 0:w], ACT.Copy).then_inc(M.a_ev, 1)

    def act(act):
        def body(p, units, prev):
            u = p + 1

            def slot(j):
                if units:
                    k.split_hi(act, st, u, j)
            slot(0)
            if prev:
                evac(act, p, 3)
            slot(1)
            if prev:
                evac(act, p, 4)
                act_sig(act, p, 0)
                act_sig(act, p, 1)
            slot(2)
            if units:
                evac(act, u, 0)
            if prev:
                act.wait_ge(M.v_tr, p + 1)
                act.activation(v_tok[:], bank[7][:].rearrange("p (a n) -> p a n", a=4), ACT.Copy).then_inc(M.v_ev, 1)
                act_sig(act, p, 2)
                act_awT(act, p, 0)
            slot(3)
            if units:
                evac(act, u, 1)
            if prev:
                act_sig(act, p, 3)
                act_awT(act, p, 1)
                act_sig(act, p, 4)
                act_awT(act, p, 2)
            slot(4)
            if prev:
                for s in (5, 6, 7):
                    act_sig(act, p, s)
                    act_awT(act, p, s - 2)
                act_awT(act, p, 6)
                act_awT(act, p, 7)
                act.wait_ge(M.y_f, p + 1)
                act.activation(k.tile_of(k.aH, p + 4), y[:], ACT.Copy).then_inc(M.y_hi, 1)
            if units:
                evac(act, u, 2)
        body(-1, True, False)
        body(0, True, True)
        with act.Fori(1, N - 1) as p:
            body(p, True, True)
        body(N - 1, False, True)
        for n in range(4):
            act.wait_ge(M.ln, 4 + n)
            wait(act, M.ln, 8 + n - 2 if n >= 2 else 0)
            act.activation(ln_sq[:, n % 2], cv[:, n], ACT.Square).then_inc(M.ln_sq, 1)
        act.wait_ge(M.ln_mm, 2)
        act.activation(ln_sum[:], bank[5][:], ACT.Ln, bias=k.eps_col[:]).then_inc(M.ln_rs, 1)
        act.wait_ge(M.ln_rs, 1)
        act.activation(ln_sum[:], ln_sum[:], ACT.Exp, scale=-0.5).then_inc(M.ln_rs, 1)
        for n in range(4):
            act.wait_ge(M.ln, 12 + n)
            act.activation(cv[:, n], cv[:, n], ACT.Silu, bias=k.col("ln_cc_b_2", n)).then_inc(M.silu, 1)
        for n in range(4):
            act.wait_ge(M.silu, n + 1)
            act.activation(k.aH[:, n], cv[:, n], ACT.Copy).then_inc(M.yc_hi, 1)

    def dve_mask(dve, p, s):
        w = score_tile(s % 4)
        dve.wait_ge(M.scores, 8 * p + (s + 1))
        diag = bank[4 + s % 2][:, w - P:w]
        dve.tensor_tensor(diag, diag, before[:], ALU.add).then_inc(M.masked, 1)

    def dve_scan(dve, p, s):
        w = score_tile(s % 4)
        dve.wait_ge(M.sig, 16 * p + (2 * s + 1))
        wait(dve, M.aw_done, 8 * p + (s - 1))
        out = later[:, s % 2, SEQ - w:SEQ]
        dve.tensor_tensor_scan(out=out[:, ::-1], data0=rest[:, s % 2, 0:w][:, ::-1], data1=zeros[:, 0:w], initial=1.0,
                               op0=ALU.mult, op1=ALU.add).then_inc(M.scan, 1)

    def dve_taps(dve, p, lo, hi):
        for n in range(lo, hi):
            w = k.colr("w_cc_2", 4 * n + p)
            if n == 0:
                wait(dve, M.g, p + 1)
                dve.tensor_scalar(acc[:], gp[:, 0:SEQ], w, k.colr("b_cc_2", p), ALU.mult, ALU.add).then_inc(M.cv, 1)
                continue
            dve.wait_ge(M.cv, TAPS * p + n)
            dst = acc[:] if n < TAPS - 1 else k.tile_of(cv, p)
            dve.scalar_tensor_tensor(dst, gp[:, n:n + SEQ], w, acc[:], ALU.mult, ALU.add).then_inc(M.cv, 1)

    def dve(dve):
        def body(p, units, prev):
            u = p + 1

            def slot(j):
                if units:
                    k.split_lo(dve, st, u, j)
            slot(0)
            if prev:
                dve.wait_ge(M.evac, PER * p + 2)
                dve.scalar_tensor_tensor(gp[:, TAPS - 1:TAPS - 1 + SEQ], tg[:], 1.0, a_half[:], ALU.add, ALU.mult)\
                   .then_inc(M.g, 1)
                dve_taps(dve, p, 0, 7)
            slot(1)
            if prev:
                dve_mask(dve, p, 0)
                dve_mask(dve, p, 1)
                dve_taps(dve, p, 7, 12)
                dve_scan(dve, p, 0)
                dve_scan(dve, p, 1)
            slot(2)
            if prev:
                dve_mask(dve, p, 2)
                dve_taps(dve, p, 12, 17)
                dve_scan(dve, p, 2)
            slot(3)
            if prev:
                dve_mask(dve, p, 3)
                dve_taps(dve, p, 17, 20)
                dve_scan(dve, p, 3)
                dve_mask(dve, p, 4)
                dve_taps(dve, p, 20, 23)
                dve_scan(dve, p, 4)
            slot(4)
            if prev:
                for s, lo, hi in ((5, 23, 26), (6, 26, 29), (7, 29, 31)):
                    dve_mask(dve, p, s)
                    dve_taps(dve, p, lo, hi)
                    dve_scan(dve, p, s)
                dve.wait_ge(M.pv, 8 * p + 8)
                wait(dve, M.y_low, p)
                dve.tensor_copy(y[:], bank[7][:]).then_inc(M.y_f, 1)
                dve.wait_ge(M.y_hi, p + 1)
                dve.tensor_tensor(k.tile_of(k.aL, p + 4), y[:], k.tile_of(k.aH, p + 4).bitcast(F32), ALU.subtract)\
                   .then_inc(M.y_low, 1)
        dve.memset(gp[:, 0:TAPS - 1], 0.0).then_inc(M.zeroed, 1)
        dve.memset(zeros[:], 0.0).then_inc(M.zeroed, 1)
        dve.memset(later[:, :, SEQ:SEQ + 1], 1.0).then_inc(M.zeroed, 1)
        dve.wait_ge(M.zeroed, 3)
        dve.wait_ge(M.mask_loaded, 16)
        body(-1, True, False)
        body(0, True, True)
        with dve.Fori(1, N - 1) as p:
            body(p, True, True)
        body(N - 1, False, True)
        dve.wait_ge(M.cv, TAPS * 4)
        dve.tensor_tensor(acc[:], cv[:, 0], cv[:, 1], ALU.add).then_inc(M.ln, 1)
        for n in (2, 3):
            dve.wait_ge(M.ln, n - 1)
            dve.tensor_tensor(acc[:], acc[:], cv[:, n], ALU.add).then_inc(M.ln, 1)
        dve.wait_ge(M.ln_mm, 1)
        for n in range(4):
            dve.tensor_tensor(cv[:, n], cv[:, n], bank[4][:], ALU.subtract).then_inc(M.ln, 1)
        for n in range(4):
            dve.wait_ge(M.ln_sq, n + 1)
            if n == 0:
                dve.tensor_copy(acc[:], ln_sq[:, 0]).then_inc(M.ln, 1)
            else:
                dve.wait_ge(M.ln, 7 + n)
                dve.tensor_tensor(acc[:], acc[:], ln_sq[:, n % 2], ALU.add).then_inc(M.ln, 1)
        dve.wait_ge(M.ln_rs, 2)
        for n in range(4):
            dve.scalar_tensor_tensor(cv[:, n], cv[:, n], k.col("ln_cc_g_2", n), ln_sum[:], ALU.mult, ALU.mult)\
               .then_inc(M.ln, 1)
        for n in range(4):
            dve.wait_ge(M.yc_hi, n + 1)
            dve.tensor_tensor(k.aL[:, n], cv[:, n], k.aH[:, n].bitcast(F32), ALU.subtract).then_inc(M.yc_low, 1)

    def pe_scores(pe, p, s):
        hh, i = s // 4, s % 4
        if s == 0:
            pe.wait_ge(M.evac, PER * p + 4)
        wait(pe, M.sig, 16 * p + 2 * (s - 1))
        pe.matmul(bank[4 + s % 2][:, 0:score_tile(i)], qk[64 * hh:64 * hh + 64, 0, P * i:P * i + P],
                  qk[64 * hh:64 * hh + 64, 1, 0:score_tile(i)], start=True, stop=True).then_inc(M.scores, 1)

    def pe_awT(pe, p, s):
        pe.wait_ge(M.aw_done, 8 * p + (s + 1))
        wait(pe, M.a_ev, 8 * p + s)
        for n in range(s % 4 + 1):
            last = pe.transpose(bank[6][:, P * n:P * n + P], aw[:, s % 4, P * n:P * n + P], k.ident[:])
        last.then_inc(M.a_tr, 1)

    def pe_pv(pe, p, s):
        hh, i = s // 4, s % 4
        pe.wait_ge(M.a_ev, 8 * p + (s + 1))
        if s == 0:
            pe.wait_ge(M.v_ev, p + 1)
        for n in range(i + 1):
            last = pe.matmul(bank[7][64 * hh:64 * hh + 64, P * i:P * i + P], v_tok[:, n, 64 * hh:64 * hh + 64],
                             awT[:, s % 2, P * n:P * n + P], start=n == 0, stop=n == i)
        last.then_inc(M.pv, 1)

    def pe(pe, h0):
        def body(p, units, prev):
            u = p + 1

            def unit(j):
                if not units:
                    return
                back = next(b for b in range(1, PER + 1) if st.bank[(j - b) % PER] == st.bank[j])
                wait(pe, M.evac, PER * u + (j - back + 1))
                ready = (lambda kk: pe.wait_ge(S.h_ready, h0 - 8 + kk + 1)) if isinstance(u, int) and u == 0 and j == 0 \
                    else None
                k.unit_product(pe, st, u, j, bank[st.bank[j]][:], (k.hH, k.hL), 0, True, True, ready)
            unit(0)
            if prev:
                pe_scores(pe, p, 0)
                pe_scores(pe, p, 1)
                pe.wait_ge(M.evac, PER * p + 5)
                wait(pe, M.y_f, p)
                for n in range(4):
                    last = pe.transpose(bank[7][:, P * n:P * n + P], vT[:, P * n:P * n + P], k.ident[:])
                last.then_inc(M.v_tr, 1)
            unit(1)
            if prev:
                pe_scores(pe, p, 2)
                pe_awT(pe, p, 0)
            unit(2)
            if prev:
                pe_pv(pe, p, 0)
                pe_scores(pe, p, 3)
                pe_awT(pe, p, 1)
                pe_scores(pe, p, 4)
                pe_pv(pe, p, 1)
                pe_awT(pe, p, 2)
            unit(3)
            if prev:
                pe_pv(pe, p, 2)
                pe_scores(pe, p, 5)
                pe_awT(pe, p, 3)
                pe_pv(pe, p, 3)
            unit(4)
            if prev:
                for s in (6, 7):
                    pe_scores(pe, p, s)
                    pe_awT(pe, p, s - 2)
                    pe_pv(pe, p, s - 2)
                for s in (6, 7):
                    pe_awT(pe, p, s)
                    pe_pv(pe, p, s)
        body(-1, True, False)
        body(0, True, True)
        with pe.Fori(1, N - 1) as p:
            body(p, True, True)
        body(N - 1, False, True)
        pe.wait_ge(M.ln, 3)
        pe.matmul(bank[4][:], k.ones_half[:], acc[:], start=True, stop=True).then_inc(M.ln_mm, 1)
        pe.wait_ge(M.ln, 11)
        pe.matmul(bank[5][:], k.ones_half[:], acc[:], start=True, stop=True).then_inc(M.ln_mm, 1)

    def pool(pool):
        def body(p):
            for s in range(8):
                w = score_tile(s % 4)
                pool.wait_ge(M.scan, 8 * p + (s + 1))
                pool.wait_ge(M.sig, 16 * p + (2 * s + 2))
                wait(pool, M.a_tr, 8 * p + (s - 3))
                pool.tensor_tensor(aw[:, s % 4, 0:w], beta[:, s % 2, 0:w], later[:, s % 2, SEQ - w + 1:SEQ + 1], ALU.mult)\
                    .then_inc(M.aw_done, 1)
        body(0)
        with pool.Fori(1, N) as p:
            body(p)

    def y_ready(pe):
        return lambda f: pe.wait_ge(M.yc_low, f + 1) if f < 4 else pe.wait_ge(M.y_low, f - 3)

    return Names(sp=sp, act=act, dve=dve, pe=pe, pool=pool, y_ready=y_ready)


def build(nc, t, last_phase=99):
    Stream.units_before = 0
    Stream.loads_before = [0] * 5
    GU1 = Stream(t["w_ffn1_gu"], FT // 2, 4, 8)
    DN1 = Stream(t["w_ffn1_down"], 4, 4, 11)
    IN1 = Stream(t["w_in"], 8, 7, 8)
    OUT1 = Stream(t["w_out"], 2, 4, 8)
    GU2 = Stream(t["w_ffn2_gu"], FT // 2, 4, 8)
    DN2 = Stream(t["w_ffn2_down"], 4, 4, 11)
    IN2 = Stream(t["w_in_even_2"], 4, 6, 8)
    OUT2 = Stream(t["w_out_even_2"], 2, 4, 8)
    GU3 = Stream(t["w_up_2a"], FT // 2, 4, 8)
    DN3 = Stream(t["w_down_2a"], 4, 4, 11)
    IN3 = Stream(t["w_in_odd_2"], 4, 5, 8)
    OUT3 = Stream(t["w_out_odd_2"], 2, 4, 8)
    GU4 = Stream(t["w_up_2b"], FT // 2, 4, 8)
    DN4 = Stream(t["w_down_2b"], 4, 4, 11)

    with ExitStack() as ctx:
        def at(name, shape, word, dt=F32):
            n = 1
            for s in shape:
                n *= s
            assert word + n <= TOP, (name, word, n, TOP)
            return nc.alloc_sbuf_tensor_at(name, [P] + list(shape), dt, offset=BASE + 4 * word)

        BASE = 4096
        TOP = (229344 - BASE) // 4
        xT = at("xT", [DT, SEQ], 0)
        hH = at("hH", [DT, SEQ], 4096, F32R)
        hL = at("hL", [DT, SEQ], 8192, F32R)
        mixT = at("mixT", [DT, SEQ], 4096)
        raw = at("raw", [5632], 12288)
        wH = at("wH", [4224], 17920, F32R)
        wL = at("wL", [4224], 22144, F32R)
        aH = at("aH", [FT, SEQ], 26368, F32R)
        aL = at("aL", [FT, SEQ], 37632, F32R)
        cols = at("cols", [N_COLS], 48896)
        o = 48896 + -(-N_COLS // 8) * 8
        ident = at("ident", [P], o)
        heads1 = at("heads1", [P], o + 128)
        ones = at("ones", [P], o + 256)
        ones_half = at("ones_half", [P], o + 384)
        lam = at("lam", [16], o + 512)
        sp2 = at("sp2", [16], o + 528)
        lam_t = at("lam_t", [4, 16], o + 544)
        hbg = at("hbg", [32], o + 608)
        qg = at("qg", [1], o + 640)
        eps_col = at("eps_col", [1], o + 648)
        T0 = o + 672
        silu_g = at("silu_g", [2, SEQ], T0)
        prod = at("prod", [2, SEQ], T0 + 1024)
        square = at("square", [2, SEQ], T0 + 2048)
        hf = at("hf", [2, SEQ], T0 + 3072)
        rs = at("rs", [SEQ], T0 + 4096)
        rstd = at("rstd", [SEQ], T0 + 4608)
        ssq = at("ssq", [SEQ], T0 + 5120)
        assert T0 + 5632 <= TOP, (T0 + 5632, TOP)
        regions = {}

        def free(which):
            regions[which] = [[26368 + 8 * SEQ, 26368 + 22 * SEQ], [37632 + 8 * SEQ, 37632 + 22 * SEQ], [T0, TOP]]

        def scratch(which, name, shape):
            n = 1
            for s in shape:
                n *= s
            n = -(-n // 8) * 8
            for r in regions[which]:
                if r[0] + n <= r[1]:
                    r[0] += n
                    return at(f"{which}_{name}", shape, r[0] - n)
            raise AssertionError((name, regions[which]))

        bank = [ctx.enter_context(nc.psum_tensor(f"bank{b}", [P, 512], F32)) for b in range(8)]

        def sems(prefix, names):
            return Names(**{n: ctx.enter_context(nc.semaphore(prefix + n)) for n in names.split()})

        S = sems("", "x_loaded consts hi_done lo_done mm_done sq_done ssq_done stat_done rs_done rstd_done hf_done hh_done"
                     " h_ready silu_done conv_done prod_done ah_done a_ready proj_ev x_upd post_t small out_done acc_done lam_exp held_dve held_pool")
        raw_loaded = [ctx.enter_context(nc.semaphore(f"raw_loaded{s}")) for s in range(5)]
        block = ctx.enter_context(nc.Block())

        def col(name, n=0):
            return cols[:, COLS[name] + n:COLS[name] + n + 1]

        def colr(name, n):
            return cols[:, bass.ds(COLS[name] + n, 1)] if not isinstance(n, int) else col(name, n)

        def colat(buf, first, n):
            return buf[:, first + n:first + n + 1] if isinstance(n, int) else buf[:, bass.ds(first + n, 1)]

        def tile_of(buf, n):
            return buf[:, n] if isinstance(n, int) else buf[:, bass.ds(n, 1)].rearrange("p a n -> p (a n)")

        def raw_at(st, j):
            return raw[:, st.raw[j] * st.K * P:(st.raw[j] + 1) * st.K * P]

        def split_at(w, st, j):
            return w[:, st.split[j] * st.K * P:(st.split[j] + 1) * st.K * P]

        def load_unit(sp, st, i, j):
            wait(sp, S.lo_done, st.before(st.raw, i, j))
            src = st.dram[st.per * i + j] if isinstance(i, int) else \
                st.dram[bass.ds(st.per * i + j, 1)].rearrange("u p n -> p (u n)")
            sp.dma_start(raw_at(st, j), src).then_inc(raw_loaded[st.raw[j]], 16)

        def split_hi(act, st, i, j):
            wait(act, S.mm_done, st.before(st.split, i, j))
            act.wait_ge(raw_loaded[st.raw[j]], st.loaded(i, j))
            act.activation(split_at(wH, st, j), raw_at(st, j), ACT.Copy).then_inc(S.hi_done, 1)

        def split_lo(dve, st, i, j):
            dve.wait_ge(S.hi_done, st.done(i, j))
            dve.tensor_tensor(split_at(wL, st, j), raw_at(st, j), split_at(wH, st, j).bitcast(F32),
                              ALU.subtract).then_inc(S.lo_done, 1)

        def unit_product(pe, st, i, j, out, rhs, k0, start, stop, ready=None):
            pe.wait_ge(S.lo_done, st.done(i, j))
            xh, xl = rhs
            for k in range(st.K):
                if ready is not None:
                    ready(k0 + k)
                w_h, w_l = (split_at(w, st, j)[:, k * P:(k + 1) * P] for w in (wH, wL))
                pe.matmul(out, w_h, xh[:, k0 + k], start=start and k == 0, stop=False)
                pe.matmul(out, w_h, xl[:, k0 + k], start=False, stop=False)
                last = pe.matmul(out, w_l, xh[:, k0 + k], start=False, stop=stop and k == st.K - 1)
            last.then_inc(S.mm_done, 1)

        class Tally:
            def __init__(self):
                self.norms = self.pres = self.posts = self.ffns = self.convs = self.projs = 0

        def square_tile(act, q, m, src, odd):
            wait(act, S.ssq_done, 9 * q + m)
            act.activation(square[:, odd], src, ACT.Square).then_inc(S.sq_done, 1)

        def clear_sum(dve, q):
            wait(dve, S.stat_done, q)
            dve.memset(ssq[:], 0.0).then_inc(S.ssq_done, 1)

        def add_square(dve, q, m, odd):
            dve.wait_ge(S.sq_done, 8 * q + 1 + m)
            dve.wait_ge(S.ssq_done, 9 * q + 1 + m)
            dve.tensor_tensor(ssq[:], ssq[:], square[:, odd], ALU.add).then_inc(S.ssq_done, 1)

        def norm_act(act, c, pre, st, then_square):
            q = c.norms
            act.wait_ge(S.stat_done, q + 1)
            act.activation(rs[:], bank[4][:], ACT.Ln, bias=eps_col[:]).then_inc(S.rs_done, 1)
            act.wait_ge(S.rs_done, q + 1)
            act.activation(rstd[:], rs[:], ACT.Exp, scale=-0.5).then_inc(S.rstd_done, 1)
            c.norms += 1
            if pre:
                for k in range(DT):
                    wait(act, S.mm_done, st.n0)
                    act.wait_ge(S.hf_done, 8 * c.pres + k + 1)
                    act.activation(hH[:, k], hf[:, k % 2], ACT.Copy).then_inc(S.hh_done, 1)
                c.pres += 1
            else:
                for k in range(DT if then_square else 0):
                    act.wait_ge(S.x_upd, 8 * c.posts + k + 1)
                    square_tile(act, q + 1, k, xT[:, k], k % 2)
                c.posts += 1

        def norm_pe(pe, c):
            pe.wait_ge(S.ssq_done, 9 * c.norms + 9)
            pe.matmul(bank[4][:], ones[:], ssq[:], start=True, stop=True).then_inc(S.stat_done, 1)
            c.norms += 1

        def norm_dve(dve, c, gain, pre, then_square):
            q = c.norms
            c.norms += 1
            if pre:
                b = 8 * c.pres
                for k in range(DT + 1):
                    if k < DT:
                        dve.wait_ge(S.rstd_done, q + 1)
                        wait(dve, S.h_ready, b + k - 1)
                        dve.scalar_tensor_tensor(hf[:, k % 2], xT[:, k], col(*gain(k)), rstd[:], ALU.mult,
                                                 ALU.mult).then_inc(S.hf_done, 1)
                    if k >= 1:
                        dve.wait_ge(S.hh_done, b + k)
                        dve.tensor_tensor(hL[:, k - 1], hf[:, (k - 1) % 2], hH[:, k - 1].bitcast(F32),
                                          ALU.subtract).then_inc(S.h_ready, 1)
                c.pres += 1
            else:
                b = 8 * c.posts
                if then_square:
                    clear_sum(dve, q + 1)
                for k in range(DT + 1):
                    if k < DT:
                        dve.wait_ge(S.rstd_done, q + 1)
                        wait(dve, S.x_upd, b + k - 1)
                        dve.scalar_tensor_tensor(hf[:, k % 2], mixT[:, k], col(*gain(k)), rstd[:], ALU.mult,
                                                 ALU.mult).then_inc(S.post_t, 1)
                        dve.wait_ge(S.post_t, b + k + 1)
                        dve.tensor_tensor(xT[:, k], xT[:, k], hf[:, k % 2], ALU.add).then_inc(S.x_upd, 1)
                    if k >= 1 and then_square:
                        add_square(dve, q + 1, k - 1, (k - 1) % 2)
                c.posts += 1

        def ffn_pe(pe, c, st):
            hb = 8 * c.pres

            def body(i, first):
                for j in range(4):
                    if not first:
                        pe.wait_ge(S.prod_done, FT * c.ffns + 2 * i + (j // 2 - 1))
                    unit_product(pe, st, i, j, bank[j][:], (hH, hL), 0, True, True,
                                 (lambda k: pe.wait_ge(S.h_ready, hb + k + 1)) if first and j == 0 else None)
            c.pres += 1
            body(0, True)
            with pe.Fori(1, st.bodies) as i:
                body(i, False)
            c.ffns += 1

        def ffn_act(act, c, st, conv):
            f0, v0 = FT * c.ffns, FT * c.convs

            def gate(i, b, jg, first=False):
                act.wait_ge(S.mm_done, st.done(i, jg))
                if not first:
                    act.wait_ge(S.prod_done, f0 + 2 * i + b - 1)
                if conv is None:
                    act.activation(silu_g[:, b], bank[jg][:], ACT.Silu).then_inc(S.silu_done, 1)
                else:
                    w, bb = conv
                    act.activation(silu_g[:, b], bank[jg][:], ACT.Identity, scale=colr(w, 2 * FT + 2 * i + b),
                                   bias=colr(bb, 2 * i + b)).then_inc(S.acc_done, 1)
                    act.wait_ge(S.conv_done, 2 * (v0 + 2 * i + b + 1) if isinstance(i, int)
                                else 2 * (v0 + b + 1) + 4 * i)
                    act.activation(silu_g[:, b], silu_g[:, b], ACT.Silu).then_inc(S.silu_done, 1)

            def up(i, b):
                act.wait_ge(S.prod_done, f0 + 2 * i + b + 1)
                act.activation(tile_of(aH, 2 * i + b), prod[:, b], ACT.Copy).then_inc(S.ah_done, 1)

            for j in range(4):
                split_hi(act, st, 0, j)
                if j >= 2:
                    gate(0, 0, 0, True) if j == 2 else up(0, 0)

            def body(i, ip, first=False):
                for j in range(4):
                    split_hi(act, st, i, j)
                    (lambda: gate(ip, 1, 2, first), lambda: up(ip, 1), lambda: gate(i, 0, 0), lambda: up(i, 0))[j]()
            body(1, 0, True)
            with act.Fori(2, st.bodies) as i:
                body(i, i - 1)
            gate(st.bodies - 1, 1, 2)
            up(st.bodies - 1, 1)
            c.ffns += 1
            c.convs += conv is not None

        def ffn_dve(dve, c, st, conv):
            f0, v0 = FT * c.ffns, FT * c.convs

            def taps(i, b, jg):
                if conv is None:
                    return
                w, _ = conv
                acc0 = v0 + b + 1
                dve.wait_ge(S.acc_done, acc0 + 2 * i)
                for n, shift in enumerate((1, 2)):
                    if n:
                        dve.wait_ge(S.conv_done, 2 * (acc0 - 1) + 1 + 4 * i)
                    dve.scalar_tensor_tensor(silu_g[:, b, shift:], bank[jg][:, 0:SEQ - shift],
                                             colr(w, (2 - shift) * FT + 2 * i + b), silu_g[:, b, shift:], ALU.mult,
                                             ALU.add).then_inc(S.conv_done, 1)

            def product(i, b, ju, first=False):
                dve.wait_ge(S.silu_done, f0 + 2 * i + b + 1)
                dve.wait_ge(S.mm_done, st.done(i, ju))
                if not first:
                    dve.wait_ge(S.a_ready, f0 + 2 * i + b - 1)
                dve.tensor_tensor(prod[:, b], silu_g[:, b], bank[ju][:], ALU.mult).then_inc(S.prod_done, 1)

            def low(i, b):
                dve.wait_ge(S.ah_done, f0 + 2 * i + b + 1)
                dve.tensor_tensor(tile_of(aL, 2 * i + b), prod[:, b], tile_of(aH, 2 * i + b).bitcast(F32),
                                  ALU.subtract).then_inc(S.a_ready, 1)

            for j in range(4):
                split_lo(dve, st, 0, j)
                if j == 2:
                    taps(0, 0, 0)
                if j == 3:
                    product(0, 0, 1, True)
            def body(i, ip, first=False):
                split_lo(dve, st, i, 0)
                low(ip, 0)
                taps(ip, 1, 2)
                split_lo(dve, st, i, 1)
                product(ip, 1, 3, first)
                split_lo(dve, st, i, 2)
                low(ip, 1)
                taps(i, 0, 0)
                split_lo(dve, st, i, 3)
                product(i, 0, 1)
            body(1, 0, True)
            with dve.Fori(2, st.bodies) as i:
                body(i, i - 1)
            i = st.bodies - 1
            low(i, 0)
            taps(i, 1, 2)
            product(i, 1, 3)
            low(i, 1)
            c.ffns += 1
            c.convs += conv is not None

        def proj_pe(pe, c, st, a_count):
            upm = 2 if st.K == 11 else 1
            p0 = 8 * c.projs

            def body(i, first):
                for j in range(4):
                    m, part = j // upm, j % upm
                    per = 4 // upm
                    if part == 0 and not (first and m < 2):
                        pe.wait_ge(S.proj_ev, p0 + per * i + m - 1)
                    unit_product(pe, st, i, j, bank[m % 2][:], (aH, aL), part * st.K, part == 0, part == upm - 1,
                                 a_count if first and m == 0 else None)
            body(0, True)
            with pe.Fori(1, st.bodies) as i:
                body(i, False)
            c.projs += 1

        def proj_act(act, c, st, src, meanwhile):
            upm = 2 if st.K == 11 else 1
            per = 4 // upm
            q, p0 = c.norms, 8 * c.projs

            def squares(i, j):
                if j % upm == upm - 1:
                    m = j // upm
                    act.wait_ge(S.proj_ev, p0 + per * i + (m + 1))
                    square_tile(act, q, per * i + m, tile_of(src, per * i + m), m % 2)

            for j in range(4):
                split_hi(act, st, 0, j)
                if j >= 2:
                    squares(0, j - 2)

            def body(i, before):
                for j in range(4):
                    split_hi(act, st, i, j)
                    squares(before if j < 2 else i, (j - 2) % 4)
            body(1, 0)
            if meanwhile is not None:
                meanwhile()
            if st.bodies > 2:
                with act.Fori(2, st.bodies) as i:
                    body(i, i - 1)
            squares(st.bodies - 1, 2)
            squares(st.bodies - 1, 3)
            c.projs += 1

        def proj_dve(dve, c, st, scale, meanwhile):
            upm = 2 if st.K == 11 else 1
            per = 4 // upm
            q = c.norms

            def take(i, j, last=False):
                if j % upm != upm - 1:
                    return
                m = j // upm
                dve.wait_ge(S.mm_done, st.done(i, j))
                src = bank[m % 2][:]
                if scale is None:
                    dve.tensor_copy(tile_of(mixT, per * i + m), src).then_inc(S.proj_ev, 1)
                else:
                    x_m = tile_of(xT, per * i + m)
                    dve.scalar_tensor_tensor(x_m, src, scale, x_m, ALU.mult, ALU.add).then_inc(S.proj_ev, 1)
                if not (isinstance(i, int) and i == 0 and m == 0):
                    add_square(dve, q, per * i + (m - 1), (m + 1) % 2)

            clear_sum(dve, q)
            for j in range(4):
                split_lo(dve, st, 0, j)
                if j >= 2:
                    take(0, j - 2)

            def body(i, before):
                for j in range(4):
                    split_lo(dve, st, i, j)
                    take(before if j < 2 else i, (j - 2) % 4)
            body(1, 0)
            if meanwhile is not None:
                meanwhile()
            if st.bodies > 2:
                with dve.Fori(2, st.bodies) as i:
                    body(i, i - 1)
            take(st.bodies - 1, 2)
            take(st.bodies - 1, 3)
            add_square(dve, q, DT - 1, 1)
            c.projs += 1

        nsp4 = at("nsp4", [16], o + 656)
        k = Names(bank=bank, S=S, free=free, scratch=scratch, sems=sems, load_unit=load_unit, split_hi=split_hi,
                            split_lo=split_lo, unit_product=unit_product, hH=hH, hL=hL, aH=aH, aL=aL, tile_of=tile_of,
                            colat=colat, colr=colr, col=col, hbg=hbg, sp2=sp2, nsp4=nsp4, qg=qg, eps_col=eps_col, ident=ident,
                            heads1=heads1, ones_half=ones_half, held_dve=S.held_dve, held_pool=S.held_pool)
        mixers = (gated_recurrence_mixer(k, IN1, t, 16), conv_attention_mixer(k, IN2, t, 32), stick_mixer(k, IN3, t, 48))

        phases = [
            ("pre", GU1, lambda k: ("norm_ffn1", k)), ("ffn", GU1, None), ("proj", DN1, 0.5),
            ("pre", IN1, lambda k: ("norm_mix", k)), ("mix", 0, IN1), ("proj", OUT1, 1.0),
            ("pre", GU2, lambda k: ("norm_ffn2", k)), ("ffn", GU2, None), ("proj", DN2, 0.5),
            ("pre", IN2, lambda k: ("norm_g_2", k)), ("mix", 1, IN2), ("proj", OUT2, None),
            ("post", None, lambda k: ("norm_g_2", 8 + k)),
            ("pre", GU3, lambda k: ("norm_g_2", 16 + k)), ("ffn", GU3, 0), ("proj", DN3, None),
            ("post", None, lambda k: ("norm_g_2", 24 + k)),
            ("pre", IN3, lambda k: ("norm_g_2", 32 + k)), ("mix", 2, IN3), ("proj", OUT3, None),
            ("post", None, lambda k: ("norm_g_2", 40 + k)),
            ("pre", GU4, lambda k: ("norm_g_2", 48 + k)), ("ffn", GU4, 1), ("proj", DN4, None),
            ("post", None, lambda k: ("norm_g_2", 56 + k)),
        ][:last_phase]

        def conv_cols(layer):
            return None if layer is None else (f"w_ffn_conv_2@{layer}", f"b_ffn_conv_2@{layer}")

        for layer in range(2):
            COLS[f"w_ffn_conv_2@{layer}"] = COLS["w_ffn_conv_2"] + 66 * layer
            COLS[f"b_ffn_conv_2@{layer}"] = COLS["b_ffn_conv_2"] + 22 * layer

        @block.sync
        def _(sp):
            sp.dma_start(xT[:], t["xT"]).then_inc(S.x_loaded, 16)
            sp.dma_start(cols[:], t["cols"]).then_inc(S.consts, 16)
            sp.dma_start(ident[:], t["ident"]).then_inc(S.consts, 16)
            sp.dma_start(heads1[:], t["heads1"]).then_inc(S.consts, 16)
            for kind, *rest in phases:
                if kind == "ffn" or kind == "proj":
                    st = rest[0]
                    for j in range(4):
                        load_unit(sp, st, 0, j)
                    with sp.Fori(1, st.bodies) as i:
                        for j in range(4):
                            load_unit(sp, st, i, j)
                if kind == "mix":
                    mixers[rest[0]].sp(sp)
            n_post = sum(p[0] == "post" for p in phases)
            n_proj = sum(p[0] == "proj" for p in phases)
            wait(sp, S.x_upd, 8 * n_post)
            wait(sp, S.proj_ev, 8 * n_proj)
            sp.wait_ge(S.x_loaded, 16)
            if last_phase < 99:
                n_pre = sum(p[0] == "pre" for p in phases)
                wait(sp, S.h_ready, 8 * n_pre)
            sp.dma_start(t["out"], xT[:]).then_inc(S.out_done, 16)
            sp.wait_ge(S.out_done, 16)

        @block.scalar
        def _(act):
            c = Tally()
            act.wait_ge(S.consts, 48)
            act.wait_ge(S.small, MEMSETS)

            def lambda_exp():
                act.wait_ge(S.small, LAM_ABS)
                act.activation(lam_t[:, 1], lam_t[:, 1], ACT.Exp, scale=-1.0).then_inc(S.lam_exp, 1)
            for n, (kind, *rest) in enumerate(phases):
                if kind == "pre":
                    if n == 0:
                        act.wait_ge(S.x_loaded, 16)
                        for m in range(DT):
                            square_tile(act, 0, m, xT[:, m], m % 2)
                    norm_act(act, c, True, rest[0], False)
                elif kind == "post":
                    norm_act(act, c, False, None, n + 1 < len(phases))
                elif kind == "ffn":
                    ffn_act(act, c, rest[0], conv_cols(rest[1]))
                elif kind == "proj":
                    proj_act(act, c, rest[0], xT if rest[1] else mixT, lambda_exp if n == 2 else None)
                else:
                    mixers[rest[0]].act(act)

        @block.vector
        def _(dve):
            c = Tally()
            steps = [0]

            def then(instruction):
                instruction.then_inc(S.small, 1)
                steps[0] += 1
                dve.wait_ge(S.small, steps[0])

            def small_constants():
                neg, y_, s_, s2 = (lam_t[:, n] for n in range(4))
                lam_, out_, acc_ = cols[:, COLS["lru_lambda"]:COLS["lru_lambda"] + 16], sp2[:], lam[:]
                then(dve.tensor_scalar(qg[:], col("q_norm"), 0.125, None, ALU.mult))
                then(dve.tensor_scalar(hbg[:], cols[:, COLS["lru_b_gates"]:COLS["lru_b_gates"] + 32], 0.5, None, ALU.mult))
                then(dve.tensor_scalar(neg, lam_, -1.0, None, ALU.mult))
                then(dve.tensor_tensor(y_, neg, lam_, ALU.max))
                assert steps[0] == LAM_ABS
                dve.wait_ge(S.lam_exp, 1)
                then(dve.tensor_scalar(s_, y_, 2.0, None, ALU.add))
                then(dve.reciprocal(s_, s_))
                then(dve.tensor_tensor(s_, s_, y_, ALU.mult))
                then(dve.tensor_tensor(s2, s_, s_, ALU.mult))
                then(dve.tensor_scalar(acc_, s2, 1.0 / 17, None, ALU.mult))
                for n in range(15, 1, -2):
                    then(dve.scalar_tensor_tensor(acc_, acc_, 1.0 / n, s2, ALU.add, ALU.mult))
                then(dve.scalar_tensor_tensor(acc_, acc_, 1.0, s_, ALU.add, ALU.mult))
                then(dve.tensor_scalar(acc_, acc_, 4.0, None, ALU.mult))
                then(dve.tensor_scalar(neg, neg, 0.0, 2.0, ALU.max, ALU.mult))
                then(dve.tensor_tensor(out_, neg, acc_, ALU.add))
                then(dve.tensor_scalar(k.nsp4[:], sp2[:], -2.0, None, ALU.mult))
                assert steps[0] == SMALL

            then(dve.memset(ones[:], 1.0 / D))
            then(dve.memset(ones_half[:], 1.0 / HALF_W))
            then(dve.memset(eps_col[:], EPS))
            dve.wait_ge(S.consts, 48)
            assert steps[0] == MEMSETS
            for n, (kind, *rest) in enumerate(phases):
                if kind == "pre":
                    if n == 0:
                        clear_sum(dve, 0)
                        for m in range(DT):
                            add_square(dve, 0, m, m % 2)
                    norm_dve(dve, c, rest[1], True, False)
                elif kind == "post":
                    norm_dve(dve, c, rest[1], False, n + 1 < len(phases))
                elif kind == "ffn":
                    ffn_dve(dve, c, rest[0], conv_cols(rest[1]))
                elif kind == "proj":
                    proj_dve(dve, c, rest[0], rest[1], small_constants if n == 2 else None)
                else:
                    mixers[rest[0]].dve(dve)

        @block.tensor
        def _(pe):
            c = Tally()
            pe.wait_ge(S.consts, 48)
            pe.wait_ge(S.small, MEMSETS)
            for n, (kind, *rest) in enumerate(phases):
                if kind in ("pre", "post"):
                    norm_pe(pe, c)
                    if kind == "pre" and n + 1 < len(phases) and phases[n + 1][0] == "mix":
                        c.pres += 1
                elif kind == "ffn":
                    ffn_pe(pe, c, rest[0])
                elif kind == "proj":
                    if phases[n - 1][0] == "ffn":
                        ready = lambda f: pe.wait_ge(S.a_ready, FT * (c.ffns - 1) + f + 1)
                    else:
                        ready = mixers[phases[n - 1][1]].y_ready(pe)
                    proj_pe(pe, c, rest[0], ready)
                else:
                    mixers[rest[0]].pe(pe, 8 * c.pres)

        @block.gpsimd
        def _(pool):
            for kind, *rest in phases:
                if kind == "mix":
                    mixers[rest[0]].pool(pool)


INPUTS = ("xT", "cols", "ident", "heads1", "win_mask", "gate_w", "rpb", "rel_bias_2", "dist_onehot", "dist_add", "before",
          "w_ffn1_gu", "w_ffn1_down", "w_in", "w_out", "w_ffn2_gu", "w_ffn2_down", "w_in_even_2", "w_out_even_2", "w_up_2a",
          "w_down_2a", "w_in_odd_2", "w_out_odd_2", "w_up_2b", "w_down_2b")


def shape_constants():
    heads1 = np.zeros((P, P), np.float32)
    heads1[:64, :64] = heads1[64:, 64:] = 1.0 / 64
    win = np.full((P, 3, 256), NEG, np.float32)
    for n in (0, 1, 3):
        for c in range(16):
            qc = 16 * n + c
            first = min(max(qc - 8, 0), GRID_W - 16)
            for kc in range(first, first + 16):
                at = (kc - KSTART[n]) * ROWS
                win[c * ROWS:(c + 1) * ROWS, MASK_OF[n], at:at + ROWS] = 0.0
    onehot = np.zeros((32, DIST), np.float32)
    add = np.full((8, DIST), NEG, np.float32)
    for y in range(DIST):
        d = y - 128
        if d < 0:
            continue
        large = 16 + int(np.float32(np.log(np.float32(max(d, 1) / 16))) / np.float32(np.log(128.0)) * 16)
        onehot[d if d < 16 else min(large, 31), y] = 1.0
        count = (d <= 128) + (d % 4 == 0) + (d % 16 == 0)
        if count:
            add[:, y] = np.log(float(count))
    before = np.where(np.arange(P)[None, :] < np.arange(P)[:, None], 0.0, NEG).astype(np.float32)
    return dict(ident=np.eye(P, dtype=np.float32), heads1=heads1, win_mask=win, dist_onehot=onehot, dist_add=add,
                before=before)


def laid_out(x):
    def units(w, K):
        rows, columns = w.shape
        w = w.reshape(rows // (K * P), K, P, columns // P, P)
        return np.ascontiguousarray(w.transpose(3, 0, 2, 1, 4)).reshape(-1, P, K * P)

    def interleaved(w, parts, K=8):
        w = units(w, K)
        return np.ascontiguousarray(w.reshape(parts, -1, P, K * P).swapaxes(0, 1)).reshape(-1, P, K * P)

    def columns(v):
        return np.ascontiguousarray(v).reshape(-1, P).T

    pieces = []
    for name in COLS:
        if "@" in name:
            continue
        v = x[name]
        if name in ("q_norm", "k_norm"):
            v = np.tile(v[0], 2)
        pieces.append(columns(v))
    out = shape_constants()
    out["cols"] = np.ascontiguousarray(np.concatenate(pieces, 1))
    out["xT"] = np.ascontiguousarray(x["x"][0].T.reshape(DT, P, SEQ).swapaxes(0, 1))
    gates = np.zeros((8, P, 4, P), np.float32)
    g = x["lru_w_gates"][0].reshape(4, 8, 2, 64, 64)
    for half in range(2):
        gates[:, 64 * half:64 * half + 64, :, 64 * half:64 * half + 64] = g[:, :, half].transpose(1, 2, 0, 3)
    out["gate_w"] = gates
    rpb = np.zeros((16, RPB_DR, RPB_W), np.float32)
    rpb[:, :, 16:16 + RPB_DC] = x["rel_pos_bias"][0]
    out["rpb"] = np.ascontiguousarray(rpb.reshape(16, -1)[:, ::-1])
    out["rel_bias_2"] = x["rel_bias_2"]
    out["w_ffn1_gu"] = interleaved(x["w_ffn1_gu"][0], 2)
    out["w_ffn1_down"] = units(x["w_ffn1_down"][0], 11)
    out["w_in"] = np.ascontiguousarray(interleaved(x["w_in"][0], 7))
    out["w_out"] = units(x["w_out"][0], 8)
    out["w_ffn2_gu"] = interleaved(x["w_ffn2_gu"][0], 2)
    out["w_ffn2_down"] = units(x["w_ffn2_down"][0], 11)
    out["w_in_even_2"] = interleaved(x["w_in_even_2"][0], 6)
    out["w_out_even_2"] = units(x["w_out_even_2"][0], 8)
    out["w_in_odd_2"] = interleaved(x["w_in_odd_2"][0], 5)
    out["w_out_odd_2"] = units(x["w_out_odd_2"][0], 8)
    for layer, name in enumerate("ab"):
        out[f"w_up_2{name}"] = interleaved(x["w_up_2"][layer], 2)
        out[f"w_down_2{name}"] = units(x["w_down_2"][layer], 11)
    return out


def kernel(**inputs):
    import concourse.bacc as bacc
    from concourse.bass_utils import run_bass_kernel_spmd

    arrays = laid_out({name: np.asarray(a) for name, a in inputs.items()})
    nc = bacc.Bacc("TRN2", target_bir_lowering=False, num_devices=1, dynamic_dma_scratch_size=1024)
    t = {name: nc.dram_tensor(f"in_{name}", arrays[name].shape, F32, kind="ExternalInput").ap() for name in INPUTS}
    t["dist_table"] = nc.dram_tensor("dist_table", (8, DIST), F32).ap()
    t["out"] = nc.dram_tensor("out_x", (P, DT, SEQ), F32, kind="ExternalOutput").ap()
    build(nc, t)
    r = run_bass_kernel_spmd(nc, [{f"in_{name}": arrays[name] for name in INPUTS}], core_ids=[0])
    y = r.results[0]["out_x"]
    return np.ascontiguousarray(y.transpose(2, 1, 0).reshape(1, SEQ, D))
```

```python
from collections import namedtuple
from contextlib import ExitStack

import numpy as np
import concourse.bass as bass
from concourse import mybir

P = 128
SEQ = 512
D = 1024
DT = D // P
FF = 2816
FT = FF // P
EPS = 1e-6
GRID_W, ROWS = 64, 8
RPB_DR, RPB_DC, RPB_W = 15, 31, 64
RUN = 7 * RPB_W + 48
NEG = -1.0e30
LAM_ABS = 7
SMALL = 24
MEMSETS = 3
HALF_W = 512
GELU_C = 0.7978845608028654
KSTART = (0, 8, 24, 32)
MASK_OF = (0, 1, 1, 2)
DIST = 640

F32 = mybir.dt.float32
F32R = mybir.dt.float32r
ALU = mybir.AluOpType
ACT = mybir.ActivationFunctionType

COLS = {}
_at = 0
for _name, _n in (("norm_ffn1", 8), ("norm_mix", 8), ("norm_ffn2", 8), ("conv_w", 32), ("conv_b", 8), ("lru_b_gates", 32),
                  ("lru_lambda", 16), ("q_norm", 1), ("k_norm", 1), ("norm_g_2", 64), ("w_sc_2", 12), ("w_cc_2", 124),
                  ("b_cc_2", 4), ("ln_cc_g_2", 4), ("ln_cc_b_2", 4), ("w_ffn_conv_2", 132), ("b_ffn_conv_2", 44)):
    COLS[_name] = _at
    _at += _n
N_COLS = _at


def Names(**things):
    return namedtuple("Names", list(things))(**things)


def wait(eng, sem, value):
    if not (isinstance(value, int) and value <= 0):
        eng.wait_ge(sem, value)


def own_wait(eng, held):
    eng.sem_inc(held, 1)


class Stream:

    units_before = 0
    loads_before = [0] * 5
    newest = None

    def __init__(self, dram, bodies, per, K, early=False):
        self.dram, self.bodies, self.per, self.K = dram, bodies, per, K
        self.raw = {4: (0, 1, 2, 3), 5: (0, 1, 2, 3, 4), 6: (0, 1, 2, 3, 4, 2), 7: (0, 1, 2, 3, 4, 2, 3)}[per]
        self.split = {(4, 8): (0, 1, 2, 3), (4, 11): (0, 1, 2, 1), (5, 8): (0, 1, 2, 3, 2), (6, 8): (0, 1, 2, 3, 0, 1),
                      (7, 8): (0, 1, 2, 3, 0, 1, 2)}[per, K]
        self.bank = {4: (0, 1, 2, 3), 5: (0, 1, 2, 3, 0), 6: (0, 1, 2, 3, 0, 1), 7: (0, 1, 2, 3, 0, 1, 2)}[per]
        self.n0 = Stream.units_before
        self.last, Stream.newest = Stream.newest, self
        self.early = 4 if early else 2
        self.l0 = list(Stream.loads_before)
        Stream.units_before += bodies * per
        Stream.loads_before = [l + bodies * self.raw.count(s) for s, l in enumerate(self.l0)]

    def done(self, i, j):
        return self.n0 + self.per * i + (j + 1)

    def before(self, kind, i, j):
        ring = self.raw if kind == "raw" else self.split
        back = next(b for b in range(1, self.per + 1) if ring[(j - b) % self.per] == ring[j])
        if isinstance(i, int) and i == 0 and j - back < 0:
            if self.last is None:
                return 0
            old = self.last
            theirs = old.raw if kind == "raw" else old.split
            over = [n for n in range(old.per) if theirs[n] == ring[j] or (
                theirs[n] * old.K < (ring[j] + 1) * self.K and ring[j] * self.K < (theirs[n] + 1) * old.K)]
            return self.n0 - old.per + (over[-1] + 1 if over else 0)
        return self.n0 + self.per * i + (j - back + 1)

    def loaded(self, i, j):
        s = self.raw[j]
        return 16 * (self.l0[s] + self.raw[:j + 1].count(s)) + 16 * self.raw.count(s) * i


def gated_recurrence_mixer(k, st, t, h1):
    bank, S, free, scratch = k.bank, k.S, k.free, k.scratch
    N = st.bodies
    free("m1")
    xr = scratch("m1", "xr", [516])
    gr = scratch("m1", "gr", [SEQ])
    qk = scratch("m1", "qk", [2, SEQ])
    vT = scratch("m1", "vT", [SEQ])
    tha = scratch("m1", "tha", [SEQ])
    thb = scratch("m1", "thb", [SEQ])
    xc = scratch("m1", "xc", [SEQ])
    qkr = scratch("m1", "qkr", [2, SEQ])
    qkn = scratch("m1", "qkn", [2, SEQ])
    g2 = scratch("m1", "g2", [SEQ])
    gate_a = scratch("m1", "gate_a", [SEQ])
    gate_b = scratch("m1", "gate_b", [SEQ])
    y1 = scratch("m1", "y1", [SEQ])
    y = scratch("m1", "y", [SEQ])
    ti = scratch("m1", "ti", [2, SEQ])
    t2 = scratch("m1", "t2", [2, SEQ])
    sq = scratch("m1", "sq", [2, SEQ])
    la = scratch("m1", "la", [2, SEQ])
    sqk = la
    prob = scratch("m1", "prob", [2, SEQ])
    probT = scratch("m1", "probT", [2, SEQ])
    v_tok = scratch("m1", "v_tok", [7, P])
    run = scratch("m1", "run", [2, RUN])
    bias = scratch("m1", "bias", [2, 4, 256])
    mask = scratch("m1", "mask", [3, 256])
    gate_w = scratch("m1", "gate_w", [4, P])
    mx = scratch("m1", "mx", [8])
    den = scratch("m1", "den", [8])
    M = k.sems("m1_", "evac gab_free zeroed sqk g2 g2p gth gelu qk_stat qk_rs qk_rr qkn conv gates gate_act t2_sqrt lru ix "
                      "v_tr v_ev scores biased negmax exps rden scaled p_tr p_ev pv bias_ready run_loaded gw_loaded "
                      "mask_loaded y1 gab yatt_used y_f y_hi y_ready hsum")
    PER = st.per

    def perm(ap):
        return ap.rearrange("p (c r) -> p r c", r=ROWS)

    def rows_of(ap):
        return ap.rearrange("p (r c) -> p r c", c=GRID_W)

    def load_params(sp, u):
        wait(sp, M.gates, 4 * u)
        src = t["gate_w"][u] if isinstance(u, int) else t["gate_w"][bass.ds(u, 1)].rearrange("a p g n -> p (a g) n")
        sp.dma_start(gate_w[:], src).then_inc(M.gw_loaded, 16)
        wait(sp, M.bias_ready, 8 * u)
        tab = t["rpb"]
        for r in range(ROWS):
            src = bass.AP(tensor=tab.tensor, offset=RPB_DR * RPB_W * 2 * u + (r * RPB_W + 1),
                          ap=[[1, 16], [RPB_DR * RPB_W, 2], [1, RUN]])
            sp.dma_start(run[r:P:ROWS], src).then_inc(M.run_loaded, 16)

    def sp(sp):
        for j in range(5):
            k.load_unit(sp, st, 0, j)
        sp.wait_ge(S.h_ready, h1)
        sp.dma_start(mask[:], t["win_mask"]).then_inc(M.mask_loaded, 16)
        load_params(sp, 0)
        for j in range(5, PER):
            k.load_unit(sp, st, 0, j)
        for j in range(PER):
            k.load_unit(sp, st, 1, j)
            if j == 4:
                load_params(sp, 1)
        with sp.Fori(2, N) as u:
            for j in range(PER):
                k.load_unit(sp, st, u, j)
                if j == 4:
                    load_params(sp, u)

    def evac(act, u, j):
        act.wait_ge(S.mm_done, st.done(u, j))
        src = bank[st.bank[j]][:]
        if j == 0:
            wait(act, M.conv, 4 * u)
            act.activation(xr[:, 2:2 + SEQ], src, ACT.Copy).then_inc(M.evac, 1)
        elif j == 1:
            wait(act, M.gelu, 2 * u)
            act.activation(gr[:], src, ACT.Copy).then_inc(M.evac, 1)
        elif j in (2, 3):
            wait(act, M.qkn, 2 * u)
            act.activation(qk[:, j - 2], src, ACT.Copy).then_inc(M.evac, 1)
        elif j == 4:
            wait(act, M.v_tr, 2 * u)
            act.activation(perm(vT[:]), rows_of(src), ACT.Copy).then_inc(M.evac, 1)
        else:
            wait(act, M.gab, 2 * u)
            act.activation((tha, thb)[j - 5][:], src, ACT.Tanh, scale=0.5).then_inc(M.evac, 1)

    def act_probs(act, p, s):
        act.wait_ge(M.negmax, 4 * p + (s + 1))
        for b in range(2):
            e = 2 * s + b
            act.activation(prob[:, s % 2, 256 * b:256 * b + 256], prob[:, s % 2, 256 * b:256 * b + 256], ACT.Exp,
                           bias=mx[:, e:e + 1], accum_out=den[:, e:e + 1]).then_inc(M.exps, 1)

    def act_probT(act, p, s):
        act.wait_ge(M.p_tr, 4 * p + (s + 1))
        wait(act, M.pv, 4 * p + (s - 1))
        act.activation(probT[:, s % 2], bank[6][:], ACT.Copy).then_inc(M.p_ev, 1)

    def act_gates(act, p, d):
        for g, dst in ((0, t2), (1, ti)):
            act.wait_ge(M.gates, 4 * p + (2 * d + g + 1))
            wait(act, M.lru, 6 * p + (3 * d - 3))
            n = (2 * d + g) * 8
            act.activation(dst[:, d], bank[4 + g][:], ACT.Tanh, scale=0.5, bias=k.colat(k.hbg, n, p))\
               .then_inc(M.gate_act, 1)
        act.wait_ge(M.gate_act, 8 * p + (4 * d + 1))
        act.wait_ge(M.qk_stat, 2 * p + 2)
        sc = k.colat(k.nsp4, 8 * d, p)
        act.activation(la[:, d], t2[:, d], ACT.Exp, scale=sc, bias=sc).then_inc(M.gate_act, 1)
        sc = k.colat(k.sp2, 8 * d, p)
        act.activation(t2[:, d], t2[:, d], ACT.Tanh, scale=sc, bias=sc).then_inc(M.gate_act, 1)

    def act(act, after):
        def body(p, units, prev, tail):
            u = p + 1

            def slot(j):
                if units and not (isinstance(u, int) and u == 0 and j < st.early):
                    k.split_hi(act, st, u, j)
                if not units and j < after.early:
                    k.split_hi(act, after, 0, j)
            slot(0)
            if tail:
                act_probT(act, p - 1, 2)
            if prev:
                evac(act, p, 5)
                for n in range(2):
                    wait(act, M.lru, 6 * p)
                    act.wait_ge(M.evac, PER * p + (3 + n))
                    act.activation(sqk[:, n], qk[:, n], ACT.Square).then_inc(M.sqk, 1)
                wait(act, M.y1, 2 * p)
                act.activation(g2[:], gr[:], ACT.Square).then_inc(M.g2, 1)
            slot(1)
            if tail:
                act_probT(act, p - 1, 3)
            if prev:
                evac(act, p, 6)
                act.wait_ge(M.g2p, 2 * p + 2)
                act.activation(g2[:], g2[:], ACT.Tanh, scale=GELU_C).then_inc(M.gth, 1)
            slot(2)
            if units:
                evac(act, u, 0)
            slot(3)
            if units:
                evac(act, u, 1)
            if tail:
                act.wait_ge(M.y_f, p)
                act.activation(k.tile_of(k.aH, p - 1), y[:], ACT.Copy).then_inc(M.y_hi, 1)
            if prev:
                for n in range(2):
                    act.wait_ge(M.qk_stat, 2 * p + (n + 1))
                    act.activation(qkr[:, n], bank[6 + n][:], ACT.Ln, bias=k.eps_col[:]).then_inc(M.qk_rs, 1)
                for n in range(2):
                    act.wait_ge(M.qk_rs, 4 * p + (n + 1))
                    act.activation(qkr[:, n], qkr[:, n], ACT.Exp, scale=-0.5).then_inc(M.qk_rs, 1)
                act_gates(act, p, 0)
            slot(4)
            if prev:
                act_gates(act, p, 1)
                wait(act, M.hsum, p)
                for d in range(2):
                    act.wait_ge(M.gate_act, 8 * p + (4 * d + 4))
                    act.activation(sq[:, d], t2[:, d], ACT.Sqrt).then_inc(M.t2_sqrt, 1)
                act.wait_ge(M.v_tr, 2 * p + 1)
                act.activation(v_tok[:, 0:4], bank[6][:].rearrange("p (a n) -> p a n", a=4), ACT.Copy)\
                   .then_inc(M.v_ev, 1)
            if units:
                evac(act, u, 2)
            slot(5)
            if units:
                evac(act, u, 3)
            if prev:
                act.wait_ge(M.v_tr, 2 * p + 2)
                act.activation(v_tok[:, 4:7], bank[6][:, 0:384].rearrange("p (a n) -> p a n", a=3), ACT.Copy)\
                   .then_inc(M.v_ev, 1)
                act_probs(act, p, 0)
                act_probs(act, p, 1)
            slot(6)
            if units:
                evac(act, u, 4)
            if prev:
                act_probT(act, p, 0)
                act_probs(act, p, 2)
                act_probs(act, p, 3)
                act_probT(act, p, 1)
        body(-1, True, False, False)
        body(0, True, True, False)
        with act.Fori(1, N - 1) as p:
            body(p, True, True, True)
        body(N - 1, False, True, True)
        act_probT(act, N - 1, 2)
        act_probT(act, N - 1, 3)
        act.wait_ge(M.y_f, N)
        act.activation(k.tile_of(k.aH, N - 1), y[:], ACT.Copy).then_inc(M.y_hi, 1)

    def dve_scores(dve, p, s):
        dve.wait_ge(M.scores, 4 * p + (s + 1))
        wait(dve, M.p_tr, 4 * p + (s - 1))
        if s == 0:
            dve.wait_ge(M.bias_ready, 8 * p + 8)
        hh, pr = s // 2, s % 2
        for b in range(2):
            e = 2 * s + b
            own_wait(dve, k.held_dve)
            dve.tensor_tensor_reduce(out=prob[:, s % 2, 256 * b:256 * b + 256],
                                     in0=bank[4 + s % 2][:, 256 * b:256 * b + 256], in1=bias[:, hh, 2 * pr + b],
                                     scale=1.0, scalar=-3.0e38, op0=ALU.add, op1=ALU.max,
                                     accum_out=mx[:, e:e + 1]).then_inc(M.biased, 1)
        dve.wait_ge(M.biased, 8 * p + (2 * s + 2))
        dve.tensor_scalar(mx[:, 2 * s:2 * s + 2], mx[:, 2 * s:2 * s + 2], -1.0, None, ALU.mult).then_inc(M.negmax, 1)

    def dve_scale(dve, p, s):
        dve.wait_ge(M.exps, 8 * p + (2 * s + 2))
        dve.reciprocal(den[:, 2 * s:2 * s + 2], den[:, 2 * s:2 * s + 2]).then_inc(M.rden, 1)
        dve.wait_ge(M.rden, 4 * p + (s + 1))
        pair = den[:, 2 * s:2 * s + 2]
        by = bass.AP(tensor=pair.tensor, offset=pair.offset, ap=[pair.ap[0], [1, 2], [0, 256]])
        both = prob[:, s % 2].rearrange("p (b n) -> p b n", b=2)
        dve.tensor_tensor(both, both, by, ALU.mult).then_inc(M.scaled, 1)

    def dve_ix(dve, p, d):
        dve.wait_ge(M.gate_act, 8 * p + (4 * d + 2))
        dve.scalar_tensor_tensor(ti[:, d], ti[:, d], 1.0, xc[:], ALU.add, ALU.mult).then_inc(M.ix, 1)

    def dve_lru(dve, p, d):
        dve.wait_ge(M.t2_sqrt, 2 * p + (d + 1))
        dve.wait_ge(M.ix, 2 * p + (d + 1))
        dve.tensor_tensor(ti[:, d], ti[:, d], sq[:, d], ALU.mult).then_inc(M.lru, 1)
        dve.wait_ge(M.lru, 6 * p + (3 * d + 1))
        dve.scalar_tensor_tensor(ti[:, d], la[:, d], 1.0, ti[:, d], ALU.add, ALU.mult).then_inc(M.lru, 1)
        dve.wait_ge(M.lru, 6 * p + (3 * d + 2))
        o_, a_, b_ = (x[:, d] if d == 0 else x[:, d, ::-1] for x in (sq, la, ti))
        dve.tensor_tensor_scan(out=o_, data0=a_, data1=b_, initial=0.0, op0=ALU.mult, op1=ALU.add).then_inc(M.lru, 1)

    def dve_tail(dve, q):
        dve.wait_ge(M.pv, 4 * q + 4)
        dve.wait_ge(M.gab, 2 * q + 2)
        wait(dve, M.y_hi, q)
        wait(dve, M.y_ready, q)
        dve.tensor_tensor(rows_of(y[:]), perm(bank[7][:]), rows_of(gate_b[:]), ALU.mult).then_inc(M.yatt_used, 1)
        dve.wait_ge(M.yatt_used, q + 1)
        dve.wait_ge(M.y1, 2 * q + 2)
        dve.tensor_tensor(y[:], y[:], y1[:], ALU.add).then_inc(M.y_f, 1)

    def dve_low(dve, q):
        dve.wait_ge(M.y_hi, q + 1)
        dve.tensor_tensor(k.tile_of(k.aL, q), y[:], k.tile_of(k.aH, q).bitcast(F32), ALU.subtract)\
           .then_inc(M.y_ready, 1)

    def dve(dve, after):
        def body(p, units, prev, tail):
            u = p + 1

            def slot(j):
                if units and not (isinstance(u, int) and u == 0 and j < st.early):
                    k.split_lo(dve, st, u, j)
                if not units and j < after.early:
                    k.split_lo(dve, after, 0, j)
            slot(0)
            if prev:
                dve.wait_ge(M.evac, PER * p + 1)
                dve.wait_ge(M.zeroed, 2)
                wait(dve, M.gates, 4 * p)
                dve.tensor_scalar(xc[:], xr[:, 0:SEQ], k.colr("conv_w", p), k.colr("conv_b", p), ALU.mult, ALU.add)\
                   .then_inc(M.conv, 1)
                for n in range(1, 4):
                    dve.wait_ge(M.conv, 4 * p + n)
                    dve.scalar_tensor_tensor(xc[:], xr[:, n:n + SEQ], k.colr("conv_w", 8 * n + p), xc[:], ALU.mult,
                                             ALU.add).then_inc(M.conv, 1)
            slot(1)
            slot(2)
            if tail:
                dve_tail(dve, p - 1)
            slot(3)
            if tail:
                dve_low(dve, p - 1)
            if prev:
                for n in range(2):
                    dve.wait_ge(M.qk_rs, 4 * p + (n + 3))
                    src, by = qk[:, n], qkr[:, n]
                    dve.scalar_tensor_tensor(perm(qkn[:, n]), rows_of(src), k.qg[:] if n == 0 else k.col("k_norm"),
                                             rows_of(by), ALU.mult, ALU.mult).then_inc(M.qkn, 1)
                dve_ix(dve, p, 0)
            slot(4)
            if prev:
                dve_ix(dve, p, 1)
            slot(5)
            if prev:
                dve_scores(dve, p, 0)
                dve_scores(dve, p, 1)
                dve_scale(dve, p, 0)
                dve_scale(dve, p, 1)
                dve_lru(dve, p, 0)
            slot(6)
            if prev:
                dve_lru(dve, p, 1)
                dve_scores(dve, p, 2)
                dve_scale(dve, p, 2)
                dve_scores(dve, p, 3)
                dve_scale(dve, p, 3)
        dve.memset(xr[:, 0:2], 0.0).then_inc(M.zeroed, 1)
        dve.memset(xr[:, 2 + SEQ:3 + SEQ], 0.0).then_inc(M.zeroed, 1)
        body(-1, True, False, False)
        body(0, True, True, False)
        with dve.Fori(1, N - 1) as p:
            body(p, True, True, True)
        body(N - 1, False, True, True)
        dve_tail(dve, N - 1)
        dve_low(dve, N - 1)

    def y_ready(pe):
        return lambda f: pe.wait_ge(M.y_ready, f + 1)

    early = (0, 1, 2, 3, 4, 5)

    def pe_scores(pe, p, s):
        hh, pr = s // 2, s % 2
        if s < 2:
            pe.wait_ge(M.qkn, 2 * p + 2)
            pe.wait_ge(M.gate_act, 8 * p + (5 + s))
        else:
            pe.wait_ge(M.biased, 8 * p + 2 * (s - 1))
        for b in range(2):
            n = 2 * pr + b
            last = pe.matmul(bank[4 + s % 2][:, 256 * b:256 * b + 256],
                             qkn[64 * hh:64 * hh + 64, 0, P * n:P * n + P],
                             qkn[64 * hh:64 * hh + 64, 1, KSTART[n] * ROWS:KSTART[n] * ROWS + 256],
                             start=True, stop=True)
        last.then_inc(M.scores, 1)

    def pe_probT(pe, p, s):
        pe.wait_ge(M.scaled, 4 * p + (s + 1))
        if s == 0:
            pe.wait_ge(M.v_ev, 2 * p + 2)
        else:
            pe.wait_ge(M.p_ev, 4 * p + s)
        for n in range(4):
            last = pe.transpose(bank[6][:, P * n:P * n + P], prob[:, s % 2, P * n:P * n + P], k.ident[:])
        last.then_inc(M.p_tr, 1)

    def pe_pv(pe, p, s):
        hh, pr = s // 2, s % 2
        pe.wait_ge(M.p_ev, 4 * p + (s + 1))
        if s == 0:
            wait(pe, M.yatt_used, p)
        for b in range(2):
            n = 2 * pr + b
            off = KSTART[n] * ROWS
            for c in range(2):
                o_ = off + P * c
                vt = o_ // P if o_ % P == 0 else 4 + o_ // P
                last = pe.matmul(bank[7][64 * hh:64 * hh + 64, P * n:P * n + P], v_tok[:, vt, 64 * hh:64 * hh + 64],
                                 probT[:, s % 2, 256 * b + P * c:256 * b + P * c + P], start=c == 0, stop=c == 1)
        last.then_inc(M.pv, 1)

    def pe_gates(pe, p, d):
        for g in range(2):
            if d == 1:
                pe.wait_ge(M.gate_act, 8 * p + (g + 1))
            pe.matmul(bank[4 + g][:], gate_w[:, 2 * d + g], xc[:], start=True, stop=True).then_inc(M.gates, 1)

    def pe(pe, h0, after):
        def body(p, units, prev, tail):
            u = p + 1

            def unit(j):
                if not units:
                    if 1 <= j <= after.early:
                        if j == 1:
                            pe.wait_ge(M.evac, PER * N)
                            for f in early:
                                y_ready(pe)(f)
                        k.proj_start(pe, after, j - 1, early)
                    return
                if isinstance(u, int) and u == 0 and j < 2:
                    if j == 0:
                        k.first_products(pe, st, (bank[0][:], bank[1][:]), h0 - 8)
                    return
                back = next(b for b in range(1, PER + 1) if st.bank[(j - b) % PER] == st.bank[j])
                wait(pe, M.evac, PER * u + (j - back + 1))
                k.unit_product(pe, st, u, j, bank[st.bank[j]][:], (k.hH, k.hL), 0, True, True)
            unit(0)
            if tail:
                pe_pv(pe, p - 1, 2)
                pe_probT(pe, p - 1, 3)
            if prev:
                pe.wait_ge(M.conv, 4 * p + 4)
                pe.wait_ge(M.gw_loaded, 16 * p + 16)
                wait(pe, M.biased, 8 * p)
                pe_gates(pe, p, 0)
            if tail:
                pe_pv(pe, p - 1, 3)
            unit(1)
            if prev:
                for n in range(2):
                    pe.wait_ge(M.sqk, 2 * p + (n + 1))
                    if n == 0:
                        wait(pe, M.p_ev, 4 * p)
                    else:
                        wait(pe, M.yatt_used, p)
                    pe.matmul(bank[6 + n][:], k.heads1[:], sqk[:, n], start=True, stop=True).then_inc(M.qk_stat, 1)
            unit(2)
            if prev:
                pe_gates(pe, p, 1)
                pe.wait_ge(M.evac, PER * p + 5)
                pe.wait_ge(M.qk_rs, 4 * p + 1)
                for n in range(4):
                    last = pe.transpose(bank[6][:, P * n:P * n + P], vT[:, P * n:P * n + P], k.ident[:])
                last.then_inc(M.v_tr, 1)
            unit(3)
            if prev:
                pe_scores(pe, p, 0)
                pe_scores(pe, p, 1)
                pe.wait_ge(M.v_ev, 2 * p + 1)
                for n in range(3):
                    last = pe.transpose(bank[6][:, P * n:P * n + P], vT[:, 64 + P * n:64 + P * n + P], k.ident[:])
                last.then_inc(M.v_tr, 1)
            unit(4)
            if prev:
                pe_probT(pe, p, 0)
                pe_scores(pe, p, 2)
            unit(5)
            if prev:
                pe.wait_ge(M.qk_rs, 4 * p + 2)
                pe_pv(pe, p, 0)
                pe_probT(pe, p, 1)
                pe_scores(pe, p, 3)
            unit(6)
            if prev:
                pe_pv(pe, p, 1)
                pe_probT(pe, p, 2)
        pe.wait_ge(S.consts, 48)
        body(-1, True, False, False)
        body(0, True, True, False)
        with pe.Fori(1, N - 1) as p:
            body(p, True, True, True)
        body(N - 1, False, True, True)
        pe_pv(pe, N - 1, 2)
        pe_probT(pe, N - 1, 3)
        pe_pv(pe, N - 1, 3)

    def pool(pool):
        def body(p):
            pool.wait_ge(M.run_loaded, 16 * ROWS * p + 16 * ROWS)
            wait(pool, M.biased, 8 * p)
            for hh in range(2):
                for n in range(4):
                    first = KSTART[n] - 16 * n + 16
                    src = bass.AP(tensor=run[:].tensor, offset=run[:, hh, RUN - 1 - first:RUN - first].offset,
                                  ap=[run[:].ap[0], [-1, 32], [-RPB_W, 8]])
                    pool.tensor_tensor(bias[:, hh, n].rearrange("p (c r) -> p c r", r=ROWS), src,
                                       mask[:, MASK_OF[n]].rearrange("p (c r) -> p c r", r=ROWS),
                                       ALU.add).then_inc(M.bias_ready, 1)
            pool.wait_ge(M.g2, p + 1)
            own_wait(pool, k.held_pool)
            pool.tensor_scalar(g2[:], g2[:], 0.044715, 1.0, ALU.mult, ALU.add).then_inc(M.g2p, 1)
            pool.wait_ge(M.g2p, 2 * p + 1)
            pool.tensor_tensor(g2[:], g2[:], gr[:], ALU.mult).then_inc(M.g2p, 1)
            pool.wait_ge(M.gth, p + 1)
            own_wait(pool, k.held_pool)
            pool.tensor_scalar(g2[:], g2[:], 1.0, None, ALU.add).then_inc(M.gelu, 1)
            pool.wait_ge(M.gelu, 2 * p + 1)
            wait(pool, M.hsum, p)
            pool.tensor_tensor(g2[:], g2[:], gr[:], ALU.mult).then_inc(M.gelu, 1)
            pool.wait_ge(M.evac, PER * p + 7)
            wait(pool, M.y1, 2 * p)
            own_wait(pool, k.held_pool)
            pool.tensor_scalar(gate_a[:], tha[:], 1.0, 0.125, ALU.add, ALU.mult).then_inc(M.gab, 1)
            wait(pool, M.yatt_used, p)
            own_wait(pool, k.held_pool)
            pool.tensor_scalar(gate_b[:], thb[:], 1.0, 0.5, ALU.add, ALU.mult).then_inc(M.gab, 1)
            pool.wait_ge(M.lru, 6 * p + 6)
            wait(pool, M.y_f, p)
            pool.tensor_tensor(y1[:], sq[:, 0], sq[:, 1], ALU.add).then_inc(M.hsum, 1)
            pool.wait_ge(M.hsum, p + 1)
            pool.wait_ge(M.gelu, 2 * p + 2)
            pool.tensor_tensor(y1[:], y1[:], g2[:], ALU.mult).then_inc(M.y1, 1)
            pool.wait_ge(M.y1, 2 * p + 1)
            pool.wait_ge(M.gab, 2 * p + 2)
            pool.tensor_tensor(y1[:], y1[:], gate_a[:], ALU.mult).then_inc(M.y1, 1)
        pool.wait_ge(M.mask_loaded, 16)
        body(0)
        with pool.Fori(1, N) as p:
            body(p)

    return Names(sp=sp, act=act, dve=dve, pe=pe, pool=pool, y_ready=y_ready, late=(6, 7))


def score_tile(i):
    return P * (i + 1)


def conv_attention_mixer(k, st, t, h1):
    bank, S, scratch = k.bank, k.S, k.scratch
    N, PER = st.bodies, st.per
    k.free("m2")
    gb = scratch("m2", "gb", [SEQ])
    gc = scratch("m2", "gc", [SEQ])
    xa = scratch("m2", "xa", [SEQ])
    cu = scratch("m2", "cu", [SEQ])
    cc = scratch("m2", "cc", [SEQ])
    yc = scratch("m2", "yc", [SEQ])
    y = scratch("m2", "y", [SEQ])
    qk = scratch("m2", "qk", [2, SEQ])
    vT = scratch("m2", "vT", [SEQ])
    prob = scratch("m2", "prob", [4, SEQ])
    probT = scratch("m2", "probT", [2, SEQ])
    v_tok = scratch("m2", "v_tok", [4, P])
    bias = scratch("m2", "bias", [2, SEQ])
    mx = scratch("m2", "mx", [8])
    den = scratch("m2", "den", [8])
    buckets = scratch("m2", "buckets", [DIST + 8])
    dist_add = scratch("m2", "dist_add", [DIST])
    table = scratch("m2", "table", [DIST])
    M = k.sems("m2_", "evac cu cc yc yc_hi yc_low v_tr v_ev scores biased negmax exps rden scaled p_tr p_ev pv "
                      "bias_loaded tab_in tab_mm tab_sum tab_out y_f y_hi y_low")

    def load_params(act, u):
        wait(act, M.biased, 8 * u)
        for hh in range(2):
            src = bass.AP(tensor=t["dist_table"].tensor, offset=DIST * 2 * u + (DIST * hh + 1), ap=[[1, P], [1, SEQ]])
            act.dma_start(bias[:, hh], src).then_inc(M.bias_loaded, 16)

    def sp(sp):
        for j in range(5):
            k.load_unit(sp, st, 0, j)
        sp.wait_ge(S.h_ready, h1)
        sp.dma_start(buckets[0:32, 0:8], t["rel_bias_2"]).then_inc(M.tab_in, 16)
        sp.dma_start(buckets[0:32, 8:8 + DIST], t["dist_onehot"]).then_inc(M.tab_in, 16)
        sp.dma_start(dist_add[0:8, :], t["dist_add"]).then_inc(M.tab_in, 16)
        k.load_unit(sp, st, 0, 5)
        with sp.Fori(1, N) as u:
            for j in range(PER):
                k.load_unit(sp, st, u, j)

    def evac(act, u, j):
        act.wait_ge(S.mm_done, st.done(u, j))
        src = bank[st.bank[j]][:]
        if j == 0:
            wait(act, M.yc, u)
            act.activation(gb[:], src, ACT.Copy).then_inc(M.evac, 1)
        elif j in (1, 2):
            wait(act, M.cu, u)
            act.activation((gc, xa)[j - 1][:], src, ACT.Copy).then_inc(M.evac, 1)
        elif j in (3, 4):
            wait(act, M.scores, 8 * u)
            act.activation(qk[:, j - 3], src, ACT.Copy, scale=0.125 if j == 3 else 1.0).then_inc(M.evac, 1)
        else:
            wait(act, M.v_tr, u)
            act.activation(vT[:], src, ACT.Copy).then_inc(M.evac, 1)

    def act_probs(act, p, s):
        w = score_tile(s % 4)
        act.wait_ge(M.negmax, 8 * p + (s + 1))
        act.activation(prob[:, s % 4, 0:w], prob[:, s % 4, 0:w], ACT.Exp, bias=mx[:, s:s + 1],
                       accum_out=den[:, s:s + 1]).then_inc(M.exps, 1)

    def act_probT(act, p, s):
        w = score_tile(s % 4)
        act.wait_ge(M.p_tr, 8 * p + (s + 1))
        wait(act, M.pv, 8 * p + (s - 1))
        act.activation(probT[:, s % 2, 0:w], bank[6][:, 0:w], ACT.Copy).then_inc(M.p_ev, 1)

    def act(act, after):
        def body(p, units, prev, tail):
            u = p + 1

            def slot(j):
                if units and not (isinstance(u, int) and u == 0 and j < st.early):
                    k.split_hi(act, st, u, j)
                if prev and not units and j < after.early:
                    k.split_hi(act, after, 0, j)
            slot(0)
            if tail:
                act_probT(act, p - 1, 4)
                act_probs(act, p - 1, 6)
                act_probT(act, p - 1, 5)
                act_probs(act, p - 1, 7)
            if prev:
                evac(act, p, 3)
                evac(act, p, 4)
            slot(1)
            if prev:
                evac(act, p, 5)
            if tail:
                if prev:
                    load_params(act, p)
                act_probT(act, p - 1, 6)
                act_probT(act, p - 1, 7)
            slot(2)
            if prev:
                act_probs(act, p, 0)
                act_probs(act, p, 1)
            if tail:
                act.wait_ge(M.y_f, p)
                act.activation(k.tile_of(k.aH, p + 3), y[:], ACT.Copy).then_inc(M.y_hi, 1)
            if units:
                evac(act, u, 0)
            slot(3)
            if prev:
                act.wait_ge(M.yc, p + 1)
                act.activation(k.tile_of(k.aH, p), yc[:], ACT.Copy).then_inc(M.yc_hi, 1)
                act.wait_ge(M.v_tr, p + 1)
                act.activation(v_tok[:], bank[6][:].rearrange("p (a n) -> p a n", a=4), ACT.Copy).then_inc(M.v_ev, 1)
            if units:
                evac(act, u, 1)
            slot(4)
            if prev:
                act_probT(act, p, 0)
                act_probs(act, p, 2)
                act_probT(act, p, 1)
                act_probs(act, p, 3)
            if units:
                evac(act, u, 2)
            slot(5)
            if prev:
                act_probT(act, p, 2)
                act_probs(act, p, 4)
                act_probT(act, p, 3)
                act_probs(act, p, 5)
        body(-1, True, False, False)
        act.wait_ge(M.tab_sum, 2)
        act.dma_start(t["dist_table"], table[0:8, :]).then_inc(M.tab_out, 16)
        act.wait_ge(M.tab_out, 16)
        load_params(act, 0)
        body(0, True, True, False)
        with act.Fori(1, N - 1) as p:
            body(p, True, True, True)
        body(N - 1, False, True, True)
        body(N, False, False, True)

    def dve_scores(dve, p, s):
        hh, i = s // 4, s % 4
        w = score_tile(i)
        dve.wait_ge(M.scores, 8 * p + (s + 1))
        wait(dve, M.p_tr, 8 * p + (s - 3))
        if s == 0:
            dve.wait_ge(M.bias_loaded, 32 * p + 32)
        own_wait(dve, k.held_dve)
        dve.tensor_tensor_reduce(out=prob[:, i, 0:w], in0=bank[4 + s % 2][:, 0:w], in1=bias[:, hh, 0:w][:, ::-1],
                                 scale=1.0, scalar=-3.0e38, op0=ALU.add, op1=ALU.max,
                                 accum_out=mx[:, s:s + 1]).then_inc(M.biased, 1)
        dve.wait_ge(M.biased, 8 * p + (s + 1))
        dve.tensor_scalar(mx[:, s:s + 1], mx[:, s:s + 1], -1.0, None, ALU.mult).then_inc(M.negmax, 1)

    def dve_scale(dve, p, s):
        w = score_tile(s % 4)
        dve.wait_ge(M.exps, 8 * p + (s + 1))
        dve.reciprocal(den[:, s:s + 1], den[:, s:s + 1]).then_inc(M.rden, 1)
        dve.wait_ge(M.rden, 8 * p + (s + 1))
        dve.tensor_scalar(prob[:, s % 4, 0:w], prob[:, s % 4, 0:w], den[:, s:s + 1], None, ALU.mult)\
           .then_inc(M.scaled, 1)

    def dve(dve, after):
        def body(p, units, prev, tail):
            u = p + 1

            def slot(j):
                if units and not (isinstance(u, int) and u == 0 and j < st.early):
                    k.split_lo(dve, st, u, j)
                if prev and not units and j < after.early:
                    k.split_lo(dve, after, 0, j)
            slot(0)
            if tail:
                dve_scores(dve, p - 1, 6)
                dve_scores(dve, p - 1, 7)
                dve_scale(dve, p - 1, 6)
                dve_scale(dve, p - 1, 7)
            slot(1)
            if prev:
                dve.wait_ge(M.evac, PER * p + 3)
                dve.tensor_tensor(cu[:], gc[:], xa[:], ALU.mult).then_inc(M.cu, 1)
                dve.wait_ge(M.cu, p + 1)
                dve.tensor_scalar(cc[:], cu[:], k.colr("w_sc_2", 8 + p), None, ALU.mult).then_inc(M.cc, 1)
                for n, shift in enumerate((1, 2)):
                    dve.wait_ge(M.cc, 3 * p + (n + 1))
                    dve.scalar_tensor_tensor(cc[:, shift:], cu[:, 0:SEQ - shift], k.colr("w_sc_2", 4 * (2 - shift) + p),
                                             cc[:, shift:], ALU.mult, ALU.add).then_inc(M.cc, 1)
                dve.wait_ge(M.cc, 3 * p + 3)
                wait(dve, M.yc_low, p)
                dve.tensor_tensor(yc[:], cc[:], gb[:], ALU.mult).then_inc(M.yc, 1)
            slot(2)
            if tail:
                dve.wait_ge(M.pv, 8 * p)
                wait(dve, M.y_low, p - 1)
                dve.tensor_copy(y[:], bank[7][:]).then_inc(M.y_f, 1)
            if prev:
                for s in (0, 1):
                    dve_scores(dve, p, s)
                for s in (0, 1):
                    dve_scale(dve, p, s)
            if tail:
                dve.wait_ge(M.y_hi, p)
                dve.tensor_tensor(k.tile_of(k.aL, p + 3), y[:], k.tile_of(k.aH, p + 3).bitcast(F32), ALU.subtract)\
                   .then_inc(M.y_low, 1)
            slot(3)
            if prev:
                dve.wait_ge(M.yc_hi, p + 1)
                dve.tensor_tensor(k.tile_of(k.aL, p), yc[:], k.tile_of(k.aH, p).bitcast(F32), ALU.subtract)\
                   .then_inc(M.yc_low, 1)
            slot(4)
            if prev:
                for s in (2, 3):
                    dve_scores(dve, p, s)
                    dve_scale(dve, p, s)
            slot(5)
            if prev:
                for s in (4, 5):
                    dve_scores(dve, p, s)
                    dve_scale(dve, p, s)
        body(-1, True, False, False)
        dve.wait_ge(M.tab_in, 48)
        for n, (a, b) in enumerate(((0, HALF_W), (HALF_W, DIST))):
            dve.wait_ge(M.tab_mm, n + 1)
            dve.tensor_tensor(table[0:8, a:b], bank[6 + n][0:8, 0:b - a], dist_add[0:8, a:b], ALU.add)\
               .then_inc(M.tab_sum, 1)
        body(0, True, True, False)
        with dve.Fori(1, N - 1) as p:
            body(p, True, True, True)
        body(N - 1, False, True, True)
        body(N, False, False, True)

    def y_ready(pe):
        return lambda f: pe.wait_ge(M.yc_low, f + 1) if f < 4 else pe.wait_ge(M.y_low, f - 3)

    early = (0, 1, 2, 4, 5)

    def pe_scores(pe, p, s):
        hh, i = s // 4, s % 4
        if s == 0:
            pe.wait_ge(M.evac, PER * p + 5)
        wait(pe, M.biased, 8 * p + (s - 1))
        pe.matmul(bank[4 + s % 2][:, 0:score_tile(i)], qk[64 * hh:64 * hh + 64, 0, P * i:P * i + P],
                  qk[64 * hh:64 * hh + 64, 1, 0:score_tile(i)], start=True, stop=True).then_inc(M.scores, 1)

    def pe_probT(pe, p, s):
        pe.wait_ge(M.scaled, 8 * p + (s + 1))
        if s == 0:
            pe.wait_ge(M.v_ev, p + 1)
        else:
            pe.wait_ge(M.p_ev, 8 * p + s)
        for n in range(s % 4 + 1):
            last = pe.transpose(bank[6][:, P * n:P * n + P], prob[:, s % 4, P * n:P * n + P], k.ident[:])
        last.then_inc(M.p_tr, 1)

    def pe_pv(pe, p, s):
        hh, i = s // 4, s % 4
        pe.wait_ge(M.p_ev, 8 * p + (s + 1))
        if s == 0:
            wait(pe, M.y_f, p)
        for n in range(i + 1):
            last = pe.matmul(bank[7][64 * hh:64 * hh + 64, P * i:P * i + P], v_tok[:, n, 64 * hh:64 * hh + 64],
                             probT[:, s % 2, P * n:P * n + P], start=n == 0, stop=n == i)
        last.then_inc(M.pv, 1)

    def pe(pe, h0, after):
        def body(p, units, prev, tail):
            u = p + 1

            def unit(j):
                if not units:
                    if prev and 1 <= j <= after.early:
                        if j == 1:
                            pe.wait_ge(M.evac, PER * N)
                            for f in early:
                                y_ready(pe)(f)
                        k.proj_start(pe, after, j - 1, early)
                    return
                if isinstance(u, int) and u == 0 and j < 2:
                    if j == 0:
                        k.first_products(pe, st, (bank[0][:], bank[1][:]), h0 - 8)
                    return
                back = next(b for b in range(1, PER + 1) if st.bank[(j - b) % PER] == st.bank[j])
                wait(pe, M.evac, PER * u + (j - back + 1))
                k.unit_product(pe, st, u, j, bank[st.bank[j]][:], (k.hH, k.hL), 0, True, True)
            unit(0)
            if tail:
                pe_pv(pe, p - 1, 6)
                pe_pv(pe, p - 1, 7)
            if prev:
                pe_scores(pe, p, 0)
                pe_scores(pe, p, 1)
            unit(1)
            if prev:
                pe.wait_ge(M.evac, PER * p + 6)
                wait(pe, M.p_ev, 8 * p)
                for n in range(4):
                    last = pe.transpose(bank[6][:, P * n:P * n + P], vT[:, P * n:P * n + P], k.ident[:])
                last.then_inc(M.v_tr, 1)
            unit(2)
            if prev:
                pe_probT(pe, p, 0)
                pe_scores(pe, p, 2)
                pe_probT(pe, p, 1)
                pe_scores(pe, p, 3)
            unit(3)
            if prev:
                pe_pv(pe, p, 0)
                pe_probT(pe, p, 2)
                pe_scores(pe, p, 4)
                pe_pv(pe, p, 1)
                pe_probT(pe, p, 3)
                pe_scores(pe, p, 5)
            unit(4)
            if prev:
                pe_pv(pe, p, 2)
                pe_probT(pe, p, 4)
                pe_scores(pe, p, 6)
                pe_pv(pe, p, 3)
                pe_probT(pe, p, 5)
                pe_scores(pe, p, 7)
            unit(5)
            if prev:
                pe_pv(pe, p, 4)
                pe_probT(pe, p, 6)
                pe_pv(pe, p, 5)
                pe_probT(pe, p, 7)
        body(-1, True, False, False)
        pe.wait_ge(M.tab_in, 48)
        pe.matmul(bank[6][0:8, 0:HALF_W], buckets[0:32, 0:8], buckets[0:32, 8:8 + HALF_W], start=True, stop=True)\
          .then_inc(M.tab_mm, 1)
        pe.matmul(bank[7][0:8, 0:DIST - HALF_W], buckets[0:32, 0:8], buckets[0:32, 8 + HALF_W:8 + DIST], start=True,
                  stop=True).then_inc(M.tab_mm, 1)
        pe.wait_ge(M.tab_sum, 2)
        body(0, True, True, False)
        with pe.Fori(1, N - 1) as p:
            body(p, True, True, True)
        body(N - 1, False, True, True)
        body(N, False, False, True)

    def pool(pool):
        pass

    return Names(sp=sp, act=act, dve=dve, pe=pe, pool=pool, y_ready=y_ready, late=(3, 6, 7))


def stick_mixer(k, st, t, h1):
    bank, S, scratch = k.bank, k.S, k.scratch
    N, PER = st.bodies, st.per
    TAPS = 31
    k.free("m3")
    a_half = scratch("m3", "a_half", [SEQ])
    tg = scratch("m3", "tg", [SEQ])
    gp = scratch("m3", "gp", [TAPS - 1 + SEQ])
    acc = scratch("m3", "acc", [SEQ])
    cv = scratch("m3", "cv", [4, SEQ])
    qk = scratch("m3", "qk", [2, SEQ])
    vT = scratch("m3", "vT", [SEQ])
    rest = scratch("m3", "rest", [2, SEQ])
    beta = scratch("m3", "beta", [2, SEQ])
    later = scratch("m3", "later", [2, SEQ + 2])
    aw = scratch("m3", "aw", [4, SEQ])
    awT = scratch("m3", "awT", [2, SEQ])
    v_tok = scratch("m3", "v_tok", [4, P])
    zeros = scratch("m3", "zeros", [SEQ])
    before = scratch("m3", "before", [P])
    y = scratch("m3", "y", [SEQ])
    ln_sq = scratch("m3", "ln_sq", [2, SEQ])
    ln_sum = scratch("m3", "ln_sum", [SEQ])
    M = k.sems("m3_", "evac zeroed g cv v_tr v_ev scores masked sig scan aw_done a_tr a_ev pv mask_loaded y_f y_hi "
                      "y_low ln ln_mm ln_sq ln_rs silu yc_hi yc_low")

    def sp(sp):
        for j in range(PER):
            k.load_unit(sp, st, 0, j)
        sp.wait_ge(S.h_ready, h1)
        sp.dma_start(before[:], t["before"]).then_inc(M.mask_loaded, 16)
        with sp.Fori(1, N) as u:
            for j in range(PER):
                k.load_unit(sp, st, u, j)

    def evac(act, u, j):
        act.wait_ge(S.mm_done, st.done(u, j))
        src = bank[st.bank[j]][:]
        if j == 0:
            wait(act, M.g, u)
            act.activation(a_half[:], src, ACT.Copy, scale=0.5).then_inc(M.evac, 1)
        elif j == 1:
            wait(act, M.g, u)
            act.activation(tg[:], src, ACT.Tanh, scale=0.5).then_inc(M.evac, 1)
        elif j in (2, 3):
            wait(act, M.scores, 8 * u)
            act.activation(qk[:, j - 2], src, ACT.Copy).then_inc(M.evac, 1)
        else:
            wait(act, M.v_tr, u)
            act.activation(vT[:], src, ACT.Copy).then_inc(M.evac, 1)

    def act_sig(act, p, s):
        w = score_tile(s % 4)
        act.wait_ge(M.masked, 8 * p + (s + 1))
        wait(act, M.scan, 8 * p + (s - 1))
        act.activation(rest[:, s % 2, 0:w], bank[4 + s % 2][:, 0:w], ACT.Sigmoid, scale=-0.125).then_inc(M.sig, 1)
        wait(act, M.aw_done, 8 * p + (s - 1))
        act.activation(beta[:, s % 2, 0:w], bank[4 + s % 2][:, 0:w], ACT.Sigmoid, scale=0.125).then_inc(M.sig, 1)

    def act_awT(act, p, s):
        w = score_tile(s % 4)
        act.wait_ge(M.a_tr, 8 * p + (s + 1))
        wait(act, M.pv, 8 * p + (s - 1))
        act.activation(awT[:, s % 2, 0:w], bank[6][:, 0:w], ACT.Copy).then_inc(M.a_ev, 1)

    def act(act, after):
        def body(p, units, prev, tail):
            u = p + 1

            def slot(j):
                if units and not (isinstance(u, int) and u == 0 and j < st.early):
                    k.split_hi(act, st, u, j)
                if prev and not units and j < after.early:
                    k.split_hi(act, after, 0, j)
            slot(0)
            if tail:
                act_awT(act, p - 1, 2)
                act_sig(act, p - 1, 6)
                act_awT(act, p - 1, 3)
                act_sig(act, p - 1, 7)
            if prev:
                evac(act, p, 2)
                evac(act, p, 3)
            slot(1)
            if tail:
                act_awT(act, p - 1, 4)
                act_awT(act, p - 1, 5)
            if prev:
                evac(act, p, 4)
            slot(2)
            if units:
                evac(act, u, 0)
            if tail:
                act_awT(act, p - 1, 6)
                act_awT(act, p - 1, 7)
            if prev:
                act_sig(act, p, 0)
                act_sig(act, p, 1)
            slot(3)
            if prev:
                act.wait_ge(M.v_tr, p + 1)
                act.activation(v_tok[:], bank[6][:].rearrange("p (a n) -> p a n", a=4), ACT.Copy).then_inc(M.v_ev, 1)
                act_sig(act, p, 2)
                act_sig(act, p, 3)
            if tail and prev:
                act.wait_ge(M.y_f, p)
                act.activation(k.tile_of(k.aH, p + 3), y[:], ACT.Copy).then_inc(M.y_hi, 1)
            if units:
                evac(act, u, 1)
            slot(4)
            if prev:
                act_awT(act, p, 0)
                act_sig(act, p, 4)
                act_awT(act, p, 1)
                act_sig(act, p, 5)
        body(-1, True, False, False)
        body(0, True, True, False)
        with act.Fori(1, N - 1) as p:
            body(p, True, True, True)
        body(N - 1, False, True, True)
        body(N, False, False, True)
        for n in range(4):
            act.wait_ge(M.ln, 4 + n)
            wait(act, M.ln, 8 + n - 2 if n >= 2 else 0)
            act.activation(ln_sq[:, n % 2], cv[:, n], ACT.Square).then_inc(M.ln_sq, 1)
        act.wait_ge(M.y_f, N)
        act.activation(k.tile_of(k.aH, N + 3), y[:], ACT.Copy).then_inc(M.y_hi, 1)
        act.wait_ge(M.ln_mm, 2)
        act.activation(ln_sum[:], bank[5][:], ACT.Ln, bias=k.eps_col[:]).then_inc(M.ln_rs, 1)
        act.wait_ge(M.ln_rs, 1)
        act.activation(ln_sum[:], ln_sum[:], ACT.Exp, scale=-0.5).then_inc(M.ln_rs, 1)
        for n in range(4):
            act.wait_ge(M.ln, 12 + n)
            act.activation(cv[:, n], cv[:, n], ACT.Silu, bias=k.col("ln_cc_b_2", n)).then_inc(M.silu, 1)
        for n in range(4):
            act.wait_ge(M.silu, n + 1)
            act.activation(k.aH[:, n], cv[:, n], ACT.Copy).then_inc(M.yc_hi, 1)

    def dve_mask(dve, p, s):
        w = score_tile(s % 4)
        dve.wait_ge(M.scores, 8 * p + (s + 1))
        diag = bank[4 + s % 2][:, w - P:w]
        dve.tensor_tensor(diag, diag, before[:], ALU.add).then_inc(M.masked, 1)

    def dve_scan(dve, p, s):
        w = score_tile(s % 4)
        dve.wait_ge(M.sig, 16 * p + (2 * s + 1))
        wait(dve, M.aw_done, 8 * p + (s - 1))
        out = later[:, s % 2, SEQ - w:SEQ]
        dve.tensor_tensor_scan(out=out[:, ::-1], data0=rest[:, s % 2, 0:w][:, ::-1], data1=zeros[:, 0:w], initial=1.0,
                               op0=ALU.mult, op1=ALU.add).then_inc(M.scan, 1)

    def dve_taps(dve, p, lo, hi):
        for n in range(lo, hi):
            w = k.colr("w_cc_2", 4 * n + p)
            if n == 0:
                wait(dve, M.g, p + 1)
                dve.tensor_scalar(acc[:], gp[:, 0:SEQ], w, k.colr("b_cc_2", p), ALU.mult, ALU.add).then_inc(M.cv, 1)
                continue
            dve.wait_ge(M.cv, TAPS * p + n)
            dst = acc[:] if n < TAPS - 1 else k.tile_of(cv, p)
            dve.scalar_tensor_tensor(dst, gp[:, n:n + SEQ], w, acc[:], ALU.mult, ALU.add).then_inc(M.cv, 1)

    def dve_out(dve, q):
        dve.wait_ge(M.pv, 8 * q + 8)
        wait(dve, M.y_low, q)
        dve.tensor_copy(y[:], bank[7][:]).then_inc(M.y_f, 1)

    def dve_low(dve, q):
        dve.wait_ge(M.y_hi, q + 1)
        dve.tensor_tensor(k.tile_of(k.aL, q + 4), y[:], k.tile_of(k.aH, q + 4).bitcast(F32), ALU.subtract)\
           .then_inc(M.y_low, 1)

    def dve(dve, after):
        def masks(p, s):
            for n in (s, s + 1):
                dve_mask(dve, p, n)

        def scans(p, s):
            for n in (s, s + 1):
                dve_scan(dve, p, n)

        def body(p, units, prev, tail):
            u = p + 1

            def slot(j):
                if units and not (isinstance(u, int) and u == 0 and j < st.early):
                    k.split_lo(dve, st, u, j)
                if prev and not units and j < after.early:
                    k.split_lo(dve, after, 0, j)
            slot(0)
            if tail:
                masks(p - 1, 6)
            if prev:
                dve.wait_ge(M.evac, PER * p + 2)
                wait(dve, M.cv, TAPS * p)
                dve.scalar_tensor_tensor(gp[:, TAPS - 1:TAPS - 1 + SEQ], tg[:], 1.0, a_half[:], ALU.add, ALU.mult)\
                   .then_inc(M.g, 1)
                dve_taps(dve, p, 0, 3)
            elif tail:
                dve.wait_ge(M.cv, TAPS * N)
                dve.tensor_tensor(acc[:], cv[:, 0], cv[:, 1], ALU.add).then_inc(M.ln, 1)
                for n in (2, 3):
                    dve.wait_ge(M.ln, n - 1)
                    dve.tensor_tensor(acc[:], acc[:], cv[:, n], ALU.add).then_inc(M.ln, 1)
            if tail:
                scans(p - 1, 6)
            if prev:
                dve_taps(dve, p, 3, 8)
            slot(1)
            if prev:
                dve_taps(dve, p, 8, 15)
            slot(2)
            if prev:
                masks(p, 0)
                dve_taps(dve, p, 15, 17)
                scans(p, 0)
                dve_taps(dve, p, 17, 20)
            slot(3)
            if prev:
                masks(p, 2)
            if tail and prev:
                dve_out(dve, p - 1)
            if prev:
                dve_taps(dve, p, 20, 22)
                scans(p, 2)
                dve_taps(dve, p, 22, 25)
            if tail and prev:
                dve_low(dve, p - 1)
            slot(4)
            if prev:
                masks(p, 4)
                dve_taps(dve, p, 25, 27)
                scans(p, 4)
                dve_taps(dve, p, 27, TAPS)
        dve.memset(gp[:, 0:TAPS - 1], 0.0).then_inc(M.zeroed, 1)
        dve.memset(zeros[:], 0.0).then_inc(M.zeroed, 1)
        dve.memset(later[:, :, SEQ:SEQ + 1], 1.0).then_inc(M.zeroed, 1)
        dve.wait_ge(M.zeroed, 3)
        dve.wait_ge(M.mask_loaded, 16)
        body(-1, True, False, False)
        body(0, True, True, False)
        with dve.Fori(1, N - 1) as p:
            body(p, True, True, True)
        body(N - 1, False, True, True)
        body(N, False, False, True)
        dve.wait_ge(M.ln_mm, 1)
        for n in range(4):
            dve.tensor_tensor(cv[:, n], cv[:, n], bank[4][:], ALU.subtract).then_inc(M.ln, 1)
        dve_out(dve, N - 1)
        for n in range(4):
            dve.wait_ge(M.ln_sq, n + 1)
            if n == 0:
                dve.tensor_copy(acc[:], ln_sq[:, 0]).then_inc(M.ln, 1)
            else:
                dve.wait_ge(M.ln, 7 + n)
                dve.tensor_tensor(acc[:], acc[:], ln_sq[:, n % 2], ALU.add).then_inc(M.ln, 1)
        dve_low(dve, N - 1)
        dve.wait_ge(M.ln_rs, 2)
        for n in range(4):
            dve.scalar_tensor_tensor(cv[:, n], cv[:, n], k.col("ln_cc_g_2", n), ln_sum[:], ALU.mult, ALU.mult)\
               .then_inc(M.ln, 1)
        for n in range(4):
            dve.wait_ge(M.yc_hi, n + 1)
            dve.tensor_tensor(k.aL[:, n], cv[:, n], k.aH[:, n].bitcast(F32), ALU.subtract).then_inc(M.yc_low, 1)

    def y_ready(pe):
        return lambda f: pe.wait_ge(M.yc_low, f + 1) if f < 4 else pe.wait_ge(M.y_low, f - 3)

    early = (4, 5)

    def pe_scores(pe, p, s):
        hh, i = s // 4, s % 4
        if s == 0:
            pe.wait_ge(M.evac, PER * p + 4)
        wait(pe, M.sig, 16 * p + 2 * (s - 1))
        pe.matmul(bank[4 + s % 2][:, 0:score_tile(i)], qk[64 * hh:64 * hh + 64, 0, P * i:P * i + P],
                  qk[64 * hh:64 * hh + 64, 1, 0:score_tile(i)], start=True, stop=True).then_inc(M.scores, 1)

    def pe_awT(pe, p, s):
        pe.wait_ge(M.aw_done, 8 * p + (s + 1))
        if s == 0:
            pe.wait_ge(M.v_ev, p + 1)
        else:
            pe.wait_ge(M.a_ev, 8 * p + s)
        for n in range(s % 4 + 1):
            last = pe.transpose(bank[6][:, P * n:P * n + P], aw[:, s % 4, P * n:P * n + P], k.ident[:])
        last.then_inc(M.a_tr, 1)

    def pe_pv(pe, p, s):
        hh, i = s // 4, s % 4
        pe.wait_ge(M.a_ev, 8 * p + (s + 1))
        if s == 0:
            wait(pe, M.y_f, p)
        for n in range(i + 1):
            last = pe.matmul(bank[7][64 * hh:64 * hh + 64, P * i:P * i + P], v_tok[:, n, 64 * hh:64 * hh + 64],
                             awT[:, s % 2, P * n:P * n + P], start=n == 0, stop=n == i)
        last.then_inc(M.pv, 1)

    def pe(pe, h0, after):
        def body(p, units, prev, tail):
            u = p + 1

            def unit(j):
                if not units:
                    if prev and 1 <= j <= after.early:
                        if j == 1:
                            pe.wait_ge(M.evac, PER * N)
                            for f in early:
                                y_ready(pe)(f)
                        k.proj_start(pe, after, j - 1, early)
                    return
                if isinstance(u, int) and u == 0 and j < 2:
                    if j == 0:
                        k.first_products(pe, st, (bank[0][:], bank[1][:]), h0 - 8)
                    return
                back = next(b for b in range(1, PER + 1) if st.bank[(j - b) % PER] == st.bank[j])
                wait(pe, M.evac, PER * u + (j - back + 1))
                k.unit_product(pe, st, u, j, bank[st.bank[j]][:], (k.hH, k.hL), 0, True, True)
            unit(0)
            if tail:
                pe_pv(pe, p - 1, 4)
                pe_awT(pe, p - 1, 6)
                pe_pv(pe, p - 1, 5)
                pe_awT(pe, p - 1, 7)
            if prev:
                pe_scores(pe, p, 0)
                pe_scores(pe, p, 1)
            elif tail:
                pe.wait_ge(M.ln, 3)
                pe.wait_ge(M.sig, 16 * p)
                pe.matmul(bank[4][:], k.ones_half[:], acc[:], start=True, stop=True).then_inc(M.ln_mm, 1)
            unit(1)
            if tail:
                pe_pv(pe, p - 1, 6)
                pe_pv(pe, p - 1, 7)
            if prev:
                pe_scores(pe, p, 2)
                pe_scores(pe, p, 3)
                pe.wait_ge(M.evac, PER * p + 5)
                wait(pe, M.a_ev, 8 * p)
                for n in range(4):
                    last = pe.transpose(bank[6][:, P * n:P * n + P], vT[:, P * n:P * n + P], k.ident[:])
                last.then_inc(M.v_tr, 1)
            unit(2)
            if prev:
                pe_awT(pe, p, 0)
                pe_scores(pe, p, 4)
                pe_awT(pe, p, 1)
                pe_scores(pe, p, 5)
            unit(3)
            if prev:
                pe_pv(pe, p, 0)
                pe_awT(pe, p, 2)
                pe_scores(pe, p, 6)
                pe_pv(pe, p, 1)
                pe_awT(pe, p, 3)
                pe_scores(pe, p, 7)
            unit(4)
            if prev:
                pe_pv(pe, p, 2)
                pe_awT(pe, p, 4)
                pe_pv(pe, p, 3)
                pe_awT(pe, p, 5)
        body(-1, True, False, False)
        body(0, True, True, False)
        with pe.Fori(1, N - 1) as p:
            body(p, True, True, True)
        body(N - 1, False, True, True)
        body(N, False, False, True)
        pe.wait_ge(M.ln, 11)
        pe.matmul(bank[5][:], k.ones_half[:], acc[:], start=True, stop=True).then_inc(M.ln_mm, 1)

    def pool(pool):
        def body(p):
            for s in range(8):
                w = score_tile(s % 4)
                pool.wait_ge(M.scan, 8 * p + (s + 1))
                pool.wait_ge(M.sig, 16 * p + (2 * s + 2))
                wait(pool, M.a_tr, 8 * p + (s - 3))
                pool.tensor_tensor(aw[:, s % 4, 0:w], beta[:, s % 2, 0:w], later[:, s % 2, SEQ - w + 1:SEQ + 1], ALU.mult)\
                    .then_inc(M.aw_done, 1)
        body(0)
        with pool.Fori(1, N) as p:
            body(p)

    return Names(sp=sp, act=act, dve=dve, pe=pe, pool=pool, y_ready=y_ready, late=(6, 7, 0, 1, 2, 3))


def build(nc, t):
    Stream.units_before = 0
    Stream.newest = None
    Stream.loads_before = [0] * 5
    GU1 = Stream(t["w_ffn1_gu"], FT // 2, 4, 8)
    DN1 = Stream(t["w_ffn1_down"], 4, 4, 11)
    IN1 = Stream(t["w_in"], 8, 7, 8)
    OUT1 = Stream(t["w_out"], 2, 4, 8, early=True)
    GU2 = Stream(t["w_ffn2_gu"], FT // 2, 4, 8)
    DN2 = Stream(t["w_ffn2_down"], 4, 4, 11)
    IN2 = Stream(t["w_in_even_2"], 4, 6, 8)
    OUT2 = Stream(t["w_out_even_2"], 2, 4, 8, early=True)
    GU3 = Stream(t["w_up_2a"], FT // 2, 4, 8)
    DN3 = Stream(t["w_down_2a"], 4, 4, 11)
    IN3 = Stream(t["w_in_odd_2"], 4, 5, 8)
    OUT3 = Stream(t["w_out_odd_2"], 2, 4, 8, early=True)
    GU4 = Stream(t["w_up_2b"], FT // 2, 4, 8)
    DN4 = Stream(t["w_down_2b"], 4, 4, 11)

    with ExitStack() as ctx:
        def at(name, shape, word, dt=F32):
            n = 1
            for s in shape:
                n *= s
            assert word + n <= TOP, (name, word, n, TOP)
            return nc.alloc_sbuf_tensor_at(name, [P] + list(shape), dt, offset=BASE + 4 * word)

        BASE = 4096
        TOP = (229344 - BASE) // 4
        xT = at("xT", [DT, SEQ], 0)
        hH = at("hH", [DT, SEQ], 4096, F32R)
        hL = at("hL", [DT, SEQ], 8192, F32R)
        mixT = at("mixT", [DT, SEQ], 4096)
        raw = at("raw", [5632], 12288)
        wH = at("wH", [4224], 17920, F32R)
        wL = at("wL", [4224], 22144, F32R)
        aH = at("aH", [FT, SEQ], 26368, F32R)
        aL = at("aL", [FT, SEQ], 37632, F32R)
        cols = at("cols", [N_COLS], 48896)
        o = 48896 + -(-N_COLS // 8) * 8
        ident = at("ident", [P], o)
        heads1 = at("heads1", [P], o + 128)
        ones = at("ones", [P], o + 256)
        ones_half = at("ones_half", [P], o + 384)
        lam = at("lam", [16], o + 512)
        sp2 = at("sp2", [16], o + 528)
        lam_t = at("lam_t", [4, 16], o + 544)
        hbg = at("hbg", [32], o + 608)
        qg = at("qg", [1], o + 640)
        eps_col = at("eps_col", [1], o + 648)
        T0 = o + 672
        silu_g = at("silu_g", [2, SEQ], T0)
        prod = at("prod", [2, SEQ], T0 + 1024)
        square = at("square", [2, SEQ], T0 + 2048)
        hf = at("hf", [2, SEQ], T0 + 3072)
        rs = at("rs", [SEQ], T0 + 4096)
        rstd = at("rstd", [SEQ], T0 + 4608)
        ssq = at("ssq", [SEQ], T0 + 5120)
        assert T0 + 5632 <= TOP, (T0 + 5632, TOP)
        regions = {}

        def free(which):
            regions[which] = [[26368 + 8 * SEQ, 26368 + 22 * SEQ], [37632 + 8 * SEQ, 37632 + 22 * SEQ], [T0, TOP]]

        def scratch(which, name, shape):
            n = 1
            for s in shape:
                n *= s
            n = -(-n // 8) * 8
            for r in regions[which]:
                if r[0] + n <= r[1]:
                    r[0] += n
                    return at(f"{which}_{name}", shape, r[0] - n)
            raise AssertionError((name, regions[which]))

        bank = [ctx.enter_context(nc.psum_tensor(f"bank{b}", [P, 512], F32)) for b in range(8)]

        def sems(prefix, names):
            return Names(**{n: ctx.enter_context(nc.semaphore(prefix + n)) for n in names.split()})

        S = sems("", "consts hi_done lo_done mm_done sq_done ssq_done stat_done rs_done rstd_done hf_done hh_done"
                     " h_ready silu_done conv_done prod_done ah_done a_ready proj_ev x_upd post_t small out_done acc_done lam_exp held_dve held_pool")
        x_loaded = [ctx.enter_context(nc.semaphore(f"x_loaded{n}")) for n in range(4)]
        raw_loaded = [ctx.enter_context(nc.semaphore(f"raw_loaded{s}")) for s in range(5)]
        block = ctx.enter_context(nc.Block())

        def col(name, n=0):
            return cols[:, COLS[name] + n:COLS[name] + n + 1]

        def colr(name, n):
            return cols[:, bass.ds(COLS[name] + n, 1)] if not isinstance(n, int) else col(name, n)

        def colat(buf, first, n):
            return buf[:, first + n:first + n + 1] if isinstance(n, int) else buf[:, bass.ds(first + n, 1)]

        def tile_of(buf, n):
            return buf[:, n] if isinstance(n, int) else buf[:, bass.ds(n, 1)].rearrange("p a n -> p (a n)")

        def raw_at(st, j):
            return raw[:, st.raw[j] * st.K * P:(st.raw[j] + 1) * st.K * P]

        def split_at(w, st, j):
            return w[:, st.split[j] * st.K * P:(st.split[j] + 1) * st.K * P]

        def load_unit(sp, st, i, j):
            wait(sp, S.lo_done, st.before("raw", i, j))
            src = st.dram[st.per * i + j] if isinstance(i, int) else \
                st.dram[bass.ds(st.per * i + j, 1)].rearrange("u p n -> p (u n)")
            sp.dma_start(raw_at(st, j), src).then_inc(raw_loaded[st.raw[j]], 16)

        def split_hi(act, st, i, j):
            wait(act, S.mm_done, st.before("split", i, j))
            act.wait_ge(raw_loaded[st.raw[j]], st.loaded(i, j))
            act.activation(split_at(wH, st, j), raw_at(st, j), ACT.Copy).then_inc(S.hi_done, 1)

        def split_lo(dve, st, i, j):
            dve.wait_ge(S.hi_done, st.done(i, j))
            dve.tensor_tensor(split_at(wL, st, j), raw_at(st, j), split_at(wH, st, j).bitcast(F32),
                              ALU.subtract).then_inc(S.lo_done, 1)

        def products(pe, st, i, j, out, rhs, k0, ks, start, stop):
            xh, xl = rhs
            for k in ks:
                w_h, w_l = (split_at(w, st, j)[:, k * P:(k + 1) * P] for w in (wH, wL))
                pe.matmul(out, w_h, xh[:, k0 + k], start=start and k == ks[0], stop=False)
                pe.matmul(out, w_h, xl[:, k0 + k], start=False, stop=False)
                last = pe.matmul(out, w_l, xh[:, k0 + k], start=False, stop=stop and k == ks[-1])
            return last

        def unit_product(pe, st, i, j, out, rhs, k0, start, stop, ready=None):
            pe.wait_ge(S.lo_done, st.done(i, j))
            if ready is None:
                products(pe, st, i, j, out, rhs, k0, range(st.K), start, stop).then_inc(S.mm_done, 1)
                return
            for k in range(st.K):
                ready(k0 + k)
                last = products(pe, st, i, j, out, rhs, k0, (k,), start and k == 0, stop and k == st.K - 1)
            last.then_inc(S.mm_done, 1)

        def first_products(pe, st, outs, h0):
            pe.wait_ge(S.lo_done, st.done(0, 1))
            for k in range(st.K):
                pe.wait_ge(S.h_ready, h0 + k + 1)
                last = [products(pe, st, 0, j, outs[j], (hH, hL), 0, (k,), k == 0, k == st.K - 1) for j in range(2)]
            for l in last:
                l.then_inc(S.mm_done, 1)

        class Tally:
            def __init__(self):
                self.norms = self.stats = self.pres = self.posts = self.ffns = self.convs = self.projs = 0

        def square_tile(act, q, m, src, odd):
            wait(act, S.ssq_done, 8 * q + m - 1)
            act.activation(square[:, odd], src, ACT.Square).then_inc(S.sq_done, 1)

        def add_square(dve, c, q, m, odd):
            dve.wait_ge(S.sq_done, 8 * q + 1 + m)
            if isinstance(m, int) and m == 0:
                wait(dve, S.stat_done, c.stats)
                dve.tensor_copy(ssq[:], square[:, odd]).then_inc(S.ssq_done, 1)
            else:
                dve.wait_ge(S.ssq_done, 8 * q + m)
                dve.tensor_tensor(ssq[:], ssq[:], square[:, odd], ALU.add).then_inc(S.ssq_done, 1)

        def norm_act(act, c, pre, st, then_square, after_post):
            q = c.norms
            if after_post:
                act.wait_ge(S.ssq_done, 8 * q + 8)
            else:
                c.stats += 1
                act.wait_ge(S.stat_done, c.stats)
            act.activation(rs[:], bank[4][:], ACT.Ln, bias=eps_col[:]).then_inc(S.rs_done, 1)
            act.wait_ge(S.rs_done, q + 1)
            act.activation(rstd[:], rs[:], ACT.Exp, scale=-0.5).then_inc(S.rstd_done, 1)
            c.norms += 1
            if pre:
                for k in range(DT):
                    wait(act, S.mm_done, st.n0)
                    act.wait_ge(S.hf_done, 8 * c.pres + k + 1)
                    act.activation(hH[:, k], hf[:, k % 2], ACT.Copy).then_inc(S.hh_done, 1)
                c.pres += 1
            else:
                for k in range(DT if then_square else 0):
                    act.wait_ge(S.x_upd, 8 * c.posts + k + 1)
                    square_tile(act, q + 1, k, xT[:, k], k % 2)
                c.posts += 1

        def norm_pe(pe, c, after_post):
            q = c.norms
            if after_post:
                pe.wait_ge(S.rs_done, q)
                for m in range(DT):
                    pe.wait_ge(S.sq_done, 8 * q + m + 1)
                    pe.matmul(bank[4][:], ones[:], square[:, m % 2], start=m == 0, stop=m == DT - 1)\
                      .then_inc(S.ssq_done, 1)
            else:
                pe.wait_ge(S.ssq_done, 8 * q + 8)
                pe.matmul(bank[4][:], ones[:], ssq[:], start=True, stop=True).then_inc(S.stat_done, 1)
            c.norms += 1

        def norm_dve(dve, c, gain, pre, after_post):
            q = c.norms
            c.norms += 1
            c.stats += not after_post
            if pre:
                b = 8 * c.pres
                for k in range(DT + 1):
                    if k < DT:
                        dve.wait_ge(S.rstd_done, q + 1)
                        wait(dve, S.h_ready, b + k - 1)
                        dve.scalar_tensor_tensor(hf[:, k % 2], xT[:, k], col(*gain(k)), rstd[:], ALU.mult,
                                                 ALU.mult).then_inc(S.hf_done, 1)
                    if k >= 1:
                        dve.wait_ge(S.hh_done, b + k)
                        dve.tensor_tensor(hL[:, k - 1], hf[:, (k - 1) % 2], hH[:, k - 1].bitcast(F32),
                                          ALU.subtract).then_inc(S.h_ready, 1)
                c.pres += 1
            else:
                b = 8 * c.posts
                for k in range(DT):
                    dve.wait_ge(S.rstd_done, q + 1)
                    wait(dve, S.x_upd, b + k - 1)
                    dve.scalar_tensor_tensor(hf[:, k % 2], mixT[:, k], col(*gain(k)), rstd[:], ALU.mult,
                                             ALU.mult).then_inc(S.post_t, 1)
                    dve.wait_ge(S.post_t, b + k + 1)
                    dve.tensor_tensor(xT[:, k], xT[:, k], hf[:, k % 2], ALU.add).then_inc(S.x_upd, 1)
                c.posts += 1

        def ffn_pe(pe, c, st):
            hb = 8 * c.pres

            def body(i, first):
                if first:
                    first_products(pe, st, (bank[0][:], bank[1][:]), hb)
                for j in range(2 if first else 0, 4):
                    if not first:
                        pe.wait_ge(S.prod_done, FT * c.ffns + 2 * i + (j // 2 - 1))
                    unit_product(pe, st, i, j, bank[j][:], (hH, hL), 0, True, True)
            c.pres += 1
            body(0, True)
            with pe.Fori(1, st.bodies) as i:
                body(i, False)
            c.ffns += 1

        def ffn_act(act, c, st, conv, after):
            f0, v0 = FT * c.ffns, FT * c.convs

            def gate(i, b, jg, first=False):
                act.wait_ge(S.mm_done, st.done(i, jg))
                if not first:
                    act.wait_ge(S.prod_done, f0 + 2 * i + b - 1)
                if conv is None:
                    act.activation(silu_g[:, b], bank[jg][:], ACT.Silu).then_inc(S.silu_done, 1)
                else:
                    w, bb = conv
                    act.activation(silu_g[:, b], bank[jg][:], ACT.Identity, scale=colr(w, 2 * FT + 2 * i + b),
                                   bias=colr(bb, 2 * i + b)).then_inc(S.acc_done, 1)
                    act.wait_ge(S.conv_done, 2 * (v0 + 2 * i + b + 1) if isinstance(i, int)
                                else 2 * (v0 + b + 1) + 4 * i)
                    act.activation(silu_g[:, b], silu_g[:, b], ACT.Silu).then_inc(S.silu_done, 1)

            def up(i, b):
                act.wait_ge(S.prod_done, f0 + 2 * i + b + 1)
                act.activation(tile_of(aH, 2 * i + b), prod[:, b], ACT.Copy).then_inc(S.ah_done, 1)

            for j in range(4):
                if j >= st.early:
                    split_hi(act, st, 0, j)
                if j >= 2:
                    gate(0, 0, 0, True) if j == 2 else up(0, 0)

            def body(i, ip, first=False):
                for j in range(4):
                    split_hi(act, st, i, j)
                    (lambda: gate(ip, 1, 2, first), lambda: up(ip, 1), lambda: gate(i, 0, 0), lambda: up(i, 0))[j]()
            body(1, 0, True)
            with act.Fori(2, st.bodies) as i:
                body(i, i - 1)
            split_hi(act, after, 0, 0)
            gate(st.bodies - 1, 1, 2)
            split_hi(act, after, 0, 1)
            up(st.bodies - 1, 1)
            c.ffns += 1
            c.convs += conv is not None

        def ffn_dve(dve, c, st, conv, after):
            f0, v0 = FT * c.ffns, FT * c.convs

            def taps(i, b, jg):
                if conv is None:
                    return
                w, _ = conv
                acc0 = v0 + b + 1
                dve.wait_ge(S.acc_done, acc0 + 2 * i)
                for n, shift in enumerate((1, 2)):
                    if n:
                        dve.wait_ge(S.conv_done, 2 * (acc0 - 1) + 1 + 4 * i)
                    dve.scalar_tensor_tensor(silu_g[:, b, shift:], bank[jg][:, 0:SEQ - shift],
                                             colr(w, (2 - shift) * FT + 2 * i + b), silu_g[:, b, shift:], ALU.mult,
                                             ALU.add).then_inc(S.conv_done, 1)

            def product(i, b, ju, first=False):
                dve.wait_ge(S.silu_done, f0 + 2 * i + b + 1)
                dve.wait_ge(S.mm_done, st.done(i, ju))
                if not first:
                    dve.wait_ge(S.a_ready, f0 + 2 * i + b - 1)
                dve.tensor_tensor(prod[:, b], silu_g[:, b], bank[ju][:], ALU.mult).then_inc(S.prod_done, 1)

            def low(i, b):
                dve.wait_ge(S.ah_done, f0 + 2 * i + b + 1)
                dve.tensor_tensor(tile_of(aL, 2 * i + b), prod[:, b], tile_of(aH, 2 * i + b).bitcast(F32),
                                  ALU.subtract).then_inc(S.a_ready, 1)

            for j in range(4):
                if j >= st.early:
                    split_lo(dve, st, 0, j)
                if j == 2:
                    taps(0, 0, 0)
                if j == 3:
                    product(0, 0, 1, True)
            def body(i, ip, first=False):
                split_lo(dve, st, i, 0)
                low(ip, 0)
                taps(ip, 1, 2)
                split_lo(dve, st, i, 1)
                product(ip, 1, 3, first)
                split_lo(dve, st, i, 2)
                low(ip, 1)
                taps(i, 0, 0)
                split_lo(dve, st, i, 3)
                product(i, 0, 1)
            body(1, 0, True)
            with dve.Fori(2, st.bodies) as i:
                body(i, i - 1)
            i = st.bodies - 1
            split_lo(dve, after, 0, 0)
            low(i, 0)
            taps(i, 1, 2)
            split_lo(dve, after, 0, 1)
            product(i, 1, 3)
            low(i, 1)
            c.ffns += 1
            c.convs += conv is not None

        def proj_start(pe, st, j, ks):
            pe.wait_ge(S.lo_done, st.done(0, j))
            products(pe, st, 0, j, bank[j][:], (aH, aL), 0, ks, True, False)

        def proj_pe(pe, c, st, ready, late):
            upm = 2 if st.K == 11 else 1
            p0 = 8 * c.projs

            def body(i, first):
                for j in range(4):
                    m, part = j // upm, j % upm
                    per = 4 // upm
                    if part == 0 and not first:
                        pe.wait_ge(S.proj_ev, p0 + per * i + (m + 1 - per))
                    if first and late is not None:
                        for k in late:
                            if j == 0:
                                ready(k)
                            last = products(pe, st, 0, j, bank[m][:], (aH, aL), 0, (k,), False, k == late[-1])
                        last.then_inc(S.mm_done, 1)
                    else:
                        unit_product(pe, st, i, j, bank[m][:], (aH, aL), part * st.K, part == 0, part == upm - 1,
                                     ready if first and m == 0 else None)
            if late is None:
                pe.wait_ge(S.prod_done, FT * c.ffns - 1)
            body(0, True)
            with pe.Fori(1, st.bodies) as i:
                body(i, False)
            c.projs += 1

        def proj_act(act, c, st, src, meanwhile, after):
            upm = 2 if st.K == 11 else 1
            per = 4 // upm
            q, p0 = c.norms, 8 * c.projs

            def squares(i, j):
                if j % upm == upm - 1:
                    m = j // upm
                    act.wait_ge(S.proj_ev, p0 + per * i + (m + 1))
                    square_tile(act, q, per * i + m, tile_of(src, per * i + m), m % 2)

            for j in range(4):
                if j >= st.early:
                    split_hi(act, st, 0, j)
                if j >= 2:
                    squares(0, j - 2)

            def body(i, before):
                for j in range(4):
                    split_hi(act, st, i, j)
                    squares(before if j < 2 else i, (j - 2) % 4)
            body(1, 0)
            if meanwhile is not None:
                meanwhile()
            if st.bodies > 2:
                with act.Fori(2, st.bodies) as i:
                    body(i, i - 1)
            if after is not None:
                split_hi(act, after, 0, 0)
            squares(st.bodies - 1, 2)
            squares(st.bodies - 1, 3)
            if after is not None:
                split_hi(act, after, 0, 1)
            c.projs += 1

        def proj_dve(dve, c, st, scale, meanwhile, after):
            upm = 2 if st.K == 11 else 1
            per = 4 // upm
            q = c.norms

            def take(i, j, last=False):
                if j % upm != upm - 1:
                    return
                m = j // upm
                dve.wait_ge(S.mm_done, st.done(i, j))
                src = bank[m][:]
                if scale is None:
                    dve.tensor_copy(tile_of(mixT, per * i + m), src).then_inc(S.proj_ev, 1)
                else:
                    x_m = tile_of(xT, per * i + m)
                    dve.scalar_tensor_tensor(x_m, src, scale, x_m, ALU.mult, ALU.add).then_inc(S.proj_ev, 1)
                if not (isinstance(i, int) and i == 0 and m == 0):
                    add_square(dve, c, q, per * i + (m - 1), (m + 1) % 2)

            for j in range(4):
                if j >= st.early:
                    split_lo(dve, st, 0, j)
                if j >= 2:
                    take(0, j - 2)

            def body(i, before):
                for j in range(4):
                    split_lo(dve, st, i, j)
                    take(before if j < 2 else i, (j - 2) % 4)
            body(1, 0)
            if meanwhile is not None:
                meanwhile()
            if st.bodies > 2:
                with dve.Fori(2, st.bodies) as i:
                    body(i, i - 1)
            if after is not None:
                split_lo(dve, after, 0, 0)
            take(st.bodies - 1, 2)
            take(st.bodies - 1, 3)
            add_square(dve, c, q, DT - 1, 1)
            if after is not None:
                split_lo(dve, after, 0, 1)
            c.projs += 1

        nsp4 = at("nsp4", [16], o + 656)
        k = Names(bank=bank, S=S, free=free, scratch=scratch, sems=sems, load_unit=load_unit, split_hi=split_hi,
                            split_lo=split_lo, unit_product=unit_product, first_products=first_products, proj_start=proj_start, hH=hH, hL=hL, aH=aH, aL=aL, tile_of=tile_of,
                            colat=colat, colr=colr, col=col, hbg=hbg, sp2=sp2, nsp4=nsp4, qg=qg, eps_col=eps_col, ident=ident,
                            heads1=heads1, ones_half=ones_half, held_dve=S.held_dve, held_pool=S.held_pool)
        mixers = (gated_recurrence_mixer(k, IN1, t, 16), conv_attention_mixer(k, IN2, t, 32), stick_mixer(k, IN3, t, 48))

        phases = [
            ("pre", GU1, lambda k: ("norm_ffn1", k)), ("ffn", GU1, None), ("proj", DN1, 0.5),
            ("pre", IN1, lambda k: ("norm_mix", k)), ("mix", 0, IN1), ("proj", OUT1, 1.0),
            ("pre", GU2, lambda k: ("norm_ffn2", k)), ("ffn", GU2, None), ("proj", DN2, 0.5),
            ("pre", IN2, lambda k: ("norm_g_2", k)), ("mix", 1, IN2), ("proj", OUT2, None),
            ("post", None, lambda k: ("norm_g_2", 8 + k)),
            ("pre", GU3, lambda k: ("norm_g_2", 16 + k)), ("ffn", GU3, 0), ("proj", DN3, None),
            ("post", None, lambda k: ("norm_g_2", 24 + k)),
            ("pre", IN3, lambda k: ("norm_g_2", 32 + k)), ("mix", 2, IN3), ("proj", OUT3, None),
            ("post", None, lambda k: ("norm_g_2", 40 + k)),
            ("pre", GU4, lambda k: ("norm_g_2", 48 + k)), ("ffn", GU4, 1), ("proj", DN4, None),
            ("post", None, lambda k: ("norm_g_2", 56 + k)),
        ]

        def after(n):
            return next((rest[0] if kind != "mix" else rest[1] for kind, *rest in phases[n + 1:]
                         if kind in ("ffn", "proj", "mix")), None)

        def conv_cols(layer):
            return None if layer is None else (f"w_ffn_conv_2@{layer}", f"b_ffn_conv_2@{layer}")

        for layer in range(2):
            COLS[f"w_ffn_conv_2@{layer}"] = COLS["w_ffn_conv_2"] + 66 * layer
            COLS[f"b_ffn_conv_2@{layer}"] = COLS["b_ffn_conv_2"] + 22 * layer

        @block.sync
        def _(sp):
            for n in range(4):
                sp.dma_start(xT[:, 2 * n:2 * n + 2], t["xT"][:, 2 * n:2 * n + 2]).then_inc(x_loaded[n], 16)
            sp.dma_start(cols[:], t["cols"]).then_inc(S.consts, 16)
            sp.dma_start(ident[:], t["ident"]).then_inc(S.consts, 16)
            sp.dma_start(heads1[:], t["heads1"]).then_inc(S.consts, 16)
            for kind, *rest in phases:
                if kind == "ffn" or kind == "proj":
                    st = rest[0]
                    for j in range(4):
                        load_unit(sp, st, 0, j)
                    with sp.Fori(1, st.bodies) as i:
                        for j in range(4):
                            load_unit(sp, st, i, j)
                if kind == "mix":
                    mixers[rest[0]].sp(sp)
            n_post = sum(p[0] == "post" for p in phases)
            n_proj = sum(p[0] == "proj" for p in phases)
            wait(sp, S.proj_ev, 8 * n_proj)
            for k in range(DT):
                wait(sp, S.x_upd, 8 * n_post - 7 + k)
                sp.dma_start(t["out"][:, k], xT[:, k]).then_inc(S.out_done, 16)
            sp.wait_ge(S.out_done, 16 * DT)

        @block.scalar
        def _(act):
            c = Tally()
            act.wait_ge(S.consts, 48)
            act.wait_ge(S.small, MEMSETS)

            def lambda_exp():
                act.wait_ge(S.small, LAM_ABS)
                act.activation(lam_t[:, 1], lam_t[:, 1], ACT.Exp, scale=-1.0).then_inc(S.lam_exp, 1)
            for n, (kind, *rest) in enumerate(phases):
                if kind == "pre":
                    if n == 0:
                        for m in range(DT):
                            act.wait_ge(x_loaded[m // 2], 16)
                            square_tile(act, 0, m, xT[:, m], m % 2)
                        for j in range(2):
                            split_hi(act, rest[0], 0, j)
                    norm_act(act, c, True, rest[0], False, n and phases[n - 1][0] == "post")
                elif kind == "post":
                    norm_act(act, c, False, None, n + 1 < len(phases), False)
                elif kind == "ffn":
                    ffn_act(act, c, rest[0], conv_cols(rest[1]), after(n))
                elif kind == "proj":
                    proj_act(act, c, rest[0], xT if rest[1] else mixT, lambda_exp if n == 2 else None,
                             after(n))
                else:
                    mixers[rest[0]].act(act, after(n))

        @block.vector
        def _(dve):
            c = Tally()
            steps = [0]

            def then(instruction):
                instruction.then_inc(S.small, 1)
                steps[0] += 1
                dve.wait_ge(S.small, steps[0])

            def small_constants():
                neg, y_, s_, s2 = (lam_t[:, n] for n in range(4))
                lam_, out_, acc_ = cols[:, COLS["lru_lambda"]:COLS["lru_lambda"] + 16], sp2[:], lam[:]
                then(dve.tensor_scalar(qg[:], col("q_norm"), 0.125, None, ALU.mult))
                then(dve.tensor_scalar(hbg[:], cols[:, COLS["lru_b_gates"]:COLS["lru_b_gates"] + 32], 0.5, None, ALU.mult))
                then(dve.tensor_scalar(neg, lam_, -1.0, None, ALU.mult))
                then(dve.tensor_tensor(y_, neg, lam_, ALU.max))
                assert steps[0] == LAM_ABS
                dve.wait_ge(S.lam_exp, 1)
                then(dve.tensor_scalar(s_, y_, 2.0, None, ALU.add))
                then(dve.reciprocal(s_, s_))
                then(dve.tensor_tensor(s_, s_, y_, ALU.mult))
                then(dve.tensor_tensor(s2, s_, s_, ALU.mult))
                then(dve.tensor_scalar(acc_, s2, 1.0 / 17, None, ALU.mult))
                for n in range(15, 1, -2):
                    then(dve.scalar_tensor_tensor(acc_, acc_, 1.0 / n, s2, ALU.add, ALU.mult))
                then(dve.scalar_tensor_tensor(acc_, acc_, 1.0, s_, ALU.add, ALU.mult))
                then(dve.tensor_scalar(acc_, acc_, 4.0, None, ALU.mult))
                then(dve.tensor_scalar(neg, neg, 0.0, 2.0, ALU.max, ALU.mult))
                then(dve.tensor_tensor(out_, neg, acc_, ALU.add))
                then(dve.tensor_scalar(k.nsp4[:], sp2[:], -2.0, None, ALU.mult))
                assert steps[0] == SMALL

            then(dve.memset(ones[:], 1.0 / D))
            then(dve.memset(ones_half[:], 1.0 / HALF_W))
            then(dve.memset(eps_col[:], EPS))
            dve.wait_ge(S.consts, 48)
            assert steps[0] == MEMSETS
            for n, (kind, *rest) in enumerate(phases):
                if kind == "pre":
                    if n == 0:
                        for m in range(DT):
                            add_square(dve, c, 0, m, m % 2)
                        for j in range(2):
                            split_lo(dve, rest[0], 0, j)
                    norm_dve(dve, c, rest[1], True, n and phases[n - 1][0] == "post")
                elif kind == "post":
                    norm_dve(dve, c, rest[1], False, False)
                elif kind == "ffn":
                    ffn_dve(dve, c, rest[0], conv_cols(rest[1]), after(n))
                elif kind == "proj":
                    proj_dve(dve, c, rest[0], rest[1], small_constants if n == 2 else None, after(n))
                else:
                    mixers[rest[0]].dve(dve, after(n))

        @block.tensor
        def _(pe):
            c = Tally()
            pe.wait_ge(S.consts, 48)
            pe.wait_ge(S.small, MEMSETS)
            for n, (kind, *rest) in enumerate(phases):
                if kind in ("pre", "post"):
                    norm_pe(pe, c, n and phases[n - 1][0] == "post")
                    if kind == "pre" and n + 1 < len(phases) and phases[n + 1][0] == "mix":
                        c.pres += 1
                elif kind == "ffn":
                    ffn_pe(pe, c, rest[0])
                elif kind == "proj":
                    if phases[n - 1][0] == "ffn":
                        proj_pe(pe, c, rest[0], lambda f: pe.wait_ge(S.a_ready, FT * (c.ffns - 1) + f + 1), None)
                    else:
                        mixer = mixers[phases[n - 1][1]]
                        proj_pe(pe, c, rest[0], mixer.y_ready(pe), mixer.late)
                else:
                    mixers[rest[0]].pe(pe, 8 * c.pres, after(n))

        @block.gpsimd
        def _(pool):
            for kind, *rest in phases:
                if kind == "mix":
                    mixers[rest[0]].pool(pool)


INPUTS = ("xT", "cols", "ident", "heads1", "win_mask", "gate_w", "rpb", "rel_bias_2", "dist_onehot", "dist_add", "before",
          "w_ffn1_gu", "w_ffn1_down", "w_in", "w_out", "w_ffn2_gu", "w_ffn2_down", "w_in_even_2", "w_out_even_2", "w_up_2a",
          "w_down_2a", "w_in_odd_2", "w_out_odd_2", "w_up_2b", "w_down_2b")


def shape_constants():
    heads1 = np.zeros((P, P), np.float32)
    heads1[:64, :64] = heads1[64:, 64:] = 1.0 / 64
    win = np.full((P, 3, 256), NEG, np.float32)
    for n in (0, 1, 3):
        for c in range(16):
            qc = 16 * n + c
            first = min(max(qc - 8, 0), GRID_W - 16)
            for kc in range(first, first + 16):
                at = (kc - KSTART[n]) * ROWS
                win[c * ROWS:(c + 1) * ROWS, MASK_OF[n], at:at + ROWS] = 0.0
    onehot = np.zeros((32, DIST), np.float32)
    add = np.full((8, DIST), NEG, np.float32)
    for y in range(DIST):
        d = y - 128
        if d < 0:
            continue
        large = 16 + int(np.float32(np.log(np.float32(max(d, 1) / 16))) / np.float32(np.log(128.0)) * 16)
        onehot[d if d < 16 else min(large, 31), y] = 1.0
        count = (d <= 128) + (d % 4 == 0) + (d % 16 == 0)
        if count:
            add[:, y] = np.log(float(count))
    before = np.where(np.arange(P)[None, :] < np.arange(P)[:, None], 0.0, NEG).astype(np.float32)
    return dict(ident=np.eye(P, dtype=np.float32), heads1=heads1, win_mask=win, dist_onehot=onehot, dist_add=add,
                before=before)


def laid_out(x):
    def units(w, K):
        rows, columns = w.shape
        w = w.reshape(rows // (K * P), K, P, columns // P, P)
        return np.ascontiguousarray(w.transpose(3, 0, 2, 1, 4)).reshape(-1, P, K * P)

    def interleaved(w, parts, K=8):
        w = units(w, K)
        return np.ascontiguousarray(w.reshape(parts, -1, P, K * P).swapaxes(0, 1)).reshape(-1, P, K * P)

    def columns(v):
        return np.ascontiguousarray(v).reshape(-1, P).T

    pieces = []
    for name in COLS:
        if "@" in name:
            continue
        v = x[name]
        if name in ("q_norm", "k_norm"):
            v = np.tile(v[0], 2)
        pieces.append(columns(v))
    out = shape_constants()
    out["cols"] = np.ascontiguousarray(np.concatenate(pieces, 1))
    out["xT"] = np.ascontiguousarray(x["x"][0].T.reshape(DT, P, SEQ).swapaxes(0, 1))
    gates = np.zeros((8, P, 4, P), np.float32)
    g = x["lru_w_gates"][0].reshape(4, 8, 2, 64, 64)
    for half in range(2):
        gates[:, 64 * half:64 * half + 64, :, 64 * half:64 * half + 64] = g[:, :, half].transpose(1, 2, 0, 3)
    out["gate_w"] = gates
    rpb = np.zeros((16, RPB_DR, RPB_W), np.float32)
    rpb[:, :, 16:16 + RPB_DC] = x["rel_pos_bias"][0]
    out["rpb"] = np.ascontiguousarray(rpb.reshape(16, -1)[:, ::-1])
    out["rel_bias_2"] = x["rel_bias_2"]
    out["w_ffn1_gu"] = interleaved(x["w_ffn1_gu"][0], 2)
    out["w_ffn1_down"] = units(x["w_ffn1_down"][0], 11)
    out["w_in"] = np.ascontiguousarray(interleaved(x["w_in"][0], 7))
    out["w_out"] = units(x["w_out"][0], 8)
    out["w_ffn2_gu"] = interleaved(x["w_ffn2_gu"][0], 2)
    out["w_ffn2_down"] = units(x["w_ffn2_down"][0], 11)
    out["w_in_even_2"] = interleaved(x["w_in_even_2"][0], 6)
    out["w_out_even_2"] = units(x["w_out_even_2"][0], 8)
    out["w_in_odd_2"] = interleaved(x["w_in_odd_2"][0], 5)
    out["w_out_odd_2"] = units(x["w_out_odd_2"][0], 8)
    for layer, name in enumerate("ab"):
        out[f"w_up_2{name}"] = interleaved(x["w_up_2"][layer], 2)
        out[f"w_down_2{name}"] = units(x["w_down_2"][layer], 11)
    return out


def kernel(**inputs):
    import concourse.bacc as bacc
    from concourse.bass_utils import run_bass_kernel_spmd

    arrays = laid_out({name: np.asarray(a) for name, a in inputs.items()})
    nc = bacc.Bacc("TRN2", target_bir_lowering=False, num_devices=1, dynamic_dma_scratch_size=1024)
    t = {name: nc.dram_tensor(f"in_{name}", arrays[name].shape, F32, kind="ExternalInput").ap() for name in INPUTS}
    t["dist_table"] = nc.dram_tensor("dist_table", (8, DIST), F32).ap()
    t["out"] = nc.dram_tensor("out_x", (P, DT, SEQ), F32, kind="ExternalOutput").ap()
    build(nc, t)
    r = run_bass_kernel_spmd(nc, [{f"in_{name}": arrays[name] for name in INPUTS}], core_ids=[0])
    y = r.results[0]["out_x"]
    return np.ascontiguousarray(y.transpose(2, 1, 0).reshape(1, SEQ, D))
```
